# Optimizing a Trainium2 kernel written in Bass

```python
import math
import jax, jax.numpy as jnp
from jax import lax
import numpy as np
import jax
import jax.numpy as jnp

D_MODEL = 1024
BATCH = 1
SEQ = 256
DEPTH = 1

N_ATTN_HEADS = 8
HEAD_DIM = 64
ATTN_WIDTH = N_ATTN_HEADS * HEAD_DIM
N_RG_BLOCKS = 8
RG_WIDTH = 512
RG_BLOCK = RG_WIDTH // N_RG_BLOCKS
MIX_WIDTH = ATTN_WIDTH + RG_WIDTH
IN_COLS = 3 * ATTN_WIDTH + 2 * RG_WIDTH
DILATED_PATTERNS = ((128, 1), (512, 4), (2048, 16))
BAND_BLOCK = 64
ROPE_THETA = 10000.0
CONV_WIDTH = 4
CONV_PAD_LEFT = 2
CONV_PAD_RIGHT = 1
RG_C = 8.0
N_MEM = 256
N_CROSS_HEADS = 4
CROSS_HEAD_DIM = 128
CROSS_WIDTH = N_CROSS_HEADS * CROSS_HEAD_DIM
D_FF = 4 * D_MODEL
NORM_EPS = 1e-6
NEG_BIG = -1e30


def rmsnorm(x, g):
    xf = x.astype(jnp.float32)
    return xf * lax.rsqrt(jnp.mean(xf * xf, axis=-1, keepdims=True) + NORM_EPS) * g.astype(jnp.float32)

def rope(t, positions):
    half = t.shape[-1] // 2
    inv_freq = ROPE_THETA ** (-jnp.arange(half, dtype=jnp.float32) / half)
    ang = positions.astype(jnp.float32)[..., None] * inv_freq
    cos = jnp.cos(ang)[:, :, None, :]
    sin = jnp.sin(ang)[:, :, None, :]
    t1, t2 = t[..., :half], t[..., half:]
    return jnp.concatenate([t1 * cos - t2 * sin, t1 * sin + t2 * cos], axis=-1)

def banded_window_attention(q, k, v, radius):
    L, dh = q.shape[-2], q.shape[-1]
    blk = BAND_BLOCK
    nb = -(-L // blk)
    Lp = nb * blk
    lead = q.shape[:-2]
    nlead = len(lead)
    qb = jnp.pad(q, [(0, 0)] * nlead + [(0, Lp - L), (0, 0)]).reshape(*lead, nb, blk, dh)
    pad_both = [(0, 0)] * nlead + [(blk, Lp - L + blk), (0, 0)]
    kb = jnp.pad(k, pad_both).reshape(*lead, nb + 2, blk, dh)
    vb = jnp.pad(v, pad_both).reshape(*lead, nb + 2, blk, dh)
    kn = jnp.concatenate([kb[..., :-2, :, :], kb[..., 1:-1, :, :], kb[..., 2:, :, :]], axis=-2)
    vn = jnp.concatenate([vb[..., :-2, :, :], vb[..., 1:-1, :, :], vb[..., 2:, :, :]], axis=-2)
    s = jnp.einsum('...nqd,...nkd->...nqk', qb, kn) * (dh ** -0.5)
    qpos = jnp.arange(nb)[:, None] * blk + jnp.arange(blk)[None, :]
    kpos = (jnp.arange(nb)[:, None] - 1) * blk + jnp.arange(3 * blk)[None, :]
    dist = qpos[:, :, None] - kpos[:, None, :]
    valid = (jnp.abs(dist) <= radius) & (kpos[:, None, :] >= 0) & (kpos[:, None, :] < L)
    s = jnp.where(valid, s, NEG_BIG)
    m = jnp.max(s, axis=-1, keepdims=True)
    p = jnp.exp(s - m)
    denom = jnp.sum(p, axis=-1, keepdims=True)
    o = jnp.einsum('...nqk,...nkd->...nqd', p, vn) / denom
    lse = (m + jnp.log(denom))[..., 0]
    o = o.reshape(*lead, Lp, dh)[..., :L, :]
    lse = lse.reshape(*lead, Lp)[..., :L]
    return o, lse

def dilated_mixture_attention(q, k, v):
    B, S, H, dh = q.shape
    outs, lses = [], []
    for window, dil in DILATED_PATTERNS:
        L = S // dil

        def to_classes(t):
            return t.reshape(B, L, dil, H, dh).transpose(0, 2, 3, 1, 4)

        o, lse = banded_window_attention(to_classes(q), to_classes(k), to_classes(v), window // (2 * dil))
        outs.append(o.transpose(0, 3, 1, 2, 4).reshape(B, S, H, dh))
        lses.append(lse.transpose(0, 3, 1, 2).reshape(B, S, H))
    w = jax.nn.softmax(jnp.stack(lses, axis=0), axis=0)
    return jnp.sum(w[..., None] * jnp.stack(outs, axis=0), axis=0)

def centred_depthwise_conv(u, w, b):
    out = lax.conv_general_dilated(
        u, w[:, None, :].astype(u.dtype), window_strides=(1,),
        padding=[(CONV_PAD_LEFT, CONV_PAD_RIGHT)],
        dimension_numbers=('NWC', 'WIO', 'NWC'),
        feature_group_count=u.shape[-1])
    return out + b

def _linear_recurrence_combine(c1, c2):
    a1, b1 = c1
    a2, b2 = c2
    return a1 * a2, a2 * b1 + b2

def bidirectional_rglru(u, a_w, a_b, x_w, x_b, lam):
    B, S, _ = u.shape
    ug = u.reshape(B, S, N_RG_BLOCKS, RG_BLOCK)
    r = jax.nn.sigmoid(jnp.einsum('bsgi,zgij->zbsgj', ug, a_w) + a_b[:, None, None]).reshape(2, B, S, RG_WIDTH)
    i = jax.nn.sigmoid(jnp.einsum('bsgi,zgij->zbsgj', ug, x_w) + x_b[:, None, None]).reshape(2, B, S, RG_WIDTH)
    log_a = -RG_C * r * jax.nn.softplus(-lam.astype(jnp.float32))[:, None, None, :]
    a = jnp.exp(log_a)
    b = jnp.sqrt(-jnp.expm1(2.0 * log_a)) * (i * u[None])
    _, h_f = lax.associative_scan(_linear_recurrence_combine, (a[0], b[0]), axis=1)
    _, h_b = lax.associative_scan(_linear_recurrence_combine, (a[1], b[1]), axis=1, reverse=True)
    return h_f + h_b

def memory_cross_attention(xn, memn, wq, wk, wv, wo):
    B, S, _ = xn.shape
    M = memn.shape[1]
    q = (xn @ wq).reshape(B, S, N_CROSS_HEADS, CROSS_HEAD_DIM)
    k = (memn @ wk).reshape(B, M, N_CROSS_HEADS, CROSS_HEAD_DIM)
    v = (memn @ wv).reshape(B, M, N_CROSS_HEADS, CROSS_HEAD_DIM)
    s = jnp.einsum('bshd,bmhd->bhsm', q, k) * (CROSS_HEAD_DIM ** -0.5)
    p = jax.nn.softmax(s, axis=-1)
    o = jnp.einsum('bhsm,bmhd->bshd', p, v).reshape(B, S, CROSS_WIDTH)
    return o @ wo

def first_inputs(seed: int = 0) -> dict:
    key = jax.random.key(seed)
    ks = jax.random.split(key, 24)
    f32 = jnp.float32

    def nrm(k, shape, scale):
        return jax.random.normal(k, shape, f32) * scale

    def gain(k, shape):
        return 1.0 + 0.05 * jax.random.normal(k, shape, f32)

    lam_u = jax.random.uniform(ks[11], (DEPTH, 2, RG_WIDTH), f32, minval=0.9, maxval=0.999)
    a0 = lam_u ** (1.0 / RG_C)
    rg_lambda = jnp.log(a0) - jnp.log1p(-a0)
    return {
        "x": nrm(ks[0], (BATCH, SEQ, D_MODEL), 1.0),
        "mem": nrm(ks[1], (BATCH, N_MEM, D_MODEL), 1.0),
        "positions": jnp.broadcast_to(jnp.arange(SEQ, dtype=jnp.int32), (BATCH, SEQ)),
        "norm_mix_g": gain(ks[2], (DEPTH, D_MODEL)),
        "w_in": nrm(ks[3], (DEPTH, D_MODEL, IN_COLS), D_MODEL ** -0.5),
        "conv_w": nrm(ks[4], (DEPTH, CONV_WIDTH, RG_WIDTH), CONV_WIDTH ** -0.5),
        "conv_b": nrm(ks[5], (DEPTH, RG_WIDTH), 0.01),
        "rg_a_w": nrm(ks[6], (DEPTH, 2, N_RG_BLOCKS, RG_BLOCK, RG_BLOCK), RG_BLOCK ** -0.5),
        "rg_a_b": nrm(ks[7], (DEPTH, 2, N_RG_BLOCKS, RG_BLOCK), 0.01),
        "rg_x_w": nrm(ks[8], (DEPTH, 2, N_RG_BLOCKS, RG_BLOCK, RG_BLOCK), RG_BLOCK ** -0.5),
        "rg_x_b": nrm(ks[9], (DEPTH, 2, N_RG_BLOCKS, RG_BLOCK), 0.01),
        "rg_lambda": rg_lambda,
        "w_out": nrm(ks[10], (DEPTH, MIX_WIDTH, D_MODEL), MIX_WIDTH ** -0.5),
        "norm_cross_g": gain(ks[12], (DEPTH, D_MODEL)),
        "norm_mem_g": gain(ks[13], (DEPTH, D_MODEL)),
        "w_cq": nrm(ks[14], (DEPTH, D_MODEL, CROSS_WIDTH), D_MODEL ** -0.5),
        "w_ck": nrm(ks[15], (DEPTH, D_MODEL, CROSS_WIDTH), D_MODEL ** -0.5),
        "w_cv": nrm(ks[16], (DEPTH, D_MODEL, CROSS_WIDTH), D_MODEL ** -0.5),
        "w_co": nrm(ks[17], (DEPTH, CROSS_WIDTH, D_MODEL), CROSS_WIDTH ** -0.5),
        "norm_mlp_g": gain(ks[18], (DEPTH, D_MODEL)),
        "w_mlp_in": nrm(ks[19], (DEPTH, D_MODEL, D_FF), D_MODEL ** -0.5),
        "w_mlp_out": nrm(ks[20], (DEPTH, D_FF, D_MODEL), D_FF ** -0.5),
        "norm_final_g": gain(ks[21], (D_MODEL,)),
    }

def first_block(x, mem, positions, norm_mix_g, w_in, conv_w, conv_b, rg_a_w, rg_a_b, rg_x_w, rg_x_b,
              rg_lambda, w_out, norm_cross_g, norm_mem_g, w_cq, w_ck, w_cv, w_co,
              norm_mlp_g, w_mlp_in, w_mlp_out, norm_final_g):
    B, S, _ = x.shape
    h = x.astype(jnp.float32)
    memf = mem.astype(jnp.float32)
    for l in range(DEPTH):
        xn = rmsnorm(h, norm_mix_g[l])
        proj = xn @ w_in[l]
        q, k, v, u, y = jnp.split(proj, [ATTN_WIDTH, 2 * ATTN_WIDTH, 3 * ATTN_WIDTH,
                                         3 * ATTN_WIDTH + RG_WIDTH], axis=-1)
        q = rope(q.reshape(B, S, N_ATTN_HEADS, HEAD_DIM), positions)
        k = rope(k.reshape(B, S, N_ATTN_HEADS, HEAD_DIM), positions)
        v = v.reshape(B, S, N_ATTN_HEADS, HEAD_DIM)
        attn = dilated_mixture_attention(q, k, v).reshape(B, S, ATTN_WIDTH)
        uc = centred_depthwise_conv(u, conv_w[l], conv_b[l])
        rec = bidirectional_rglru(uc, rg_a_w[l], rg_a_b[l], rg_x_w[l], rg_x_b[l], rg_lambda[l]) * jax.nn.gelu(y)
        h = h + jnp.concatenate([attn, rec], axis=-1) @ w_out[l]
        h = h + memory_cross_attention(rmsnorm(h, norm_cross_g[l]), rmsnorm(memf, norm_mem_g[l]),
                                       w_cq[l], w_ck[l], w_cv[l], w_co[l])
        hid = jnp.square(jax.nn.relu(rmsnorm(h, norm_mlp_g[l]) @ w_mlp_in[l]))
        h = h + hid @ w_mlp_out[l]
    return rmsnorm(h, norm_final_g).astype(x.dtype)


DEPTH_2 = 2

N_BRANCH = 4
BRANCH_WIDTH = 256
MLA_HEADS = 4
MLA_Q_LORA = 384
MLA_KV_LORA = 128
MLA_NOPE = 64
MLA_ROPE = 32
MLA_V = 64
FNET_GROUPS = 4
FNET_GROUP_DIM = 64
DIFF_HEADS = 4
DIFF_HEAD_DIM = 32
HGRN_HEADS = 4
HGRN_KEY_DIM = 64
HGRN_VAL_DIM = 64
HGRN_CHUNK = 64
D_FF_2 = -(-8 * D_MODEL // (3 * 256)) * 256

Q_BLOCK = 128
EPS = 1e-6

IN_WIDTHS = (
    MLA_Q_LORA,
    MLA_KV_LORA,
    MLA_ROPE,
    FNET_GROUPS * FNET_GROUP_DIM,
    2 * DIFF_HEADS * DIFF_HEAD_DIM,
    2 * DIFF_HEADS * DIFF_HEAD_DIM,
    DIFF_HEADS * 2 * DIFF_HEAD_DIM,
    HGRN_HEADS * HGRN_KEY_DIM,
    HGRN_HEADS * HGRN_VAL_DIM,
    HGRN_HEADS * HGRN_KEY_DIM,
    HGRN_HEADS * HGRN_KEY_DIM,
    HGRN_HEADS * HGRN_VAL_DIM,
    N_BRANCH * D_MODEL,
)
IN_TOTAL = sum(IN_WIDTHS)


def rmsnorm_2(x, g):
    xf = x.astype(jnp.float32)
    y = xf * lax.rsqrt(jnp.mean(xf * xf, axis=-1, keepdims=True) + EPS)
    return (y * g.astype(jnp.float32)).astype(x.dtype)

def split_cols(z, widths):
    offsets = [int(o) for o in np.cumsum(widths)[:-1]]
    return jnp.split(z, offsets, axis=-1)

def rope_tables(seq_len, dim):
    inv_freq = 1.0 / (ROPE_THETA ** (jnp.arange(0, dim, 2, dtype=jnp.float32) / dim))
    ang = jnp.arange(seq_len, dtype=jnp.float32)[:, None] * inv_freq[None, :]
    return jnp.cos(ang), jnp.sin(ang)

def apply_rope(t, cos, sin):
    tf = t.astype(jnp.float32)
    t1, t2 = jnp.split(tf, 2, axis=-1)
    c = cos[None, :, None, :]
    s = sin[None, :, None, :]
    return jnp.concatenate([t1 * c - t2 * s, t1 * s + t2 * c], axis=-1).astype(t.dtype)

def to_query_blocks(t):
    b, s, h, d = t.shape
    return t.reshape(b, s // Q_BLOCK, Q_BLOCK, h, d).transpose(1, 0, 2, 3, 4)

def from_query_blocks(t):
    nb, b, qb, h, d = t.shape
    return t.transpose(1, 0, 2, 3, 4).reshape(b, nb * qb, h, d)

def block_softmax_attention(q, k, v, scale):
    def one_block(qb):
        s = jnp.einsum('bqhd,bkhd->bhqk', qb, k).astype(jnp.float32) * scale
        p = jax.nn.softmax(s, axis=-1)
        return jnp.einsum('bhqk,bkhd->bqhd', p.astype(v.dtype), v)
    return from_query_blocks(lax.map(one_block, to_query_blocks(q)))

def block_diff_attention(q1, q2, k1, k2, v, lam, scale):
    def one_block(qs):
        qb1, qb2 = qs
        s1 = jnp.einsum('bqhd,bkhd->bhqk', qb1, k1).astype(jnp.float32) * scale
        s2 = jnp.einsum('bqhd,bkhd->bhqk', qb2, k2).astype(jnp.float32) * scale
        p = jax.nn.softmax(s1, axis=-1) - lam * jax.nn.softmax(s2, axis=-1)
        return jnp.einsum('bhqk,bkhd->bqhd', p.astype(v.dtype), v)
    return from_query_blocks(lax.map(one_block, (to_query_blocks(q1), to_query_blocks(q2))))

def mla_mixer(c_q, c_kv, k_rope, g_qa, w_uq, g_kva, w_ukv, g_qn, g_kn, cos, sin):
    b, s, _ = c_q.shape
    qk_dim = MLA_NOPE + MLA_ROPE
    q = (rmsnorm_2(c_q, g_qa) @ w_uq).reshape(b, s, MLA_HEADS, qk_dim)
    kv = (rmsnorm_2(c_kv, g_kva) @ w_ukv).reshape(b, s, MLA_HEADS, MLA_NOPE + MLA_V)
    k_nope, v = jnp.split(kv, [MLA_NOPE], axis=-1)
    k_pe = jnp.broadcast_to(k_rope[:, :, None, :], (b, s, MLA_HEADS, MLA_ROPE))
    k = jnp.concatenate([k_nope, k_pe], axis=-1)
    q = rmsnorm_2(q, g_qn)
    k = rmsnorm_2(k, g_kn)
    q = jnp.concatenate([q[..., :MLA_NOPE], apply_rope(q[..., MLA_NOPE:], cos, sin)], axis=-1)
    k = jnp.concatenate([k[..., :MLA_NOPE], apply_rope(k[..., MLA_NOPE:], cos, sin)], axis=-1)
    o = block_softmax_attention(q, k, v, qk_dim ** -0.5)
    return o.reshape(b, s, MLA_HEADS * MLA_V)

def fnet_mixer(u):
    b, s, _ = u.shape
    uf = u.astype(jnp.float32).reshape(b, s, FNET_GROUPS, FNET_GROUP_DIM)
    y = jnp.fft.fft2(uf, axes=(1, 3), norm='ortho').real
    return y.reshape(b, s, FNET_GROUPS * FNET_GROUP_DIM).astype(u.dtype)

def diff_mixer(q_in, k_in, v_in, g_qn, g_kn, lq1, lk1, lq2, lk2, g_sub, layer_idx, cos, sin):
    b, s, _ = q_in.shape
    d = DIFF_HEAD_DIM
    q = apply_rope(rmsnorm_2(q_in.reshape(b, s, 2 * DIFF_HEADS, d), g_qn), cos, sin)
    k = apply_rope(rmsnorm_2(k_in.reshape(b, s, 2 * DIFF_HEADS, d), g_kn), cos, sin)
    q = q.reshape(b, s, DIFF_HEADS, 2, d)
    k = k.reshape(b, s, DIFF_HEADS, 2, d)
    v = v_in.reshape(b, s, DIFF_HEADS, 2 * d)
    lambda_init = 0.8 - 0.6 * math.exp(-0.3 * layer_idx)
    lam = (jnp.exp(jnp.sum(lq1.astype(jnp.float32) * lk1.astype(jnp.float32)))
           - jnp.exp(jnp.sum(lq2.astype(jnp.float32) * lk2.astype(jnp.float32)))
           + lambda_init)
    o = block_diff_attention(q[:, :, :, 0], q[:, :, :, 1], k[:, :, :, 0], k[:, :, :, 1], v, lam, d ** -0.5)
    o = rmsnorm_2(o, g_sub) * (1.0 - lambda_init)
    return o.reshape(b, s, DIFF_HEADS * 2 * d)

def hgrn2_chunk_scan(q, k, v, log_f):
    b, s, h, dk = q.shape
    dv = v.shape[-1]
    c = HGRN_CHUNK
    n_chunks = s // c

    def chunks(t):
        return t.reshape(b, n_chunks, c, h, t.shape[-1]).transpose(1, 0, 3, 2, 4)

    lower_tri = jnp.tril(jnp.ones((c, c), dtype=bool))[:, :, None]

    def step(state, inp):
        qc, kc, vc, lc = inp
        cum = jnp.cumsum(lc, axis=2)
        inter = jnp.einsum('bhtk,bhkv->bhtv', qc * jnp.exp(cum), state)
        rel = cum[:, :, :, None, :] - cum[:, :, None, :, :]
        decay = jnp.exp(jnp.where(lower_tri, rel, -jnp.inf))
        scores = jnp.einsum('bhtk,bhtsk,bhsk->bhts', qc, decay, kc)
        intra = jnp.einsum('bhts,bhsv->bhtv', scores, vc)
        last = cum[:, :, -1:, :]
        new_state = (jnp.exp(last[:, :, 0, :])[..., None] * state
                     + jnp.einsum('bhsk,bhsv->bhkv', kc * jnp.exp(last - cum), vc))
        return new_state, inter + intra

    init = jnp.zeros((b, h, dk, dv), jnp.float32)
    _, o = lax.scan(step, init, (chunks(q), chunks(k), chunks(v), chunks(log_f)))
    return o.transpose(1, 0, 3, 2, 4).reshape(b, s, h, dv)

def hgrn2_mixer(q_in, i_in, f_fwd_in, f_bwd_in, g_in, lb_fwd, lb_bwd, g_on):
    b, s, _ = q_in.shape
    h, dk, dv = HGRN_HEADS, HGRN_KEY_DIM, HGRN_VAL_DIM
    q = q_in.astype(jnp.float32).reshape(b, s, h, dk)
    v = i_in.astype(jnp.float32).reshape(b, s, h, dv)

    def forget(z, lb):
        lbh = lb.reshape(h, dk)
        f = lbh + (1.0 - lbh) * jax.nn.sigmoid(z.astype(jnp.float32).reshape(b, s, h, dk))
        return 1.0 - f, jnp.log(f)

    k_f, lf_f = forget(f_fwd_in, lb_fwd)
    k_b, lf_b = forget(f_bwd_in, lb_bwd)
    o_fwd = hgrn2_chunk_scan(q, k_f, v, lf_f)
    o_bwd = jnp.flip(hgrn2_chunk_scan(jnp.flip(q, 1), jnp.flip(k_b, 1), jnp.flip(v, 1), jnp.flip(lf_b, 1)), 1)
    o = rmsnorm_2(o_fwd + o_bwd, g_on) * jax.nn.sigmoid(g_in.astype(jnp.float32).reshape(b, s, h, dv))
    return o.reshape(b, s, h * dv).astype(q_in.dtype)

def second_inputs(seed: int = 0) -> dict:
    key = jax.random.key(seed)
    ks = jax.random.split(key, 24)
    L = DEPTH_2
    qk_m = MLA_NOPE + MLA_ROPE

    def nrm(k, shape, scale):
        return jax.random.normal(k, shape, jnp.float32) * scale

    def gain(k, shape):
        return 1.0 + 0.02 * jax.random.normal(k, shape, jnp.float32)

    return {
        'x': nrm(ks[0], (BATCH, SEQ, D_MODEL), 1.0),
        'ln_mix': gain(ks[1], (L, D_MODEL)),
        'w_in': nrm(ks[2], (L, D_MODEL, IN_TOTAL), D_MODEL ** -0.5),
        'mla_g_qa': gain(ks[3], (L, MLA_Q_LORA)),
        'mla_w_uq': nrm(ks[4], (L, MLA_Q_LORA, MLA_HEADS * qk_m), MLA_Q_LORA ** -0.5),
        'mla_g_kva': gain(ks[5], (L, MLA_KV_LORA)),
        'mla_w_ukv': nrm(ks[6], (L, MLA_KV_LORA, MLA_HEADS * (MLA_NOPE + MLA_V)), MLA_KV_LORA ** -0.5),
        'mla_g_qn': gain(ks[7], (L, qk_m)),
        'mla_g_kn': gain(ks[8], (L, qk_m)),
        'diff_g_qn': gain(ks[9], (L, DIFF_HEAD_DIM)),
        'diff_g_kn': gain(ks[10], (L, DIFF_HEAD_DIM)),
        'diff_lq1': nrm(ks[11], (L, DIFF_HEAD_DIM), 0.1),
        'diff_lk1': nrm(ks[12], (L, DIFF_HEAD_DIM), 0.1),
        'diff_lq2': nrm(ks[13], (L, DIFF_HEAD_DIM), 0.1),
        'diff_lk2': nrm(ks[14], (L, DIFF_HEAD_DIM), 0.1),
        'diff_g_sub': gain(ks[15], (L, 2 * DIFF_HEAD_DIM)),
        'hgrn_lb_logits': nrm(ks[16], (2, L, HGRN_HEADS * HGRN_KEY_DIM), 0.5),
        'hgrn_g_on': gain(ks[17], (L, HGRN_VAL_DIM)),
        'w_branch': nrm(ks[18], (L, N_BRANCH, BRANCH_WIDTH, D_MODEL), BRANCH_WIDTH ** -0.5),
        'w_out': nrm(ks[19], (L, D_MODEL, D_MODEL), D_MODEL ** -0.5),
        'ln_ffn': gain(ks[20], (L, D_MODEL)),
        'w_gate_up': nrm(ks[21], (L, D_MODEL, 2 * D_FF_2), D_MODEL ** -0.5),
        'w_down': nrm(ks[22], (L, D_FF_2, D_MODEL), D_FF_2 ** -0.5),
    }

def second_block(x, ln_mix, w_in, mla_g_qa, mla_w_uq, mla_g_kva, mla_w_ukv, mla_g_qn, mla_g_kn,
              diff_g_qn, diff_g_kn, diff_lq1, diff_lk1, diff_lq2, diff_lk2, diff_g_sub,
              hgrn_lb_logits, hgrn_g_on, w_branch, w_out, ln_ffn, w_gate_up, w_down):
    seq_len = x.shape[1]
    cos_m, sin_m = rope_tables(seq_len, MLA_ROPE)
    cos_d, sin_d = rope_tables(seq_len, DIFF_HEAD_DIM)
    lb_p = jax.nn.softmax(hgrn_lb_logits.astype(jnp.float32), axis=1)
    lower_bounds = jnp.cumsum(lb_p, axis=1) - lb_p[:, :1]

    for l in range(DEPTH_2):
        h = rmsnorm_2(x, ln_mix[l])
        z = h @ w_in[l]
        (c_q, c_kv, k_rope, fnet_in, dq, dk, dv,
         hq, hi, hf_fwd, hf_bwd, hg, gate_logits) = split_cols(z, IN_WIDTHS)

        o_mla = mla_mixer(c_q, c_kv, k_rope, mla_g_qa[l], mla_w_uq[l], mla_g_kva[l], mla_w_ukv[l],
                          mla_g_qn[l], mla_g_kn[l], cos_m, sin_m)
        o_fnet = fnet_mixer(fnet_in)
        o_diff = diff_mixer(dq, dk, dv, diff_g_qn[l], diff_g_kn[l], diff_lq1[l], diff_lk1[l],
                            diff_lq2[l], diff_lk2[l], diff_g_sub[l], l, cos_d, sin_d)
        o_hgrn = hgrn2_mixer(hq, hi, hf_fwd, hf_bwd, hg, lower_bounds[0, l], lower_bounds[1, l],
                             hgrn_g_on[l])

        merged = jnp.zeros_like(x)
        for n, o_branch in enumerate((o_mla, o_fnet, o_diff, o_hgrn)):
            gate = jax.nn.sigmoid(gate_logits[..., n * D_MODEL:(n + 1) * D_MODEL].astype(jnp.float32))
            merged = merged + gate.astype(x.dtype) * (o_branch @ w_branch[l, n])
        x = x + merged @ w_out[l]

        h2 = rmsnorm_2(x, ln_ffn[l])
        g_part, u_part = jnp.split(h2 @ w_gate_up[l], 2, axis=-1)
        x = x + (jax.nn.silu(g_part) * u_part) @ w_down[l]
    return x


def setup_inputs(seed=0):
    out = dict(first_inputs(seed))
    for name, value in second_inputs(seed + 1).items():
        if name != "x":
            out[name + "_2"] = value
    return out


def reference(
    x, mem, positions, norm_mix_g, w_in, conv_w, conv_b, rg_a_w, rg_a_b, rg_x_w, rg_x_b,
    rg_lambda, w_out, norm_cross_g, norm_mem_g, w_cq, w_ck, w_cv, w_co, norm_mlp_g, w_mlp_in,
    w_mlp_out, norm_final_g, ln_mix_2, w_in_2, mla_g_qa_2, mla_w_uq_2, mla_g_kva_2, mla_w_ukv_2,
    mla_g_qn_2, mla_g_kn_2, diff_g_qn_2, diff_g_kn_2, diff_lq1_2, diff_lk1_2, diff_lq2_2,
    diff_lk2_2, diff_g_sub_2, hgrn_lb_logits_2, hgrn_g_on_2, w_branch_2, w_out_2, ln_ffn_2,
    w_gate_up_2, w_down_2,
):
    x = first_block(
        x, mem, positions, norm_mix_g, w_in, conv_w, conv_b, rg_a_w, rg_a_b, rg_x_w, rg_x_b,
        rg_lambda, w_out, norm_cross_g, norm_mem_g, w_cq, w_ck, w_cv, w_co, norm_mlp_g,
        w_mlp_in, w_mlp_out, norm_final_g,
    )
    return second_block(
        x, ln_mix_2, w_in_2, mla_g_qa_2, mla_w_uq_2, mla_g_kva_2, mla_w_ukv_2, mla_g_qn_2,
        mla_g_kn_2, diff_g_qn_2, diff_g_kn_2, diff_lq1_2, diff_lk1_2, diff_lq2_2, diff_lk2_2,
        diff_g_sub_2, hgrn_lb_logits_2, hgrn_g_on_2, w_branch_2, w_out_2, ln_ffn_2, w_gate_up_2,
        w_down_2,
    )


_drawn_inputs = setup_inputs


def setup_inputs(seed=0):
    import zlib

    import numpy as np

    out = dict(_drawn_inputs(seed))
    spreads = {}
    factors = {'rg_a_b': 8.0,
     'rg_x_b': 8.0,
     'norm_cross_g': 8.0,
     'norm_mem_g': 4.862,
     'mla_g_qa_2': 8.0,
     'mla_g_kva_2': 8.0,
     'mla_g_qn_2': 8.0,
     'mla_g_kn_2': 8.0,
     'diff_g_qn_2': 8.0,
     'diff_g_kn_2': 8.0,
     'diff_lk2_2': 3.487,
     'diff_g_sub_2': 8.0,
     'hgrn_g_on_2': 7.758,
     'ln_ffn_2': 3.156}
    for name, (base, spread) in spreads.items():
        noise = np.random.default_rng([zlib.crc32(name.encode()), seed]).standard_normal(out[name].shape)
        drawn = base * np.exp(spread * noise) if base else spread * noise
        out[name] = jnp.asarray(drawn.astype(out[name].dtype))
    for name, factor in factors.items():
        out[name] = (out[name] * factor).astype(out[name].dtype)
    return out
```

```python
from contextlib import ExitStack

import numpy as np
import concourse.bass as bass
from concourse import mybir

ALU = mybir.AluOpType
ACT = mybir.ActivationFunctionType
F32 = mybir.dt.float32
BF16 = mybir.dt.bfloat16
I32 = mybir.dt.int32
AX_X = mybir.AxisListType.X

P = 128
D = 1024
S = 256
TT = S // P
KT = D // P
L2 = 2
EPS = 1e-6
UNIT = 4096
RING = 4
RG_C = 8.0
LEVELS = (128, 64, 32, 16, 8, 4, 2, 1)
MASKED = (32, 16, 8, 4, 2, 1, 0)
N_UNITS_1 = 27
N_UNITS_2 = 35
NU = N_UNITS_1 + L2 * N_UNITS_2
LAMBDA_INIT = [0.8 - 0.6 * float(np.exp(-0.3 * l)) for l in range(L2)]
RSQRT_MAGIC = 0x5F3759DF
TWO_PI_HI = 6.28125
TWO_PI_MID = 0.0019350051879882812
TWO_PI_LO = 2.0 * np.pi - TWO_PI_HI - TWO_PI_MID
ROUND = 1.5 * 2.0 ** 23

C_IDENT = 0
C_LOGC = C_IDENT + P
C_FREQ = C_LOGC + TT * S
C_COS = C_FREQ + 1
C_SIN = C_COS + TT * 16
C_DFTD = C_SIN + TT * 16 + 1
C_DFTC = C_DFTD + 2 * P
C_DFTS = C_DFTC + TT * S
C_MASK = C_DFTS + TT * S
C_SIZE = C_MASK + len(MASKED) * P

GAINS = ("norm_mix_g", "norm_cross_g", "norm_mem_g", "norm_mlp_g", "ln_mix_0", "ln_mix_1", "ln_ffn_0", "ln_ffn_1")
V_GAIN = 0
V_CONVW = V_GAIN + len(GAINS) * KT
V_CONVB = V_CONVW + 16
V_RGB = V_CONVB + 4
V_LAM = V_RGB + 16
V_QA = V_LAM + 8
V_LB = V_QA + 4 * L2
V_SIZE = V_LB + 4 * L2

R_FINAL = 0
R_LAYER = D
R_QN, R_DQN, R_SUB, R_ON, R_LQ = 0, 192, 256, 320, 384
R_PER = 512
R_SIZE = R_LAYER + L2 * R_PER

A_HID = 0
A_RG_R, A_RG_I, A_RG_T, A_RG_A = 0, 2048, 4096, 6144
A_MEM = 0
A_Q1 = 8192
A_K1 = A_Q1 + 1024
A_V1 = A_K1 + 1024
A_CK = A_Q1
A_CV = A_V1
A_CQ = A_K1
A_U = A_V1 + 1024
UPAD = S + 3
A_UC = A_U + 4 * UPAD
A_YG = A_UC + 1024
A_RGW = A_YG + 1024
A_ROPE = A_RGW + 16 * P
A_CO = A_ROPE
A_SC1 = A_ROPE + 2048
A_GATE = 0
A_FT, A_AB = 0, 512
A_VC = 4096
A_SG = A_VC + 1024
A_HO = A_SG + 512
A_DO = A_HO + 512
A_HQ = A_DO + 512
A_KK = A_HQ + 1024
A_E = A_KK + 1024
A_F = A_E + 4 * (S + 1)
A_ZB = A_F + 1024
A_DT = A_ZB + 1024
A_SC = A_DT + 1024
A_VM = A_SC + 6 * 512
A_ZA = A_VM + 512
A_CT = A_ZA + 1024
A_Z = A_CT + 1024
A_QKT = A_Z + 1536
A_ST = A_ZA
A_X = A_ST + 2048
A_QL = A_X + 1024
A_KL = A_QL + 1024
A_ACT = 0
ARENA = A_QKT + 2048
assert A_KL + 1024 <= ARENA and A_SC1 + 6 * 512 <= ARENA



def attention_plan():
    heads = [("dil", h, 1) for h in range(8)] + [("cross", h, 1) for h in range(4)]
    for l in range(L2):
        heads += [(f"mla{l}", h, 1) for h in range(4)]
        heads += [(f"diff{l}", h, 2) for h in range(4)]
    plan, unit = {}, 0
    for n, (phase, h, k) in enumerate(heads):
        plan[phase, h] = (n, unit, k)
        unit += k
    return heads, plan, unit


HEADS, ATT, N_SCORES = attention_plan()
EVEN = {n: sum(1 for m in HEADS[:n + 1] if m[0][:3] in ("dil", "mla") and m[1] % 2 == 0) for n in range(len(HEADS))}
HEAD_OF_UNIT = [(phase, h) for phase, h, k in HEADS for _ in range(k)]


def build(nc, x_d, mem_d, pos_d, const_d, vec_d, row_d, rgw_d, units_d, out_d):
    with ExitStack() as ctx:
        def sb(name, shape, dt=F32):
            return ctx.enter_context(nc.sbuf_tensor(name, shape, dt))

        def sem(name):
            return ctx.enter_context(nc.semaphore(name))

        ring = sb("ring", [P, RING, UNIT])
        const = sb("const", [P, C_SIZE])
        vec = sb("vec", [P, V_SIZE])
        row = sb("row", [P, R_SIZE])
        h = sb("h", [P, TT, D])
        xs = sb("xs", [P, TT, D])
        xT = sb("xT", [P, KT, S])
        oT = sb("oT", [P, KT, S])
        W = sb("W", [P, ARENA])
        junk = sb("junk", [P, D], BF16)
        stat = sb("stat", [P, 448])
        psum = [ctx.enter_context(nc.psum_tensor(f"bank{b}", [P, 512], F32)) for b in range(8)]

        def at(off, *dims):
            n = int(np.prod(dims))
            v = W[:, off:off + n]
            if len(dims) == 1:
                return v
            names = "abcd"[:len(dims)]
            return v.rearrange(f"p ({' '.join(names)}) -> p {' '.join(names)}", **dict(zip(names[1:], dims[1:])))

        memT = xs[:].rearrange("p a b -> p (a b)").rearrange("p (k t) -> p k t", k=KT)
        merged = memT
        mixT = oT
        ident = const[:, C_IDENT:C_IDENT + P]
        logc = const[:, C_LOGC:C_LOGC + TT * S].rearrange("p (a k) -> p a k", a=TT)
        vec_lb = vec[:, V_LB:V_LB + 4 * L2].rearrange("p (l h) -> p l h", l=L2)

        cols = {}

        def col(name, n):
            if name not in cols:
                at0 = sum(k for _, k in cols.values())
                assert at0 + n <= 448, at0
                cols[name] = (at0, n)
            at0, n = cols[name]
            return stat[:, at0:at0 + n]

        s_x, s_mem, s_pos, s_const, s_vec, s_row, s_rgw = (sem(n) for n in (
            "x_loaded", "mem_loaded", "positions_loaded", "const_loaded", "vec_loaded", "row_loaded", "rgw_loaded"))
        unit_loaded = [sem(f"unit_loaded{i}") for i in range(RING)]
        filled = [sem(f"filled{b}") for b in range(8)]
        drained = [sem(f"drained{b}") for b in range(8)]
        jobs = {}
        uses = [0] * 8
        last_job = [None] * NU
        dve_link, act_link, pool_link = sem("dve_link"), sem("act_link"), sem("pool_link")
        s_sumsq, s_scaled = sem("sumsq_ready"), sem("scaled_ready")
        s_max, s_exp, s_prob = sem("max_ready"), sem("exp_ready"), sem("prob_ready")
        s_conv, s_rec = sem("conv_ready"), sem("rec_ready")
        s_rgy, s_rgta, s_rgw2, s_rgs = sem("rg_y"), sem("rg_tanh_exp"), sem("rg_w"), sem("rg_sqrt")
        s_sp = sem("softplus_in")
        s_spe = sem("softplus_exp")
        s_ang, s_trig, s_rope = sem("angles_ready"), sem("cos_sin_ready"), sem("rope_done")
        s_even, s_unit = sem("even_value_done"), sem("unit_read")
        s_tok = sem("token_side_ready")
        s_lb, s_lbe, s_f, s_lf, s_hkk = (sem(n) for n in ("lb_in", "lb_exp", "f_ready", "log_f_ready", "hgrn_k_ready"))
        s_E, s_F = sem("E_ready"), sem("F_ready")
        s_Dl, s_Xl, s_Ql, s_Kl, s_zero = (sem(n) for n in ("decay_log", "decay", "q_level", "k_level", "levels_zeroed"))
        s_lam, s_lame = sem("lambda_in"), sem("lambda_exp")
        s_merged = sem("merged_ready")
        s_zero1 = sem("pads_zeroed")
        s_hn, s_out = sem("h_normed"), sem("out_stored")

        def wait_filled(eng, name):
            b, use = jobs[name]
            eng.wait_ge(filled[b], use + 1)
            return psum[b]

        def wait_drained(eng, name):
            b, use = jobs[name]
            eng.wait_ge(drained[b], use + 1)

        def drains(ins, name):
            ins.then_inc(drained[jobs[name][0]], 1)

        def slot(u):
            return ring[:, u % RING, :]

        steps = []
        u = 0

        def proj(name, n=1):
            nonlocal u
            steps.append(("proj", name, u))
            u += n

        def attend(phase, count, filler=()):
            filler = list(filler)
            for i in range(count + 3):
                if i < count:
                    steps.append(("score", phase, i))
                if 1 <= i <= count:
                    steps.append(("prob", phase, i - 1))
                if filler:
                    steps.append(filler.pop(0))
                if 2 <= i <= count + 1:
                    steps.append(("turn", phase, i - 2))
                if 3 <= i:
                    steps.append(("value", phase, i - 3))
            steps.extend(filler)

        steps.append(("setup",))
        steps.append(("norm", "norm_mix_g"))
        proj("q")
        proj("k")
        steps.append(("norm", "norm_mem_g"))
        proj("v")
        proj("u")
        steps.append(("conv",))
        proj("y")
        steps.append(("rggate",))
        attend("dil", 8)
        steps.append(("rg1",))
        proj("ck")
        steps.append(("rg2",))
        proj("cv")
        steps.append(("rg3",))
        proj("wout", 2)
        steps.append(("norm", "norm_cross_g"))
        proj("cq")
        attend("cross", 4)
        proj("co")
        steps.append(("norm", "norm_mlp_g"))
        for i in range(8):
            proj(f"up{i}")
        for i in range(8):
            proj(f"down{i}")
        steps.append(("finalnorm",))
        assert u == N_UNITS_1
        for l in range(L2):
            steps.append(("norm", f"ln_mix_{l}"))
            proj(f"a{l}")
            proj(f"b{l}")
            steps.append(("aturn", l))
            proj(f"d{l}")
            proj(f"c{l}")
            steps.append(("bturn", l))
            proj(f"f{l}")
            steps.append(("zturn", l))
            proj(f"e{l}")
            steps.append(("fnet", l))
            gates = []
            for g in range(4):
                gates.append(("gate", l, g, 0, u))
                gates.append(("gate", l, g, 1, u))
                u += 1
            attend(f"mla{l}", 4, gates[:4])
            attend(f"diff{l}", 4, gates[4:])
            steps.append(("diffout", l))
            lev = [(i, hp) for i in range(len(LEVELS) + 1) for hp in range(2)]
            for i, hp in lev[:6]:
                steps.append(("level", l, i, hp))
            steps.append(("levelflush", l))
            steps.append(("merge", l, 0, u, 0))
            steps.append(("merge", l, 1, u, 1))
            u += 1
            gates = []
            for g in range(4, 8):
                gates.append(("gate", l, g, 0, u))
                gates.append(("gate", l, g, 1, u))
                u += 1
            for n, (i, hp) in enumerate(lev[6:]):
                steps.append(("level", l, i, hp))
                if n % 2 == 1 and gates:
                    steps.append(gates.pop(0))
            steps.append(("levelflush", l))
            steps.append(("hval", l))
            steps.extend(gates)
            steps.append(("hout", l))
            steps.append(("merge", l, 2, u, 0))
            steps.append(("merge", l, 3, u, 1))
            u += 1
            proj(f"wout{l}", 2)
            steps.append(("norm", f"ln_ffn_{l}"))
            for i in range(11):
                proj(f"gu{l}.{i}")
            for i in range(6):
                proj(f"wd{l}.{i}")
        assert u == NU, u
        norms = [s[1] for s in steps if s[0] == "norm"]
        stats = [s[1] if s[0] == "norm" else "final" for s in steps if s[0] in ("norm", "finalnorm")]

        side_order = [(l, what) for l in range(L2) for what in ("a", "b", "z", "do", "ho")]

        def layer_of(name):
            return int(name[1]) if len(name) == 2 and name[1] in "01" else None

        def wait_h(eng, name, tt):
            if name == "ln_mix_0":
                eng.wait_ge(s_hn, tt + 1)
            elif name not in ("norm_mix_g", "norm_mem_g"):
                wait_drained(eng, {"norm_cross_g": f"wout.1.{tt}", "norm_mlp_g": f"co.1.{tt}", "final": f"down.{tt}1", "ln_mix_1": f"wd0.{tt}1",
                                   "ln_ffn_0": f"wout0.1.{tt}", "ln_ffn_1": f"wout1.1.{tt}"}[name])

        block = ctx.enter_context(nc.Block())

        @block.tensor
        def _(pe):
            rot = {"g": 0, "m": 0}
            banks = {"g": (0, 1, 2), "m": (3, 4, 5, 6, 7)}

            def fill(name, group):
                if isinstance(group, int):
                    b = group
                else:
                    b = banks[group][rot[group] % len(banks[group])]
                    rot[group] += 1
                if uses[b]:
                    pe.wait_ge(drained[b], uses[b])
                jobs[name] = (b, uses[b])
                uses[b] += 1
                return psum[b]

            def full(ins, name):
                ins.then_inc(filled[jobs[name][0]], 1)

            seen = set()
            units_read = 0

            def unit(n):
                if n not in seen:
                    seen.add(n)
                    pe.wait_ge(unit_loaded[n % RING], 16 * (n // RING + 1))
                return slot(n)

            def mm(out, lhsT, rhs, first, last):
                return nc.tensor.matmul(out, lhsT, rhs, start=first, stop=last)

            def tok(name, group, src, w, kts, c0, n, un=None):
                for tt in range(TT):
                    bank = fill(f"{name}.{tt}", group)
                    for i, k in enumerate(kts):
                        ins = mm(bank[:, 0:n], src[:, k, tt * P:(tt + 1) * P], w[:, i, c0:c0 + n], i == 0, i == len(kts) - 1)
                    full(ins, f"{name}.{tt}")
                if un is not None:
                    last_job[un] = f"{name}.{TT - 1}"

            def feat(name, group, src, w, cts, un=None):
                for j in range(0, len(cts), 2):
                    job = f"{name}.{j // 2}"
                    bank = fill(job, group)
                    for jj in range(2):
                        c0 = cts[j + jj] * P
                        for k in range(KT):
                            ins = mm(bank[:, jj * S:(jj + 1) * S], w[:, k, c0:c0 + P], src[:, k, :], k == 0, k == KT - 1)
                    full(ins, job)
                if un is not None:
                    last_job[un] = job

            def k8(n):
                return unit(n).rearrange("p (k c) -> p k c", k=8)

            def k4(n):
                return unit(n).rearrange("p (k c) -> p k c", k=4)

            def turns(name, src, tiles, group="m"):
                for j in range(0, tiles, 2):
                    job = f"{name}.{j // 2}"
                    bank = fill(job, group)
                    for jj in range(min(2, tiles - j)):
                        for tt in range(TT):
                            piece = src(j + jj, tt)
                            ins = nc.tensor.transpose(bank[0:piece.shape[1], jj * S + tt * P:jj * S + (tt + 1) * P], piece, ident)
                    full(ins, job)

            def score_operands(phase, hd, j):
                if phase == "dil":
                    q, k = at(A_Q1, 2, 2, S), at(A_K1, 2, 2, S)
                    p0 = 32 * (hd % 4)
                    return [(lambda qt, f=f: q[p0:p0 + 32, hd // 4, f, qt * P:(qt + 1) * P], k[p0:p0 + 32, hd // 4, f, :]) for f in range(2)]
                if phase == "cross":
                    q, k = at(A_CQ, 4, S), at(A_CK, 4, S)
                    return [(lambda qt: q[:, hd, qt * P:(qt + 1) * P], k[:, hd, :])]
                if phase[:3] == "mla":
                    z = at(A_QKT, 8, S)
                    return [(lambda qt: z[0:96, hd, qt * P:(qt + 1) * P], z[0:96, 4 + hd, :])]
                z = at(A_DT, 4, S)
                hh = 2 * hd + j
                p0 = 32 * (hh % 4)
                return [(lambda qt: z[p0:p0 + 32, hh // 4, qt * P:(qt + 1) * P], z[p0:p0 + 32, 2 + hh // 4, :])]

            for step in steps:
                kind = step[0]
                if kind == "setup":
                    pe.wait_ge(s_const, 16)
                elif kind == "norm":
                    name = step[1]
                    pe.wait_ge(s_scaled, norms.index(name) + 1)
                    src = at(A_MEM, TT, D) if name == "norm_mem_g" else xs
                    turns(name, lambda k, tt: src[:, tt, k * P:(k + 1) * P], KT)
                elif kind == "proj":
                    name, n = step[1], step[2]
                    src_norm = {"q": "norm_mix_g", "ck": "norm_mem_g", "cq": "norm_cross_g", "a0": "ln_mix_0", "a1": "ln_mix_1",
                                "up0": "norm_mlp_g", "gu0.0": "ln_ffn_0", "gu1.0": "ln_ffn_1"}.get(name)
                    if src_norm:
                        for j in range(KT // 2):
                            wait_drained(pe, f"{src_norm}.{j}")
                    if name in ("q", "k", "u", "y", "cq"):
                        feat(name, "g", xT, k8(n), range(4), n)
                    elif name == "v":
                        tok(name, "g", xT, k8(n), range(KT), 0, 512, n)
                    elif name == "ck":
                        feat(name, "g", memT, k8(n), range(4), n)
                    elif name == "cv":
                        tok(name, "g", memT, k8(n), range(KT), 0, 512, n)
                    elif name[:4] == "wout":
                        if name == "wout":
                            for p in range(4):
                                wait_drained(pe, f"value.dil{p}")
                            pe.wait_ge(s_rec, 1)
                            src = mixT
                        else:
                            pe.wait_ge(s_merged, 2 * (int(name[4:]) + 1))
                            src = merged
                        for j in range(2):
                            tok(f"{name}.{j}", "g", src, k8(n + j), range(KT), 0, 512, n + j)
                    elif name == "co":
                        co = at(A_CO, 4, S)
                        for p in range(4):
                            wait_drained(pe, f"value.cross{p}")
                        for j in range(2):
                            tok(f"co.{j}", "g", co, k4(n), range(4), 512 * j, 512, n)
                    elif name[:2] == "up":
                        feat(name, "m", xT, k8(n), range(4), n)
                    elif name[:4] == "down" or name[:2] == "wd":
                        if name[:4] == "down":
                            i, count, src, tag = int(name[4:]), 8, at(A_HID, 32, S), "down"
                        else:
                            i, count, src, tag = int(name[4:]), 6, at(A_ACT, 22, S), name[:3]
                        w = k4(n)
                        if i == 0:
                            acc = {(tt, j): fill(f"{tag}.{tt}{j}", 2 * tt + j) for tt in range(TT) for j in range(2)}
                        ks = range(4 * i, min(4 * i + 4, 32 if tag == "down" else 22))
                        for k in ks[::2]:
                            wait_drained(pe, f"up{k // 4}.{k // 2 % 2}" if tag == "down" else f"gu{name[2]}.{k // 2}.1")
                        for tt in range(TT):
                            for j in range(2):
                                for k in ks:
                                    ins = mm(acc[tt, j][:, :], src[:, k, tt * P:(tt + 1) * P], w[:, k - 4 * i, 512 * j:512 * j + 512],
                                             k == 0, i == count - 1 and k == ks[-1])
                                if i == count - 1:
                                    full(ins, f"{tag}.{tt}{j}")
                        if i < count - 1:
                            ins.then_inc(s_unit, 1)
                            units_read += 1
                            last_job[n] = units_read
                        else:
                            last_job[n] = f"{tag}.11"
                    elif name[0] in "abc":
                        tok(name, "g", xT, k8(n), range(KT), 0, 512, n)
                    elif name[0] == "d":
                        l = name[1]
                        w = unit(n)
                        wd = w[:, 0:8 * 288].rearrange("p (k c) -> p k c", k=8)
                        tok(name, "g", xT, wd, range(KT), 0, 288)
                        cT = at(A_CT, 4, S)
                        for j in range(2):
                            wait_drained(pe, f"aturn{l}.{j}")
                        wuq = w[:, 2304:2304 + 1152].rearrange("p (k c) -> p k c", k=3)
                        tok(f"uq{l}", "m", cT, wuq, range(3), 0, 384)
                        wukv = w[:, 3456:3968].rearrange("p (k c) -> p k c", k=1)
                        tok(f"ukv{l}", "m", cT, wukv, [3], 0, 512, n)
                    elif name[0] in "ef":
                        feat(name, "g", xT, k8(n), range(4), n)
                    elif name[:2] == "gu":
                        feat(name, "m", xT, k8(n), range(4), n)
                elif kind == "rggate":
                    pe.wait_ge(s_rgw, 16)
                    pe.wait_ge(s_conv, 1)
                    rgw = at(A_RGW, 2, 4, 2, P)
                    uc = at(A_UC, 4, S)
                    for z in range(2):
                        for ct in range(4):
                            name = f"rg.{z}{ct}"
                            bank = fill(name, "m")
                            for ax in range(2):
                                ins = mm(bank[:, ax * S:(ax + 1) * S], rgw[:, z, ct, ax, :], uc[:, ct, :], True, True)
                            full(ins, name)
                elif kind == "score":
                    phase, hd = step[1:]
                    _, a0, count = ATT[phase, hd]
                    if hd == 0:
                        for name in {"dil": ["rope"], "cross": ["cq.0", "cq.1", "ck.0", "ck.1"], "mla": [f"zturn{phase[-1]}.{j}" for j in range(4)],
                                     "dif": [f"bturn{phase[-1]}.{j}" for j in range(2)]}[phase[:3] if phase != "cross" else phase]:
                            if name == "rope":
                                pe.wait_ge(s_rope, 1)
                                for tt in range(TT):
                                    wait_drained(pe, f"v.{tt}")
                            else:
                                wait_drained(pe, name)
                    for j in range(count):
                        name = f"score{a0 + j}"
                        bank = fill(name, "m")
                        ops = score_operands(phase, hd, j)
                        for qt in range(TT):
                            for f, (lhs, rhs) in enumerate(ops):
                                ins = mm(bank[:, qt * S:(qt + 1) * S], lhs(qt), rhs, f == 0, f == len(ops) - 1)
                        full(ins, name)
                elif kind == "turn":
                    phase, hd = step[1:]
                    n, a0, count = ATT[phase, hd]
                    pe.wait_ge(s_prob, n + 1)
                    name = f"turn{n}"
                    bank = fill(name, "m")
                    base = A_SC1 if phase in ("dil", "cross") else A_SC
                    prob = at(base + 512 * (a0 % 4), TT, S)
                    for kt in range(TT):
                        for qt in range(TT):
                            ins = nc.tensor.transpose(bank[:, kt * S + qt * P:kt * S + (qt + 1) * P], prob[:, qt, kt * P:(kt + 1) * P], ident)
                    full(ins, name)
                elif kind == "value":
                    phase, hd = step[1:]
                    n, a0, count = ATT[phase, hd]
                    wait_drained(pe, f"turn{n}")
                    base = A_SC1 if phase in ("dil", "cross") else A_SC
                    pT = at(base + 2048 + 512 * (n % 2), TT, S)
                    if phase == "dil" or phase[:3] == "mla":
                        v = at(A_V1, TT, 512) if phase == "dil" else at(A_VM, TT, 256)
                        name = f"value.{phase}{hd // 2}"
                        if hd % 2 == 0:
                            bank = fill(name, "m")
                        else:
                            bank = psum[jobs[name][0]]
                        p0 = 64 * (hd % 2)
                        for kt in range(TT):
                            ins = mm(bank[p0:p0 + 64, 0:S], v[:, kt, 64 * hd:64 * hd + 64], pT[:, kt, :], kt == 0, kt == TT - 1)
                        if hd % 2:
                            full(ins, name)
                        else:
                            ins.then_inc(s_even, 1)
                    elif phase == "cross":
                        v = at(A_CV, TT, 512)
                        if hd == 0:
                            for tt in range(TT):
                                wait_drained(pe, f"cv.{tt}")
                        name = f"value.cross{hd}"
                        bank = fill(name, "m")
                        for kt in range(TT):
                            ins = mm(bank[:, 0:S], v[:, kt, P * hd:P * hd + P], pT[:, kt, :], kt == 0, kt == TT - 1)
                        full(ins, name)
                    else:
                        v = at(A_VC, TT, 512)
                        if hd == 0:
                            for tt in range(TT):
                                wait_drained(pe, f"c{phase[4]}.{tt}")
                        name = f"value.{phase}{hd}"
                        bank = fill(name, "m")
                        for qt in range(TT):
                            for kt in range(TT):
                                ins = mm(bank[:, qt * P:(qt + 1) * P], pT[:, kt, qt * P:(qt + 1) * P], v[:, kt, P * (hd // 2):P * (hd // 2) + P],
                                         kt == 0, kt == TT - 1)
                        full(ins, name)
                elif kind == "aturn":
                    l = step[1]
                    pe.wait_ge(s_tok, side_order.index((l, "a")) + 1)
                    za = at(A_ZA, TT, 512)
                    turns(f"aturn{l}", lambda k, tt: za[:, tt, k * P:(k + 1) * P], 4)
                elif kind == "bturn":
                    l = step[1]
                    pe.wait_ge(s_tok, side_order.index((l, "b")) + 1)
                    zb = at(A_ZB, TT, 512)
                    turns(f"bturn{l}", lambda k, tt: zb[:, tt, k * P:(k + 1) * P], 4)
                elif kind == "zturn":
                    l = step[1]
                    pe.wait_ge(s_tok, side_order.index((l, "z")) + 1)
                    z = at(A_Z, TT, 8, 96)
                    turns(f"zturn{l}", lambda k, tt: z[:, tt, k, :], 8)
                elif kind == "diffout":
                    l = step[1]
                    pe.wait_ge(s_tok, side_order.index((l, "do")) + 1)
                    do = at(A_DO, TT, 256)
                    turns(f"diffout{l}", lambda k, tt: do[:, tt, k * P:(k + 1) * P], 2)
                elif kind == "hout":
                    l = step[1]
                    pe.wait_ge(s_tok, side_order.index((l, "ho")) + 1)
                    ho = at(A_HO, TT, 256)
                    turns(f"hout{l}", lambda k, tt: ho[:, tt, k * P:(k + 1) * P], 2)
                elif kind == "fnet":
                    l = step[1]
                    fT, ab = at(A_FT, 2, S), at(A_AB, TT, 2, S)
                    dftd = const[:, C_DFTD:C_DFTD + 2 * P]
                    dc = const[:, C_DFTC:C_DFTC + TT * S].rearrange("p (s t) -> p s t", s=TT)
                    ds = const[:, C_DFTS:C_DFTS + TT * S].rearrange("p (s t) -> p s t", s=TT)
                    wait_drained(pe, f"e{l}.0")
                    for st in range(TT):
                        bank = fill(f"fab{l}.{st}", "m")
                        for ft in range(2):
                            ins = mm(bank[:, ft * S:(ft + 1) * S], fT[:, ft, st * P:(st + 1) * P], dftd, True, True)
                        full(ins, f"fab{l}.{st}")
                    for st in range(TT):
                        wait_drained(pe, f"fab{l}.{st}")
                    bank = fill(f"fy{l}", "m")
                    for ft in range(2):
                        for st in range(TT):
                            mm(bank[:, ft * S:(ft + 1) * S], ab[:, st, ft, 0:P], dc[:, st, :], st == 0, False)
                            ins = mm(bank[:, ft * S:(ft + 1) * S], ab[:, st, ft, P:2 * P], ds[:, st, :], False, st == TT - 1)
                    full(ins, f"fy{l}")
                elif kind == "gate":
                    _, l, g, half, n = step
                    w = k8(n)
                    job = f"gate{l}.{g}{half}"
                    bank = fill(job, "g")
                    for jj in range(2):
                        c0 = (2 * half + jj) * P
                        for k in range(KT):
                            ins = mm(bank[:, jj * S:(jj + 1) * S], w[:, k, c0:c0 + P], xT[:, k, :], k == 0, k == KT - 1)
                    full(ins, job)
                    if half:
                        last_job[n] = job
                elif kind == "merge":
                    _, l, br, n, part = step
                    if br == 0:
                        for j in range(2):
                            wait_drained(pe, f"value.mla{l}{j}")
                    elif br == 1:
                        wait_drained(pe, f"fy{l}")
                    elif br == 2:
                        wait_drained(pe, f"diffout{l}.0")
                    else:
                        wait_drained(pe, f"hout{l}.0")
                    w = unit(n)[:, part * 2048:(part + 1) * 2048].rearrange("p (k c) -> p k c", k=2)
                    for j in range(4):
                        job = f"merge{l}.{br}{j}"
                        bank = fill(job, "g")
                        for jj in range(2):
                            for k in range(2):
                                c0 = (2 * j + jj) * P
                                ins = mm(bank[:, jj * S:(jj + 1) * S], w[:, k, c0:c0 + P], oT[:, 2 * br + k, :], k == 0, k == 1)
                        full(ins, job)
                    if part:
                        last_job[n] = job
                elif kind == "level":
                    _, l, i, hp = step
                    job = f"level{l}.{i}{hp}"
                    if i < len(LEVELS):
                        idx = (l * len(LEVELS) + i) * 2 + hp
                        pe.wait_ge(s_Ql, idx + 1)
                        pe.wait_ge(s_Kl, idx + 1)
                        q = at(A_QL + 512 * (idx % 2), 2, S)
                        k = at(A_KL + 512 * (idx % 2), 2, S)
                        q0 = 0
                    else:
                        q, k, q0 = at(A_HQ, 4, S), at(A_KK, 4, S), 2 * hp
                        pe.wait_ge(s_hkk, l + 1)
                        wait_drained(pe, f"e{l}.1")
                    bank = fill(job, "m")
                    for hh in range(2):
                        for st in range(TT):
                            t0 = 1 - st if i == 0 else st
                            ins = mm(bank[:, (2 * hh + st) * P:(2 * hh + st + 1) * P], k[:, q0 + hh, st * P:(st + 1) * P],
                                     q[:, q0 + hh, t0 * P:(t0 + 1) * P], True, True)
                    full(ins, job)
                elif kind == "hval":
                    l = step[1]
                    sT, v = at(A_ST, 4, TT, S), at(A_VC, TT, 512)
                    for hp in range(2):
                        wait_drained(pe, f"level{l}.{len(LEVELS)}{hp}")
                        job = f"hval{l}.{hp}"
                        bank = fill(job, "m")
                        for tt in range(TT):
                            for hh in range(2):
                                for st in range(TT):
                                    ins = mm(bank[:, (2 * tt + hh) * P:(2 * tt + hh + 1) * P], sT[:, 2 * hp + hh, st, tt * P:(tt + 1) * P],
                                             v[:, st, 256 + hp * P:256 + (hp + 1) * P], st == 0, st == TT - 1)
                        full(ins, job)

        @block.sync
        def _(sp):
            sp.dma_start(h[:], x_d.rearrange("(t p) d -> p t d", p=P)).then_inc(s_x, 16)
            sp.dma_start(vec[:], vec_d).then_inc(s_vec, 16)
            sp.dma_start(const[:], const_d).then_inc(s_const, 16)

            def load_unit(n):
                if n >= RING:
                    last = last_job[n - RING]
                    if isinstance(last, int):
                        sp.wait_ge(s_unit, last)
                    else:
                        wait_filled(sp, last)
                sp.dma_start(slot(n), units_d[n]).then_inc(unit_loaded[n % RING], 16)

            load_unit(0)
            sp.dma_start(at(A_ROPE, S).bitcast(I32), pos_d).then_inc(s_pos, 16)
            load_unit(1)
            sp.dma_start(at(A_MEM, TT, D), mem_d.rearrange("(t p) d -> p t d", p=P)).then_inc(s_mem, 16)
            load_unit(2)
            sp.dma_start(at(A_RGW, 16 * P), rgw_d).then_inc(s_rgw, 16)
            load_unit(3)
            sp.dma_start(row[:], row_d).then_inc(s_row, 16)
            for n in range(RING, NU):
                load_unit(n)
            for tt in range(TT):
                wait_drained(sp, f"wd1.{tt}1")
                sp.dma_start(out_d[tt * P:(tt + 1) * P, :], h[:, tt, :]).then_inc(s_out, 16)
            sp.wait_ge(s_out, 16 * TT)

        @block.gpsimd
        def _(pool):
            n_link = 0

            def link(ins):
                nonlocal n_link
                n_link += 1
                ins.then_inc(pool_link, 1)
                pool.wait_ge(pool_link, n_link)

            up = at(A_U, 4, UPAD)
            link(nc.gpsimd.memset(up[:, :, 0:2], 0.0))
            nc.gpsimd.memset(up[:, :, S + 2:S + 3], 0.0).then_inc(s_zero1, 1)
            for step in steps:
                if step[0] == "level" and step[2] < len(LEVELS):
                    _, l, i, hp = step
                    idx = (l * len(LEVELS) + i) * 2 + hp
                    half = LEVELS[i]
                    if idx >= 2:
                        prev = idx - 2
                        wait_filled(pool, f"level{prev // (2 * len(LEVELS))}.{prev // 2 % len(LEVELS)}{prev % 2}")
                    if i == 0:
                        wait_filled(pool, f"score{ATT[f'mla{l}', 3][1]}")
                        wait_filled(pool, f"zturn{l}.3")
                        wait_drained(pool, f"zturn{l}.3")
                    q, k = at(A_QL + 512 * (idx % 2), 2 * S), at(A_KL + 512 * (idx % 2), 2 * S)
                    if idx:
                        pool.wait_ge(s_Kl, idx)
                    nc.gpsimd.memset(q, 0.0).then_inc(s_zero, 1)
                    pool.wait_ge(s_zero, idx + 1)
                    link(nc.gpsimd.memset(k, 0.0))
                    pool.wait_ge(s_Xl, idx + 1)
                    x = at(A_X + 512 * (idx % 2), 2 * S).rearrange("p (b w c) -> p b w c", w=2, c=half)
                    kk = at(A_KK, 4 * S)[:, hp * 512:(hp + 1) * 512].rearrange("p (b w c) -> p b w c", w=2, c=half)
                    kl = k.rearrange("p (b w c) -> p b w c", w=2, c=half)
                    link(nc.gpsimd.tensor_tensor(kl[0:64, :, 0, :], kk[0:64, :, 0, :], x[0:64, :, 0, :], ALU.mult))
                    nc.gpsimd.tensor_tensor(kl[64:128, :, 1, :], kk[64:128, :, 1, :], x[64:128, :, 1, :], ALU.mult).then_inc(s_Kl, 1)

        @block.scalar
        def _(act):
            n_link = 0

            def link(ins):
                nonlocal n_link
                n_link += 1
                ins.then_inc(act_link, 1)
                act.wait_ge(act_link, n_link)

            def copy(out, in_, scale=1.0):
                return nc.scalar.activation(out, in_, ACT.Copy, scale=scale)

            def bank2(bank):
                return bank[:].rearrange("p (a t) -> p a t", a=2)

            for step in steps:
                kind = step[0]
                if kind == "setup":
                    pass
                elif kind == "norm" or kind == "finalnorm":
                    name = step[1] if kind == "norm" else "final"
                    src = at(A_MEM, TT, D) if name == "norm_mem_g" else h
                    if name == "norm_mix_g":
                        act.wait_ge(s_x, 16)
                    elif name == "norm_mem_g":
                        act.wait_ge(s_mem, 16)
                    ss = col("ss." + name, TT)
                    for tt in range(TT):
                        wait_h(act, name, tt)
                        ins = nc.scalar.activation(junk[:], src[:, tt, :], ACT.Square, accum_out=ss[:, tt:tt + 1])
                        if tt < TT - 1:
                            link(ins)
                        else:
                            ins.then_inc(s_sumsq, 1)
                    if kind == "norm":
                        if name == "norm_mix_g":
                            act.wait_ge(s_vec, 16)
                        dst = memT if name == "norm_mem_g" else xT
                        gi = V_GAIN + GAINS.index(name) * KT
                        for j in (1, 3):
                            bank = bank2(wait_filled(act, f"{name}.{j}"))
                            copy(dst[:, 2 * j, :], bank[:, 0, :], vec[:, gi + 2 * j:gi + 2 * j + 1])
                            drains(copy(dst[:, 2 * j + 1, :], bank[:, 1, :], vec[:, gi + 2 * j + 1:gi + 2 * j + 2]), f"{name}.{j}")
                    if name == "norm_mix_g":
                        act.wait_ge(s_ang, 1)
                        cs = at(A_ROPE, 2 * S)
                        nc.scalar.activation(cs, cs, ACT.Sin).then_inc(s_trig, 1)
                elif kind == "proj":
                    name = step[1]
                    if name == "v":
                        v = at(A_V1, TT, 512)
                        for tt in range(TT):
                            drains(copy(v[:, tt, :], wait_filled(act, f"v.{tt}")[:]), f"v.{tt}")
                    elif name == "u":
                        up = at(A_U, 4, UPAD)
                        for j in range(2):
                            drains(copy(up[:, 2 * j:2 * j + 2, 2:2 + S], bank2(wait_filled(act, f"u.{j}"))), f"u.{j}")
                    elif name == "y":
                        yg = at(A_YG, 4, S)
                        for j in range(2):
                            bank = bank2(wait_filled(act, f"y.{j}"))
                            drains(nc.scalar.activation(yg[:, 2 * j:2 * j + 2, :], bank, ACT.Gelu_apprx_tanh), f"y.{j}")
                    elif name in ("ck", "cq"):
                        if name == "ck":
                            wait_filled(act, "value.dil3")
                        dst = at(A_CK if name == "ck" else A_CQ, 4, S)
                        for j in range(2):
                            drains(copy(dst[:, 2 * j:2 * j + 2, :], bank2(wait_filled(act, f"{name}.{j}"))), f"{name}.{j}")
                    elif name == "cv":
                        v = at(A_CV, TT, 512)
                        for tt in range(TT):
                            drains(copy(v[:, tt, :], wait_filled(act, f"cv.{tt}")[:]), f"cv.{tt}")
                    elif name[:2] == "up":
                        i = int(name[2:])
                        hid = at(A_HID, 32, S)
                        for j in range(2):
                            bank = bank2(wait_filled(act, f"{name}.{j}"))
                            k = 4 * i + 2 * j
                            link(nc.scalar.activation(hid[:, k:k + 2, :], bank, ACT.Relu))
                            drains(nc.scalar.activation(hid[:, k:k + 2, :], hid[:, k:k + 2, :], ACT.Square), f"{name}.{j}")
                    elif layer_of(name) is not None and name[0] == "a":
                        l = layer_of(name)
                        za = at(A_ZA, TT, 512)
                        if l:
                            wait_filled(act, "hval0.1")
                        ss = col(f"ss.a{l}", 2 * TT)
                        for tt in range(TT):
                            bank = wait_filled(act, f"a{l}.{tt}")
                            copy(za[:, tt, :], bank[:])
                            nc.scalar.activation(junk[:, 512 * tt:512 * tt + 384], bank[:, 0:384], ACT.Square, scale=384.0 ** -0.5, accum_out=ss[:, 2 * tt:2 * tt + 1])
                            drains(nc.scalar.activation(junk[:, 512 * tt + 384:512 * tt + 512], bank[:, 384:512], ACT.Square, scale=128.0 ** -0.5,
                                                        accum_out=ss[:, 2 * tt + 1:2 * tt + 2]), f"a{l}.{tt}")
                    elif layer_of(name) is not None and name[0] in "bc":
                        dst = at(A_ZB if name[0] == "b" else A_VC, TT, 512)
                        for tt in range(TT):
                            drains(copy(dst[:, tt, :], wait_filled(act, f"{name}.{tt}")[:]), f"{name}.{tt}")
                    elif layer_of(name) is not None and name[0] == "d":
                        l = layer_of(name)
                        z = at(A_Z, TT, 8, 96)
                        sg = at(A_SG, TT, 256)
                        for tt in range(TT):
                            bank = wait_filled(act, f"d{l}.{tt}")
                            copy(z[:, tt, 4:8, 64:96], bank[:, None, 0:32].broadcast_to([P, 4, 32]))
                            drains(nc.scalar.activation(sg[:, tt, :], bank[:, 32:288], ACT.Tanh, scale=0.5), f"d{l}.{tt}")
                        for tt in range(TT):
                            bank = wait_filled(act, f"uq{l}.{tt}")
                            drains(copy(z[:, tt, 0:4, :], bank[:, 0:384].rearrange("p (h d) -> p h d", h=4)), f"uq{l}.{tt}")
                        vm = at(A_VM, TT, 256)
                        for tt in range(TT):
                            bank = wait_filled(act, f"ukv{l}.{tt}")
                            copy(z[:, tt, 4:8, 0:64], bank[:, 0:256].rearrange("p (h d) -> p h d", h=4))
                            drains(copy(vm[:, tt, :], bank[:, 256:512]), f"ukv{l}.{tt}")
                    elif layer_of(name) is not None and name[0] == "f":
                        l = layer_of(name)
                        kk = at(A_KK, 4, S)
                        for j in range(2):
                            bank = bank2(wait_filled(act, f"f{l}.{j}"))
                            drains(nc.scalar.activation(kk[:, 2 * j:2 * j + 2, :], bank, ACT.Sigmoid), f"f{l}.{j}")
                        act.wait_ge(s_f, l + 1)
                        nc.scalar.activation(at(A_F, 4 * S), at(A_F, 4 * S), ACT.Ln).then_inc(s_lf, 1)
                    elif layer_of(name) is not None and name[0] == "e":
                        l = layer_of(name)
                        fT, hq = at(A_FT, 2, S), at(A_HQ, 4, S)
                        if l:
                            wait_filled(act, "wd0.11")
                        drains(copy(fT, bank2(wait_filled(act, f"e{l}.0"))), f"e{l}.0")
                        bank = wait_filled(act, f"e{l}.1")
                        for hd in range(4):
                            for d in range(2):
                                src = bank[64 * (hd % 2):64 * (hd % 2) + 64, S * (hd // 2):S * (hd // 2) + S]
                                ins = copy(hq[64 * d:64 * d + 64, hd, :], src)
                        drains(ins, f"e{l}.1")
                    elif name[:2] == "gu":
                        l, i = int(name[2]), int(name[4:])
                        a = at(A_ACT, 22, S)
                        drains(nc.scalar.activation(a[:, 2 * i:2 * i + 2, :], bank2(wait_filled(act, f"{name}.0")), ACT.Silu), f"{name}.0")
                elif kind == "rggate":
                    r, ii = at(A_RG_R, 2, 4, S), at(A_RG_I, 2, 4, S)
                    wait_drained(act, "norm_mem_g.3")
                    for z in range(2):
                        for ct in range(4):
                            name = f"rg.{z}{ct}"
                            bank = bank2(wait_filled(act, name))
                            b0 = V_RGB + (z * 4 + ct) * 2
                            nc.scalar.activation(r[:, z, ct, :], bank[:, 0, :], ACT.Sigmoid, bias=vec[:, b0:b0 + 1])
                            drains(nc.scalar.activation(ii[:, z, ct, :], bank[:, 1, :], ACT.Sigmoid, bias=vec[:, b0 + 1:b0 + 2]), name)
                    act.wait_ge(s_sp, 1)
                    nc.scalar.activation(col("sp.x", 8), col("sp.na", 8), ACT.Exp).then_inc(s_spe, 1)
                    act.wait_ge(s_lb, 1)
                    nc.scalar.activation(col("lb.x", 8), col("lb.e", 8), ACT.Exp).then_inc(s_lbe, 1)
                elif kind == "rg1":
                    act.wait_ge(s_rgy, 1)
                    nc.scalar.activation(at(A_RG_T, 2048), at(A_RG_R, 2048), ACT.Tanh)
                    nc.scalar.activation(at(A_RG_A, 2048), at(A_RG_R, 2048), ACT.Exp, scale=-1.0).then_inc(s_rgta, 1)
                elif kind == "rg2":
                    act.wait_ge(s_rgw2, 1)
                    nc.scalar.activation(at(A_RG_T, 2048), at(A_RG_T, 2048), ACT.Sqrt).then_inc(s_rgs, 1)
                elif kind == "score":
                    phase, hd = step[1:]
                    n, a0, count = ATT[phase, hd]
                    masked = phase == "dil"
                    scale = {"dil": 1.0, "cro": 128.0 ** -0.5, "mla": 96.0 ** -0.5, "dif": 32.0 ** -0.5}[phase[:3]]
                    base = A_SC1 if phase in ("dil", "cross") else A_SC
                    if phase[:4] == "diff" and hd == 0:
                        act.wait_ge(s_lam, int(phase[4]) + 1)
                        nc.scalar.activation(col(f"lam.e{phase[4]}", 2), col(f"lam.d{phase[4]}", 2), ACT.Exp).then_inc(s_lame, 1)
                    for j in range(count):
                        a = a0 + j
                        sc = at(base + 512 * (a % 4), TT, S)
                        act.wait_ge(s_max, a + 1)
                        if not masked:
                            if a >= 4:
                                n4 = ATT[HEAD_OF_UNIT[a - 4]][0]
                                wait_filled(act, f"turn{n4}")
                            src = bank2(wait_filled(act, f"score{a}"))
                        else:
                            src = sc
                        nm, sm = col(f"nmax{a % 16}", TT), col(f"sum{a % 16}", TT)
                        for qt in range(TT):
                            ins = nc.scalar.activation(sc[:, qt, :], src[:, qt, :], ACT.Exp, bias=nm[:, qt:qt + 1], scale=scale, accum_out=sm[:, qt:qt + 1])
                        if masked:
                            ins.then_inc(s_exp, 1)
                        else:
                            drains(ins, f"score{a}")
                elif kind == "turn":
                    phase, hd = step[1:]
                    n, a0, count = ATT[phase, hd]
                    base = A_SC1 if phase in ("dil", "cross") else A_SC
                    pT = at(base + 2048 + 512 * (n % 2), 512)
                    if n >= 2:
                        ph, h2, _ = HEADS[n - 2]
                        if ph in ("cross", "diff0", "diff1"):
                            wait_filled(act, f"value.{ph}{h2}")
                        elif h2 % 2:
                            wait_filled(act, f"value.{ph}{h2 // 2}")
                        else:
                            act.wait_ge(s_even, EVEN[n - 2])
                    drains(copy(pT, wait_filled(act, f"turn{n}")[:]), f"turn{n}")
                elif kind == "value":
                    phase, hd = step[1:]
                    if phase == "cross":
                        name = f"value.cross{hd}"
                        drains(copy(at(A_CO, 4, S)[:, hd, :], wait_filled(act, name)[:, 0:S]), name)
                    elif phase[:4] == "diff":
                        name = f"value.{phase}{hd}"
                        do = at(A_DO, TT, 4, 64)
                        bank = wait_filled(act, name)[:, 0:256].rearrange("p (q c) -> p q c", q=2)
                        drains(copy(do[:, :, hd, :], bank[:, :, 64 * (hd % 2):64 * (hd % 2) + 64]), name)
                    elif hd % 2:
                        name = f"value.{phase}{hd // 2}"
                        drains(copy(oT[:, hd // 2, :], wait_filled(act, name)[:, 0:S]), name)
                elif kind == "aturn":
                    l = step[1]
                    cT = at(A_CT, 4, S)
                    for j in range(2):
                        bank = bank2(wait_filled(act, f"aturn{l}.{j}"))
                        for jj in range(2):
                            k = 2 * j + jj
                            ins = copy(cT[:, k, :], bank[:, jj, :], vec[:, V_QA + 4 * l + k:V_QA + 4 * l + k + 1])
                        drains(ins, f"aturn{l}.{j}")
                elif kind == "bturn":
                    l = step[1]
                    dT = at(A_DT, 4, S)
                    for j in range(2):
                        drains(copy(dT[:, 2 * j:2 * j + 2, :], bank2(wait_filled(act, f"bturn{l}.{j}"))), f"bturn{l}.{j}")
                elif kind == "zturn":
                    l = step[1]
                    z = at(A_QKT, 8, S)
                    for j in range(4):
                        bank = bank2(wait_filled(act, f"zturn{l}.{j}"))
                        drains(copy(z[0:96, 2 * j:2 * j + 2, :], bank[0:96, :, :]), f"zturn{l}.{j}")
                elif kind == "fnet":
                    l = step[1]
                    ab = at(A_AB, TT, 2, S)
                    for st in range(TT):
                        drains(copy(ab[:, st, :, :], bank2(wait_filled(act, f"fab{l}.{st}"))), f"fab{l}.{st}")
                    drains(copy(oT[:, 2:4, :], bank2(wait_filled(act, f"fy{l}"))), f"fy{l}")
                elif kind == "gate":
                    _, l, g, half, n = step
                    gate = at(A_GATE, 16, S)
                    k = (4 * g + 2 * half) % 16
                    if g >= 4:
                        act.wait_ge(s_merged, 2 * l + 1)
                    drains(nc.scalar.activation(gate[:, k:k + 2, :], bank2(wait_filled(act, f"gate{l}.{g}{half}")), ACT.Tanh, scale=0.5), f"gate{l}.{g}{half}")
                elif kind in ("diffout", "hout"):
                    l = step[1]
                    k = 4 if kind == "diffout" else 6
                    drains(copy(oT[:, k:k + 2, :], bank2(wait_filled(act, f"{kind}{l}.0"))), f"{kind}{l}.0")
                elif kind == "level" and step[2] < len(LEVELS):
                    _, l, i, hp = step
                    idx = (l * len(LEVELS) + i) * 2 + hp
                    act.wait_ge(s_Dl, idx + 1)
                    x = at(A_X + 512 * (idx % 2), 512)
                    nc.scalar.activation(x, x, ACT.Exp).then_inc(s_Xl, 1)
                elif kind == "hval":
                    l = step[1]
                    ho = at(A_HO, TT, 4, 64)
                    for hp in range(2):
                        name = f"hval{l}.{hp}"
                        bank = wait_filled(act, name)[:].rearrange("p (t h c) -> p t h c", t=2, h=2)
                        copy(ho[:, :, 2 * hp, :], bank[:, :, 0, 0:64])
                        drains(copy(ho[:, :, 2 * hp + 1, :], bank[:, :, 1, 64:128]), name)

        @block.vector
        def _(dve):
            n_link = 0
            v = nc.vector

            def link(ins):
                nonlocal n_link
                n_link += 1
                ins.then_inc(dve_link, 1)
                dve.wait_ge(dve_link, n_link)

            def bank2(bank):
                return bank[:].rearrange("p (a t) -> p a t", a=2)

            def rsqrt(x, y, t, n):
                link(v.tensor_scalar(t.bitcast(I32), x.bitcast(I32), 1, None, ALU.logical_shift_right))
                link(v.tensor_scalar(y.bitcast(I32), t.bitcast(I32), -1.0, float(RSQRT_MAGIC), ALU.mult, ALU.add))
                for _ in range(3):
                    link(v.tensor_tensor(t, y, y, ALU.mult))
                    link(v.scalar_tensor_tensor(t, t, -0.5, x, ALU.mult, ALU.mult))
                    link(v.scalar_tensor_tensor(y, t, 1.5, y, ALU.add, ALU.mult))

            def heads_norm(zv, groups, n, scratch):
                sq = scratch[:, 0:groups * n].rearrange("p (a g n) -> p a g n", a=TT, n=n)
                ss, rs, t = col("hn.ss", 32)[:, 0:groups], col("hn.rs", 32)[:, 0:groups], col("hn.t", 32)[:, 0:groups]
                link(v.tensor_tensor(sq, zv, zv, ALU.mult))
                link(v.tensor_reduce(ss, sq.rearrange("p a g n -> p (a g) n"), AX_X, ALU.add))
                link(v.tensor_scalar(ss, ss, 1.0 / n, EPS, ALU.mult, ALU.add))
                rsqrt(ss, rs, t, groups)
                return rs

            def rope32(x1, x2, heads):
                c = const[:, C_COS:C_COS + TT * 16].rearrange("p (a d) -> p a d", a=TT)[:, :, None, :].broadcast_to([P, TT, heads, 16])
                s = const[:, C_SIN:C_SIN + TT * 16].rearrange("p (a d) -> p a d", a=TT)[:, :, None, :].broadcast_to([P, TT, heads, 16])
                n = TT * heads * 16
                t = [scratch_xs[:, i * n:(i + 1) * n].rearrange("p (a g d) -> p a g d", a=TT, d=16) for i in range(4)]
                v.tensor_tensor(t[0], x1, c, ALU.mult)
                v.tensor_tensor(t[1], x2, s, ALU.mult)
                v.tensor_tensor(t[2], x1, s, ALU.mult)
                link(v.tensor_tensor(t[3], x2, c, ALU.mult))
                v.tensor_tensor(x1, t[0], t[1], ALU.subtract)
                return v.tensor_tensor(x2, t[2], t[3], ALU.add)

            scratch_xs = xs[:].rearrange("p a b -> p (a b)")
            factors, pending = [], []

            def level_decay(l, i, hp):
                idx, half = (l * len(LEVELS) + i) * 2 + hp, LEVELS[i]
                nb = S // (2 * half)
                E, F = at(A_E, 4, S + 1), at(A_F, 4, S)
                if idx >= 2:
                    dve.wait_ge(s_Kl, idx - 1)
                    dve.wait_ge(s_Ql, idx - 1)
                x = at(A_X + 512 * (idx % 2), 2 * S).rearrange("p (g b w c) -> p g b w c", g=2, w=2, c=half)
                f5 = F[:, 2 * hp:2 * hp + 2, :].rearrange("p g (b w c) -> p g b w c", w=2, c=half)
                mid = E[:, 2 * hp:2 * hp + 2, half:S:2 * half][:, :, :, None].broadcast_to([P, 2, nb, half])
                v.tensor_tensor(x[:, :, :, 0, :], mid, f5[:, :, :, 0, :], ALU.subtract)
                v.tensor_tensor(x[:, :, :, 1, :], f5[:, :, :, 1, :], mid, ALU.subtract).then_inc(s_Dl, 1)

            def level_query(l, i, hp):
                idx, half = (l * len(LEVELS) + i) * 2 + hp, LEVELS[i]
                dve.wait_ge(s_zero, idx + 1)
                dve.wait_ge(s_Xl, idx + 1)
                q = at(A_HQ, 4 * S)[:, hp * 512:(hp + 1) * 512].rearrange("p (b w c) -> p b w c", w=2, c=half)
                ql = at(A_QL + 512 * (idx % 2), 2 * S).rearrange("p (b w c) -> p b w c", w=2, c=half)
                xx = at(A_X + 512 * (idx % 2), 2 * S).rearrange("p (b w c) -> p b w c", w=2, c=half)
                v.tensor_tensor(ql[0:64, :, 1, :], q[0:64, :, 1, :], xx[0:64, :, 1, :], ALU.mult)
                v.tensor_tensor(ql[64:128, :, 0, :], q[64:128, :, 0, :], xx[64:128, :, 0, :], ALU.mult).then_inc(s_Ql, 1)

            def level_place(l, i, hp):
                job = f"level{l}.{i}{hp}"
                bank = wait_filled(dve, job)[:].rearrange("p (g s c) -> p g s c", g=2, s=2)
                sT = at(A_ST + 1024 * hp, 2, 4, P)
                if i == 0:
                    drains(v.tensor_copy(sT[:, :, 1:3, :], bank), job)
                elif i == 1:
                    drains(v.tensor_copy(sT[:, :, 0:4:3, :], bank), job)
                else:
                    if i == 2:
                        wait_drained(dve, f"level{l}.1{hp}")
                    else:
                        wait_drained(dve, f"level{l}.{i - 1}{hp}")
                    m0 = C_MASK + (i - 2) * P
                    mask = const[:, m0:m0 + P].bitcast(I32)[:, None, None, :].broadcast_to([P, 2, 2, P])
                    drains(v.copy_predicated(sT[:, :, 0:4:3, :], mask, bank), job)
            for step in steps:
                kind = step[0]
                if kind == "setup":
                    pass
                elif kind in ("norm", "finalnorm"):
                    name = step[1] if kind == "norm" else "final"
                    dve.wait_ge(s_sumsq, stats.index(name) + 1)
                    ss, rs, t = col("ss." + name, TT), col("rs." + name, TT), col("nt", TT)
                    link(v.tensor_scalar(ss, ss, 1.0 / D, EPS, ALU.mult, ALU.add))
                    rsqrt(ss, rs, t, TT)
                    if kind == "finalnorm":
                        dve.wait_ge(s_row, 16)
                        for tt in range(TT):
                            ins = v.scalar_tensor_tensor(h[:, tt, :], h[:, tt, :], rs[:, tt:tt + 1], row[:, R_FINAL:R_FINAL + D], ALU.mult, ALU.mult)
                            ins.then_inc(s_hn, 1)
                        continue
                    src = at(A_MEM, TT, D) if name == "norm_mem_g" else h
                    dst = src if name == "norm_mem_g" else xs
                    v.tensor_scalar(dst[:, 0, :], src[:, 0, :], rs[:, 0:1], None, ALU.mult)
                    v.tensor_scalar(dst[:, 1, :], src[:, 1, :], rs[:, 1:2], None, ALU.mult).then_inc(s_scaled, 1)
                    if name == "norm_mix_g":
                        dve.wait_ge(s_vec, 16)
                    dst = memT if name == "norm_mem_g" else xT
                    gi = V_GAIN + GAINS.index(name) * KT
                    for j in (0, 2):
                        bank = bank2(wait_filled(dve, f"{name}.{j}"))
                        v.tensor_scalar(dst[:, 2 * j, :], bank[:, 0, :], vec[:, gi + 2 * j:gi + 2 * j + 1], None, ALU.mult)
                        drains(v.tensor_scalar(dst[:, 2 * j + 1, :], bank[:, 1, :], vec[:, gi + 2 * j + 1:gi + 2 * j + 2], None, ALU.mult), f"{name}.{j}")
                    if name == "norm_mix_g":
                        dve.wait_ge(s_pos, 16)
                        dve.wait_ge(s_const, 16)
                        r4 = at(A_ROPE, 4, S)
                        ang, n = r4[:, 2, :], r4[:, 3, :]
                        link(v.tensor_copy(n, r4[:, 0, :].bitcast(I32)))
                        link(v.tensor_scalar(ang, n, const[:, C_FREQ:C_FREQ + 1], None, ALU.mult))
                        for f, (quarter, shift) in enumerate(((0.25, 0.5 * np.pi), (0.0, 0.0))):
                            out = r4[:, f, :]
                            link(v.tensor_scalar(n, ang, float(1.0 / (2.0 * np.pi)), quarter, ALU.mult, ALU.add))
                            link(v.tensor_scalar(n, n, ROUND, None, ALU.add))
                            link(v.tensor_scalar(n, n, ROUND, None, ALU.subtract))
                            link(v.scalar_tensor_tensor(out, n, -TWO_PI_HI, ang, ALU.mult, ALU.add))
                            link(v.scalar_tensor_tensor(out, n, -TWO_PI_MID, out, ALU.mult, ALU.add))
                            link(v.scalar_tensor_tensor(out, n, -TWO_PI_LO, out, ALU.mult, ALU.add))
                            link(v.tensor_scalar(out, out, shift, 3.1415925, ALU.add, ALU.min))
                            ins = v.tensor_scalar(out, out, -3.1415925, None, ALU.max)
                            if f == 0:
                                link(ins)
                            else:
                                ins.then_inc(s_ang, 1)
                        l0, l1 = vec_lb[:, 0, :], vec_lb[:, 1, :]
                        m, e = col("lb.m", 4), col("lb.e", 8)
                        link(v.tensor_tensor(m, l0, l1, ALU.max))
                        v.tensor_tensor(e[:, 0:4], l0, m, ALU.subtract)
                        v.tensor_tensor(e[:, 4:8], l1, m, ALU.subtract).then_inc(s_lb, 1)
                        lam = vec[:, V_LAM:V_LAM + 8]
                        na = col("sp.na", 8)
                        link(v.tensor_scalar(na, lam, -1.0, None, ALU.mult))
                        v.tensor_tensor(na, na, lam, ALU.min).then_inc(s_sp, 1)
                elif kind == "proj":
                    name = step[1]
                    if name in ("q", "k"):
                        if name == "q":
                            dve.wait_ge(s_trig, 1)
                        cs = at(A_ROPE, 2, S)
                        C = cs[:, None, 0, :].broadcast_to([P, 2, S])
                        Sn = cs[:, None, 1, :].broadcast_to([P, 2, S])
                        tmp = at(A_SC1, 4, S)
                        dst = at(A_Q1 if name == "q" else A_K1, 2, 2, S)
                        for j in range(2):
                            bank = bank2(wait_filled(dve, f"{name}.{j}"))
                            v.tensor_tensor(tmp[:, 0:2, :], bank, C, ALU.mult)
                            drains(v.tensor_tensor(tmp[:, 2:4, :], bank, Sn, ALU.mult), f"{name}.{j}")
                            wait_drained(dve, f"{name}.{j}")
                            v.tensor_tensor(dst[:, j, 0, :], tmp[:, 0, :], tmp[:, 3, :], ALU.subtract)
                            ins = v.tensor_tensor(dst[:, j, 1, :], tmp[:, 2, :], tmp[:, 1, :], ALU.add)
                            if j == 1 and name == "k":
                                ins.then_inc(s_rope, 1)
                            else:
                                link(ins)
                    elif name[:4] == "wout" or name == "co":
                        gain = 1.0 if name in ("wout", "co") else 0.5
                        for j in range(2):
                            for tt in range(TT):
                                job = f"{name}.{j}.{tt}"
                                bank = wait_filled(dve, job)
                                hh = h[:, tt, 512 * j:512 * j + 512]
                                drains(v.scalar_tensor_tensor(hh, bank[:], gain, hh, ALU.mult, ALU.add), job)
                    elif name in ("down7", "wd0.5", "wd1.5"):
                        tag = "down" if name == "down7" else name[:3]
                        for tt in range(TT):
                            for j in range(2):
                                job = f"{tag}.{tt}{j}"
                                bank = wait_filled(dve, job)
                                hh = h[:, tt, 512 * j:512 * j + 512]
                                drains(v.tensor_tensor(hh, bank[:], hh, ALU.add), job)
                    elif name[:2] == "gu":
                        l, i = int(name[2]), int(name[4:])
                        a = at(A_ACT, 22, S)
                        wait_drained(dve, f"{name}.0")
                        bank = bank2(wait_filled(dve, f"{name}.1"))
                        drains(v.tensor_tensor(a[:, 2 * i:2 * i + 2, :], bank, a[:, 2 * i:2 * i + 2, :], ALU.mult), f"{name}.1")
                    elif layer_of(name) is not None and name[0] == "a":
                        l = layer_of(name)
                        za = at(A_ZA, TT, 512)
                        ss, rs, t = col(f"ss.a{l}", 2 * TT), col(f"rs.a{l}", 2 * TT), col("hn.t", 32)[:, 0:2 * TT]
                        for tt in range(TT):
                            wait_drained(dve, f"a{l}.{tt}")
                        link(v.tensor_scalar(ss, ss, EPS, None, ALU.add))
                        rsqrt(ss, rs, t, 2 * TT)
                        for tt in range(TT):
                            v.tensor_scalar(za[:, tt, 0:384], za[:, tt, 0:384], rs[:, 2 * tt:2 * tt + 1], None, ALU.mult)
                            ins = v.tensor_scalar(za[:, tt, 384:512], za[:, tt, 384:512], rs[:, 2 * tt + 1:2 * tt + 2], None, ALU.mult)
                        ins.then_inc(s_tok, 1)
                        if l == 0:
                            dve.wait_ge(s_lbe, 1)
                            e, sm, p = col("lb.x", 8), col("lb.s", 4), col("lb.p", 8)
                            link(v.tensor_tensor(sm, e[:, 0:4], e[:, 4:8], ALU.add))
                            link(v.reciprocal(sm, sm))
                            v.tensor_tensor(p[:, 0:4], e[:, 0:4], sm, ALU.mult)
                            link(v.tensor_tensor(p[:, 4:8], e[:, 4:8], sm, ALU.mult))
                            lb, om = col("lb.lb", 8), col("lb.om", 8)
                            v.tensor_tensor(lb[:, 0:4], p[:, 0:4], p[:, 0:4], ALU.subtract)
                            link(v.tensor_tensor(sm, p[:, 0:4], p[:, 4:8], ALU.add))
                            link(v.tensor_tensor(lb[:, 4:8], sm, p[:, 0:4], ALU.subtract))
                            link(v.tensor_scalar(om, lb, -1.0, 1.0, ALU.mult, ALU.add))
                            dve.wait_ge(s_row, 16)
                            for ll in range(L2):
                                r0 = R_LAYER + ll * R_PER + R_LQ
                                lq = row[:, r0:r0 + 128].rearrange("p (a d) -> p a d", a=4)
                                prod = scratch_xs[:, 0:64].rearrange("p (a d) -> p a d", a=2)
                                link(v.tensor_tensor(prod, lq[:, 0:2, :], lq[:, 2:4, :], ALU.mult))
                                ins = v.tensor_reduce(col(f"lam.d{ll}", 2), prod, AX_X, ALU.add)
                                ins.then_inc(s_lam, 1)
                                dve.wait_ge(s_lam, ll + 1)
                    elif layer_of(name) is not None and name[0] == "b":
                        l = layer_of(name)
                        zb = at(A_ZB, TT, 16, 32)
                        for tt in range(TT):
                            wait_drained(dve, f"b{l}.{tt}")
                        rs = heads_norm(zb, 32, 32, scratch_xs)
                        link(v.tensor_tensor(zb, zb, rs.rearrange("p (a g) -> p a g", a=TT)[:, :, :, None].broadcast_to([P, TT, 16, 32]), ALU.mult))
                        r0 = R_LAYER + l * R_PER + R_DQN
                        g = row[:, r0:r0 + 64].rearrange("p (a d) -> p a d", a=2)[:, :, None, :].broadcast_to([P, 2, 8, 32])
                        for tt in range(TT):
                            z4 = zb[:, tt, :, :].rearrange("p (a g) d -> p a g d", a=2)
                            ins = v.tensor_tensor(z4, z4, g, ALU.mult)
                        link(ins)
                        rope32(zb[:, :, :, 0:16], zb[:, :, :, 16:32], 16).then_inc(s_tok, 1)
                    elif layer_of(name) is not None and name[0] == "d":
                        l = layer_of(name)
                        z = at(A_Z, TT, 8, 96)
                        for tt in range(TT):
                            for n in ("d", "uq", "ukv"):
                                wait_drained(dve, f"{n}{l}.{tt}")
                        dve.wait_ge(s_tok, side_order.index((l, "b")) + 1)
                        rs = heads_norm(z, 16, 96, scratch_xs)
                        link(v.tensor_tensor(z, z, rs.rearrange("p (a g) -> p a g", a=TT)[:, :, :, None].broadcast_to([P, TT, 8, 96]), ALU.mult))
                        r0 = R_LAYER + l * R_PER + R_QN
                        g = row[:, r0:r0 + 192].rearrange("p (a d) -> p a d", a=2)[:, :, None, :].broadcast_to([P, 2, 4, 96])
                        for tt in range(TT):
                            z4 = z[:, tt, :, :].rearrange("p (a g) d -> p a g d", a=2)
                            ins = v.tensor_tensor(z4, z4, g, ALU.mult)
                        link(ins)
                        rope32(z[:, :, :, 64:80], z[:, :, :, 80:96], 8).then_inc(s_tok, 1)
                    elif layer_of(name) is not None and name[0] == "f":
                        l = layer_of(name)
                        kk, F = at(A_KK, 4, S), at(A_F, 4, S)
                        E = at(A_E, 4, S + 1)
                        lb, om = col("lb.lb", 8), col("lb.om", 8)
                        for j in range(2):
                            wait_drained(dve, f"f{l}.{j}")
                        for hd in range(4):
                            c = 4 * l + hd
                            ins = v.tensor_scalar(kk[:, hd, :], kk[:, hd, :], om[:, c:c + 1], lb[:, c:c + 1], ALU.mult, ALU.add)
                        link(ins)
                        v.tensor_scalar(F, kk, 2.0 ** -63, None, ALU.max).then_inc(s_f, 1)
                        v.tensor_scalar(kk, kk, -1.0, 1.0, ALU.mult, ALU.add).then_inc(s_hkk, 1)
                        v.memset(E[:, :, 0:1], 0.0)
                        ones = scratch_xs[:, 0:S]
                        dve.wait_ge(s_tok, side_order.index((l, "z")) + 1)
                        link(v.memset(ones, 1.0))
                        dve.wait_ge(s_lf, l + 1)
                        for hd in range(4):
                            ins = v.tensor_tensor_scan(E[:, hd, 1:S + 1], ones, F[:, hd, :], 0.0, ALU.mult, ALU.add)
                        link(ins)
                        v.tensor_copy(F[0:64, :, :], E[0:64, :, 1:S + 1])
                        link(v.tensor_copy(F[64:128, :, :], E[64:128, :, 0:S]))
                elif kind == "conv":
                    for j in range(2):
                        wait_drained(dve, f"u.{j}")
                    dve.wait_ge(s_zero1, 1)
                    up, uc = at(A_U, 4, UPAD), at(A_UC, 4, S)
                    cw = vec[:, V_CONVW:V_CONVW + 16]
                    for tap in range(4):
                        for ct in range(4):
                            w = cw[:, 4 * ct + tap:4 * ct + tap + 1]
                            src = up[:, ct, tap:tap + S]
                            if tap == 0:
                                ins = v.tensor_scalar(uc[:, ct, :], src, w, vec[:, V_CONVB + ct:V_CONVB + ct + 1], ALU.mult, ALU.add)
                            else:
                                ins = v.scalar_tensor_tensor(uc[:, ct, :], src, w, uc[:, ct, :], ALU.mult, ALU.add)
                        if tap < 3:
                            link(ins)
                        else:
                            ins.then_inc(s_conv, 1)
                elif kind == "rg1":
                    dve.wait_ge(s_spe, 1)
                    x, s1, s2, acc = col("sp.x", 8), col("sp.s", 8), col("sp.s2", 8), col("sp.acc", 8)
                    link(v.tensor_scalar(s1, x, 2.0, None, ALU.add))
                    link(v.reciprocal(s1, s1))
                    link(v.tensor_tensor(s1, s1, x, ALU.mult))
                    link(v.tensor_tensor(s2, s1, s1, ALU.mult))
                    link(v.memset(acc, 1.0 / 19.0))
                    for n in range(17, 0, -2):
                        link(v.tensor_tensor(acc, acc, s2, ALU.mult))
                        link(v.tensor_scalar(acc, acc, 1.0 / n, None, ALU.add))
                    link(v.tensor_tensor(acc, acc, s1, ALU.mult))
                    link(v.tensor_scalar(s2, vec[:, V_LAM:V_LAM + 8], -1.0, 0.0, ALU.mult, ALU.max))
                    link(v.tensor_scalar(s2, s2, RG_C, None, ALU.mult))
                    link(v.scalar_tensor_tensor(acc, acc, 2.0 * RG_C, s2, ALU.mult, ALU.add))
                    r = at(A_RG_R, 8, S)
                    wait_drained(dve, "rg.13")
                    v.tensor_tensor(r, r, acc[:, :, None].broadcast_to([P, 8, S]), ALU.mult).then_inc(s_rgy, 1)
                    ii = at(A_RG_I, 2, 4, S)
                    uc = at(A_UC, 4, S)
                    for z in range(2):
                        link(v.tensor_tensor(ii[:, z], ii[:, z], uc, ALU.mult))
                    dve.wait_ge(s_rgta, 1)
                    r, t, a = at(A_RG_R, 2048), at(A_RG_T, 2048), at(A_RG_A, 2048)
                    link(v.tensor_tensor(r, a, a, ALU.mult))
                    v.scalar_tensor_tensor(t, r, 1.0, t, ALU.add, ALU.mult).then_inc(s_rgw2, 1)
                elif kind == "rg2":
                    t, ii = at(A_RG_T, 2048), at(A_RG_I, 2048)
                    dve.wait_ge(s_rgs, 1)
                    link(v.tensor_tensor(ii, ii, t, ALU.mult))
                    a4, b4, h4 = at(A_RG_A, 2, 4, S), at(A_RG_I, 2, 4, S), at(A_RG_R, 2, 4, S)
                    for ct in range(4):
                        v.tensor_tensor_scan(h4[:, 0, ct, :], a4[:, 0, ct, :], b4[:, 0, ct, :], 0.0, ALU.mult, ALU.add)
                        ins = v.tensor_tensor_scan(h4[:, 1, ct, ::-1], a4[:, 1, ct, ::-1], b4[:, 1, ct, ::-1], 0.0, ALU.mult, ALU.add)
                    link(ins)
                    link(v.tensor_tensor(h4[:, 0], h4[:, 0], h4[:, 1], ALU.add))
                    v.tensor_tensor(mixT[:, 4:8, :], h4[:, 0], at(A_YG, 4, S), ALU.mult).then_inc(s_rec, 1)
                elif kind == "score":
                    phase, hd = step[1:]
                    n, a0, count = ATT[phase, hd]
                    scale = {"dil": 64.0 ** -0.5, "cro": 128.0 ** -0.5, "mla": 96.0 ** -0.5, "dif": 32.0 ** -0.5}[phase[:3]]
                    if phase[:4] == "diff" and hd == 0:
                        l = int(phase[4])
                        dve.wait_ge(s_lame, l + 1)
                        e, nl = col(f"lam.e{l}", 2), col(f"lam.n{l}", 1)
                        link(v.tensor_tensor(nl, e[:, 1:2], e[:, 0:1], ALU.subtract))
                        link(v.tensor_scalar(nl, nl, LAMBDA_INIT[l], None, ALU.subtract))
                    for j in range(count):
                        a = a0 + j
                        bank = bank2(wait_filled(dve, f"score{a}"))
                        nm = col(f"nmax{a % 16}", TT)
                        if phase == "dil":
                            if a >= 4:
                                wait_filled(dve, f"turn{ATT[HEAD_OF_UNIT[a - 4]][0]}")
                            sc = at(A_SC1 + 512 * (a % 4), TT, S)
                            drains(v.scalar_tensor_tensor(sc, bank, scale, logc, ALU.mult, ALU.add), f"score{a}")
                            wait_drained(dve, f"score{a}")
                            v.tensor_reduce(nm, sc, AX_X, ALU.max, negate=True).then_inc(s_max, 1)
                        else:
                            mx = col(f"max{a % 4}", TT)
                            link(v.tensor_reduce(mx, bank, AX_X, ALU.max, negate=True))
                            v.tensor_scalar(nm, mx, scale, None, ALU.mult).then_inc(s_max, 1)
                elif kind == "prob":
                    phase, hd = step[1:]
                    n, a0, count = ATT[phase, hd]
                    base = A_SC1 if phase in ("dil", "cross") else A_SC
                    for j in range(count):
                        a = a0 + j
                        if phase == "dil":
                            dve.wait_ge(s_exp, a + 1)
                        else:
                            wait_drained(dve, f"score{a}")
                        ins = v.reciprocal(col(f"rsum{a % 16}", TT), col(f"sum{a % 16}", TT))
                    link(ins)
                    p0 = at(base + 512 * (a0 % 4), TT, S)
                    rs = col(f"rsum{a0 % 16}", TT)
                    if count == 1:
                        v.tensor_scalar(p0[:, 0, :], p0[:, 0, :], rs[:, 0:1], None, ALU.mult)
                        v.tensor_scalar(p0[:, 1, :], p0[:, 1, :], rs[:, 1:2], None, ALU.mult).then_inc(s_prob, 1)
                    else:
                        p1 = at(base + 512 * ((a0 + 1) % 4), TT, S)
                        rs1 = col(f"rsum{(a0 + 1) % 16}", TT)
                        v.tensor_scalar(rs1, rs1, col(f"lam.n{phase[4]}", 1), None, ALU.mult)
                        v.tensor_scalar(p0[:, 0, :], p0[:, 0, :], rs[:, 0:1], None, ALU.mult)
                        link(v.tensor_scalar(p0[:, 1, :], p0[:, 1, :], rs[:, 1:2], None, ALU.mult))
                        v.scalar_tensor_tensor(p0[:, 0, :], p1[:, 0, :], rs1[:, 0:1], p0[:, 0, :], ALU.mult, ALU.add)
                        v.scalar_tensor_tensor(p0[:, 1, :], p1[:, 1, :], rs1[:, 1:2], p0[:, 1, :], ALU.mult, ALU.add).then_inc(s_prob, 1)
                elif kind in ("diffout", "hval"):
                    l = step[1]
                    if kind == "diffout":
                        o = at(A_DO, TT, 4, 64)
                        for hd in range(4):
                            wait_drained(dve, f"value.diff{l}{hd}")
                        factor, g0 = 1.0 - LAMBDA_INIT[l], R_SUB
                    else:
                        o = at(A_HO, TT, 4, 64)
                        for hp in range(2):
                            wait_drained(dve, f"hval{l}.{hp}")
                        factor, g0 = 0.5, R_ON
                    rs = heads_norm(o, 8, 64, at(A_DT, 512))
                    link(v.tensor_scalar(rs, rs, factor, None, ALU.mult))
                    link(v.tensor_tensor(o, o, rs.rearrange("p (a g) -> p a g", a=TT)[:, :, :, None].broadcast_to([P, TT, 4, 64]), ALU.mult))
                    r0 = R_LAYER + l * R_PER + g0
                    g = row[:, r0:r0 + 64][:, None, None, :].broadcast_to([P, TT, 4, 64])
                    ins = v.tensor_tensor(o, o, g, ALU.mult)
                    if kind == "hval":
                        link(ins)
                        ins = v.scalar_tensor_tensor(at(A_HO, 512), at(A_SG, 512), 1.0, at(A_HO, 512), ALU.add, ALU.mult)
                    ins.then_inc(s_tok, 1)
                elif kind == "level":
                    _, l, i, hp = step
                    if i == 0 and hp == 0:
                        wait_filled(dve, f"value.mla{l}1")
                        wait_drained(dve, f"e{l}.1")
                        dve.wait_ge(s_tok, side_order.index((l, "do")) + 1)
                    if i < len(LEVELS):
                        level_decay(l, i, hp)
                    if factors:
                        level_query(*factors.pop())
                    if i < len(LEVELS):
                        factors.append((l, i, hp))
                    pending.append((l, i, hp))
                    while len(pending) > 2:
                        level_place(*pending.pop(0))
                elif kind == "levelflush":
                    while factors:
                        level_query(*factors.pop())
                    while pending:
                        level_place(*pending.pop(0))
                elif kind == "merge":
                    _, l, br, n, part = step
                    gate = at(A_GATE, 16, S)
                    tmp = junk[:].bitcast(F32)[:, 0:512].rearrange("p (a t) -> p a t", a=2)
                    for j in range(4):
                        job = f"merge{l}.{br}{j}"
                        k = (8 * br + 2 * j) % 16
                        g = (8 * br + 2 * j) // 4
                        wait_drained(dve, f"gate{l}.{g}{(8 * br + 2 * j) // 2 % 2}")
                        bank = bank2(wait_filled(dve, job))
                        gk, mk = gate[:, k:k + 2, :], merged[:, 2 * j:2 * j + 2, :]
                        if br == 0:
                            drains(v.scalar_tensor_tensor(mk, gk, 1.0, bank, ALU.add, ALU.mult), job)
                        else:
                            drains(v.scalar_tensor_tensor(tmp, gk, 1.0, bank, ALU.add, ALU.mult), job)
                            wait_drained(dve, job)
                            ins = v.tensor_tensor(mk, mk, tmp, ALU.add)
                            if j == 3 and br % 2:
                                ins.then_inc(s_merged, 1)
                            else:
                                link(ins)




def constants():
    c = np.zeros((P, C_SIZE), np.float64)
    p = np.arange(P)
    c[:, C_IDENT:C_IDENT + P] = np.eye(P)
    i, j = np.arange(S)[:, None], np.arange(S)[None, :]
    count = np.zeros((S, S))
    for window, dil in ((128, 1), (512, 4), (2048, 16)):
        count += ((i - j) % dil == 0) & (np.abs(i - j) // dil <= window // (2 * dil))
    logc = np.where(count > 0, np.log(np.maximum(count, 1)), -1e30)
    c[:, C_LOGC:C_LOGC + TT * S] = logc.reshape(TT, P, S).transpose(1, 0, 2).reshape(P, -1)
    c[:, C_FREQ] = 10000.0 ** (-(p % 32) / 32.0)
    ang = np.arange(S)[:, None] / 10000.0 ** (np.arange(0, 32, 2) / 32.0)[None, :]
    for off, f in ((C_COS, np.cos), (C_SIN, np.sin)):
        c[:, off:off + TT * 16] = f(ang).reshape(TT, P, 16).transpose(1, 0, 2).reshape(P, -1)
    d = np.arange(64)
    ph = 2 * np.pi * d[:, None] * d[None, :] / 64
    for g in range(2):
        c[64 * g:64 * g + 64, C_DFTD + 64 * g:C_DFTD + 64 * g + 64] = np.cos(ph) / 8.0
        c[64 * g:64 * g + 64, C_DFTD + P + 64 * g:C_DFTD + P + 64 * g + 64] = np.sin(ph) / 8.0
    ph = 2 * np.pi * ((i * j) % S) / S
    c[:, C_DFTC:C_DFTC + TT * S] = (np.cos(ph) / 16.0).reshape(TT, P, S).transpose(1, 0, 2).reshape(P, -1)
    c[:, C_DFTS:C_DFTS + TT * S] = (-np.sin(ph) / 16.0).reshape(TT, P, S).transpose(1, 0, 2).reshape(P, -1)
    for n, half in enumerate(MASKED):
        same = p[:, None] // (2 * half) == p[None, :] // (2 * half) if half else np.eye(P, dtype=bool)
        c[:, C_MASK + n * P:C_MASK + (n + 1) * P] = same
    return c.astype(np.float32)




def fold(w):
    k = w.shape[0] // P
    return w.reshape(k, P, -1).transpose(1, 0, 2).reshape(P, -1)


def pack_units(a):
    units = []

    def put(*parts):
        parts = [fold(p) for p in parts]
        n = sum(p.shape[1] for p in parts)
        units.append(np.concatenate(parts + ([np.zeros((P, UNIT - n), np.float32)] if n < UNIT else []), axis=1))

    w = a["w_in"][0]
    halves = np.concatenate([np.concatenate([64 * hd + 32 * f + np.arange(32) for hd in range(4 * g, 4 * g + 4)]) for g in range(2) for f in range(2)])
    put(w[:, halves])
    put(w[:, 512 + halves])
    for n in range(2, 5):
        put(w[:, 512 * n:512 * n + 512])
    put(a["w_ck"][0])
    put(a["w_cv"][0])
    for n in range(2):
        put(a["w_out"][0][:, 512 * n:512 * n + 512])
    put(a["w_cq"][0])
    put(a["w_co"][0])
    for n in range(8):
        put(a["w_mlp_in"][0][:, 512 * n:512 * n + 512])
    for n in range(8):
        put(a["w_mlp_out"][0][512 * n:512 * n + 512])
    for l in range(L2):
        w = a["w_in_2"][l]
        o = np.cumsum([0, 384, 128, 32, 256, 256, 256, 256, 256, 256, 256, 256, 256, 4096])
        c_q, c_kv, k_rope, fnet, dq, dk, dv, hq, hi, hff, hfb, hg, gate = (w[:, o[i]:o[i + 1]] for i in range(13))
        put(np.concatenate([c_q, c_kv], 1))
        put(np.concatenate([dq, dk], 1))
        ukv = a["mla_w_ukv_2"][l].reshape(P, 4, 2, 64).transpose(0, 2, 1, 3).reshape(P, 512)
        put(np.concatenate([k_rope, hg], 1), a["mla_w_uq_2"][l], ukv)
        put(np.concatenate([dv, hi], 1))
        put(np.stack([hff.reshape(D, 4, 64), hfb.reshape(D, 4, 64)], 2).reshape(D, 512))
        put(np.concatenate([fnet, hq], 1))
        br = a["w_branch_2"][l]
        for n in range(4):
            put(gate[:, 512 * n:512 * n + 512])
        put(br[0], br[1])
        for n in range(4, 8):
            put(gate[:, 512 * n:512 * n + 512])
        put(br[2], br[3])
        for n in range(2):
            put(a["w_out_2"][l][:, 512 * n:512 * n + 512])
        gu = a["w_gate_up_2"][l]
        for n in range(11):
            put(np.concatenate([gu[:, 256 * n:256 * n + 256], gu[:, 2816 + 256 * n:2816 + 256 * n + 256]], 1))
        wd = a["w_down_2"][l]
        for n in range(6):
            put(wd[512 * n:512 * n + 512])
    return np.ascontiguousarray(np.stack(units))


def pack_vectors(a):
    gains = [a[n][0] for n in GAINS[:4]] + [a["ln_mix_2"][l] for l in range(L2)] + [a["ln_ffn_2"][l] for l in range(L2)]
    parts = [g.reshape(KT, P).T for g in gains]
    parts.append(a["conv_w"][0].reshape(4, 4, P).transpose(2, 1, 0).reshape(P, 16))
    parts.append(a["conv_b"][0].reshape(4, P).T)
    ab, xb = (a[n][0].reshape(2, 4, P).transpose(2, 0, 1) for n in ("rg_a_b", "rg_x_b"))
    parts.append(np.stack([ab, xb], 3).reshape(P, 16))
    parts.append(a["rg_lambda"][0].reshape(2, 4, P).transpose(2, 0, 1).reshape(P, 8))
    for l in range(L2):
        parts.append(a["mla_g_qa_2"][l].reshape(3, P).T)
        parts.append(a["mla_g_kva_2"][l].reshape(P, 1))
    lb = a["hgrn_lb_logits_2"].reshape(2, L2, 4, 64).transpose(0, 3, 1, 2).reshape(P, L2 * 4)
    parts.append(lb)
    out = np.ascontiguousarray(np.concatenate(parts, 1))
    assert out.shape == (P, V_SIZE), out.shape
    return out


def pack_rows(a):
    r = [a["norm_final_g"]]
    for l in range(L2):
        r += [a[n + "_2"][l] for n in ("mla_g_qn", "mla_g_kn", "diff_g_qn", "diff_g_kn", "diff_g_sub", "hgrn_g_on",
                                       "diff_lq1", "diff_lq2", "diff_lk1", "diff_lk2")]
    r = np.concatenate(r)
    assert r.shape == (R_SIZE,)
    return np.ascontiguousarray(np.broadcast_to(r, (P, R_SIZE)))


def pack_rg(a):
    out = np.zeros((P, 2, 4, 2, P), np.float32)
    for ax, n in enumerate(("rg_a_w", "rg_x_w")):
        w = a[n][0]
        for z in range(2):
            for g in range(8):
                p0 = 64 * (g % 2)
                out[p0:p0 + 64, z, g // 2, ax, p0:p0 + 64] = w[z, g]
    return out.reshape(P, 16 * P)


def kernel(**inputs):
    import concourse.bacc as bacc
    from concourse.bass_utils import run_bass_kernel_spmd

    a = {n: np.asarray(x) for n, x in inputs.items()}
    arrays = {
        "x": np.ascontiguousarray(a["x"][0]),
        "mem": np.ascontiguousarray(a["mem"][0]),
        "positions": np.ascontiguousarray(np.broadcast_to(a["positions"][0], (P, S))),
        "constants": constants(),
        "vectors": pack_vectors(a),
        "rows": pack_rows(a),
        "rg_weights": pack_rg(a),
        "weight_units": pack_units(a),
    }
    nc = bacc.Bacc("TRN2", target_bir_lowering=False, num_devices=1)
    args = [nc.dram_tensor(n, v.shape, mybir.dt.from_np(v.dtype), kind="ExternalInput").ap() for n, v in arrays.items()]
    args.append(nc.dram_tensor("out", (S, D), F32, kind="ExternalOutput").ap())
    build(nc, *args)
    r = run_bass_kernel_spmd(nc, [arrays], core_ids=[0])
    return r.results[0]["out"].reshape(1, S, D)
```

```python
from contextlib import ExitStack

import numpy as np
import concourse.bass as bass
from concourse import mybir

ALU = mybir.AluOpType
ACT = mybir.ActivationFunctionType
F32 = mybir.dt.float32
F32R = mybir.dt.float32r
BF16 = mybir.dt.bfloat16
I32 = mybir.dt.int32
AX_X = mybir.AxisListType.X

P = 128
D = 1024
S = 256
TT = S // P
KT = D // P
L2 = 2
EPS = 1e-6
PIECE = 2048
RING = 3
SPLITS = 2
RG_C = 8.0
LEVELS = (128, 64, 32, 16, 8, 4, 2, 1)
MASKED = (32, 16, 8, 4, 2, 1, 0)
N_PIECES_1 = 54
N_PIECES_2 = 69
NP = N_PIECES_1 + L2 * N_PIECES_2
LAMBDA_INIT = [0.8 - 0.6 * float(np.exp(-0.3 * l)) for l in range(L2)]
RSQRT_MAGIC = 0x5F3759DF
TWO_PI_HI = 6.28125
TWO_PI_MID = 0.0019350051879882812
TWO_PI_LO = 2.0 * np.pi - TWO_PI_HI - TWO_PI_MID
ROUND = 1.5 * 2.0 ** 23

C_IDENT = 0
C_LOGC = C_IDENT + P
C_FREQ = C_LOGC + TT * S
C_COS = C_FREQ + 1
C_SIN = C_COS + TT * 16
C_DFTD = C_SIN + TT * 16 + 1
C_DFTC = C_DFTD + 2 * P
C_DFTS = C_DFTC + TT * S
C_MASK = C_DFTS + TT * S
C_SIZE = C_MASK + len(MASKED) * P

GAINS = ("norm_mix_g", "norm_cross_g", "norm_mem_g", "norm_mlp_g", "ln_mix_0", "ln_mix_1", "ln_ffn_0", "ln_ffn_1")
V_GAIN = 0
V_CONVW = V_GAIN + len(GAINS) * KT
V_CONVB = V_CONVW + 16
V_RGB = V_CONVB + 4
V_LAM = V_RGB + 16
V_QA = V_LAM + 8
V_LB = V_QA + 4 * L2
V_SIZE = V_LB + 4 * L2

R_FINAL = 0
R_LAYER = D
R_QN, R_DQN, R_SUB, R_ON, R_LQ = 0, 192, 256, 320, 384
R_PER = 512
R_SIZE = R_LAYER + L2 * R_PER

A_HID_HI, A_HID_LO = 0, 8192
A_PROD = 16384
A_RG_R, A_RG_I, A_RG_T, A_RG_A = 0, 2048, 4096, 6144
A_MEM = 0
A_Q1 = 8192
A_K1 = A_Q1 + 1024
A_V1 = A_K1 + 1024
A_CQ = A_K1
A_CO = A_Q1
A_U = A_V1 + 1024
UPAD = S + 3
A_UC = A_U + 4 * UPAD
A_YG = A_UC + 1024
A_RGW = A_YG + 1024
A_ROPE = A_RGW + 16 * P
A_CK = A_ROPE
A_CV = A_ROPE + 1024
A_SC1 = A_ROPE + 2048
A_GATE = 0
A_FT, A_AB = 0, 512
A_VC = 4096
A_SG = A_VC + 1024
A_HO = A_SG + 512
A_DO = A_HO + 512
A_HQ = A_DO + 512
A_KK = A_HQ + 1024
A_E = A_KK + 1024
A_F = A_E + 4 * (S + 1)
A_ZB = A_F + 1024
A_DT = A_ZB + 1024
A_SC = A_DT + 1024
A_VM = A_SC + 6 * 512
A_ZA = A_VM + 512
A_CT = A_ZA + 1024
A_Z = A_CT + 1024
A_QKT = A_Z + 1536
A_ST = A_ZA
A_X = A_ST + 2048
A_KL = A_ZB
A_QL = A_SC
A_SCR = A_SC + 2048
A_KR = 0
ARENA = A_QKT + 2048
assert A_X + 2048 <= ARENA and A_SC1 + 6 * 512 <= ARENA



def attention_plan():
    heads = [("dil", h, 1) for h in range(8)] + [("cross", h, 1) for h in range(4)]
    for l in range(L2):
        heads += [(f"mla{l}", h, 1) for h in range(4)]
        heads += [(f"diff{l}", h, 2) for h in range(4)]
    plan, unit = {}, 0
    for n, (phase, h, k) in enumerate(heads):
        plan[phase, h] = (n, unit, k)
        unit += k
    return heads, plan, unit


HEADS, ATT, N_SCORES = attention_plan()
EVEN = {n: sum(1 for m in HEADS[:n + 1] if m[0][:3] in ("dil", "mla") and m[1] % 2 == 0) for n in range(len(HEADS))}
HEAD_OF_UNIT = [(phase, h) for phase, h, k in HEADS for _ in range(k)]


def build(nc, x_d, mem_d, pos_d, const_d, vec_d, row_d, rgw_d, pieces_d, out_d):
    with ExitStack() as ctx:
        def sb(name, shape, dt=F32):
            return ctx.enter_context(nc.sbuf_tensor(name, shape, dt))

        def sem(name):
            return ctx.enter_context(nc.semaphore(name))

        ring = sb("ring", [P, RING, PIECE])
        w_hi = sb("w_hi", [P, SPLITS, PIECE], F32R)
        w_lo = sb("w_lo", [P, SPLITS, PIECE], F32R)
        const = sb("const", [P, C_SIZE])
        vec = sb("vec", [P, V_SIZE])
        row = sb("row", [P, R_SIZE])
        h = sb("h", [P, TT, D])
        xs = sb("xs", [P, TT, D])
        x_hi = sb("x_hi", [P, KT, S], F32R)
        x_lo = sb("x_lo", [P, KT, S], F32R)
        oT = sb("oT", [P, KT, S])
        W = sb("W", [P, ARENA])
        arena0 = nc.sbuf_base - 4 * ARENA
        hid_hi = nc.alloc_sbuf_tensor_at("hid_hi", [P, 32, S], F32R, offset=arena0 + 4 * A_HID_HI)
        hid_lo = nc.alloc_sbuf_tensor_at("hid_lo", [P, 32, S], F32R, offset=arena0 + 4 * A_HID_LO)
        junk = sb("junk", [P, D], BF16)
        stat = sb("stat", [P, 448])
        psum = [ctx.enter_context(nc.psum_tensor(f"bank{b}", [P, 512], F32)) for b in range(8)]

        def at(off, *dims):
            n = int(np.prod(dims))
            v = W[:, off:off + n]
            if len(dims) == 1:
                return v
            names = "abcd"[:len(dims)]
            return v.rearrange(f"p ({' '.join(names)}) -> p {' '.join(names)}", **dict(zip(names[1:], dims[1:])))

        merged = xs[:].rearrange("p a b -> p (a b)").rearrange("p (k t) -> p k t", k=KT)
        product = at(A_PROD, 2, 512)
        ident = const[:, C_IDENT:C_IDENT + P]
        logc = const[:, C_LOGC:C_LOGC + TT * S].rearrange("p (a k) -> p a k", a=TT)
        vec_lb = vec[:, V_LB:V_LB + 4 * L2].rearrange("p (l h) -> p l h", l=L2)

        cols = {}

        def col(name, n):
            if name not in cols:
                at0 = sum(k for _, k in cols.values())
                assert at0 + n <= 448, at0
                cols[name] = (at0, n)
            at0, n = cols[name]
            return stat[:, at0:at0 + n]

        s_x, s_mem, s_pos, s_const, s_vec, s_row, s_rgw = (sem(n) for n in (
            "x_loaded", "mem_loaded", "positions_loaded", "const_loaded", "vec_loaded", "row_loaded", "rgw_loaded"))
        piece_loaded = [sem(f"piece_loaded{i}") for i in range(RING)]
        s_whi, s_wlo, s_wlo_pool = sem("weights_high"), sem("weights_low"), sem("weights_low_pool")
        s_nhi = sem("norm_high")
        s_relu, s_phi, s_plo = sem("relu"), sem("product_high"), sem("product_low")
        s_xhi, s_xlo = sem("mix_high"), sem("mix_low")
        s_msum, s_mhi, s_mlo = sem("merged_sum"), sem("merged_high"), sem("merged_low")
        filled = [sem(f"filled{b}") for b in range(8)]
        drained = [sem(f"drained{b}") for b in range(8)]
        jobs = {}
        uses = [0] * 8
        last_job = [None] * NP
        dve_link, act_link, pool_link = sem("dve_link"), sem("act_link"), sem("pool_link")
        s_sumsq, s_scaled = sem("sumsq_ready"), sem("scaled_ready")
        s_max, s_exp, s_prob = sem("max_ready"), sem("exp_ready"), sem("prob_ready")
        s_conv, s_rec = sem("conv_ready"), sem("rec_ready")
        s_rgy, s_rgta, s_rgw2, s_rgs = sem("rg_y"), sem("rg_tanh_exp"), sem("rg_w"), sem("rg_sqrt")
        s_sp = sem("softplus_in")
        s_spe = sem("softplus_exp")
        s_ang, s_trig, s_rope = sem("angles_ready"), sem("cos_sin_ready"), sem("rope_done")
        s_even, s_read = sem("even_value_done"), sem("piece_read")
        s_tok = sem("token_side_ready")
        s_lb, s_lbe, s_f, s_lf, s_hkk = (sem(n) for n in ("lb_in", "lb_exp", "f_ready", "log_f_ready", "hgrn_k_ready"))
        s_E, s_F = sem("E_ready"), sem("F_ready")
        s_Dl, s_Xl, s_Ql, s_Kl, s_zero = (sem(n) for n in ("decay_log", "decay", "q_level", "k_level", "levels_zeroed"))
        s_lam, s_lame = sem("lambda_in"), sem("lambda_exp")
        s_merged = sem("merged_ready")
        s_zero1 = sem("pads_zeroed")
        s_hn, s_out = sem("h_normed"), sem("out_stored")

        def wait_filled(eng, name):
            b, use = jobs[name]
            eng.wait_ge(filled[b], use + 1)
            return psum[b]

        def wait_drained(eng, name):
            b, use = jobs[name]
            eng.wait_ge(drained[b], use + 1)

        def drains(ins, name):
            ins.then_inc(drained[jobs[name][0]], 1)

        def raw(p):
            return ring[:, p % RING, :]

        def wait_read(eng, p):
            if isinstance(last_job[p], int):
                eng.wait_ge(s_read, last_job[p])
            else:
                wait_filled(eng, last_job[p])

        steps = []
        split = []
        split_of = {}
        low = []
        s_low = {"dve": s_wlo, "pool": s_wlo_pool}

        def piece(n=PIECE, by="dve"):
            nonlocal pieces
            if n:
                split_of[pieces] = len(split)
                split.append((pieces, n))
                low.append((by, 1 + sum(b == by for b, _ in low)))
            pieces += 1
            return pieces - 1

        pieces = 0

        def proj(name, l=None, js=range(2), n=PIECE):
            by = "pool" if name in ("v", "u", "y", "ck", "cv", "b", "hg", "kr", "c", "e", "f") else "dve"
            return [("proj", name, l, j, piece(n, by)) for j in js]

        def wait_low(eng, q):
            by, n = low[q]
            eng.wait_ge(s_low[by], n)

        def attend(phase, count, filler=()):
            filler = list(filler)
            for i in range(count + 3):
                if i < count:
                    steps.append(("score", phase, i))
                if 1 <= i <= count:
                    steps.append(("prob", phase, i - 1))
                if filler:
                    steps.append(filler.pop(0))
                if 2 <= i <= count + 1:
                    steps.append(("turn", phase, i - 2))
                if 3 <= i:
                    steps.append(("value", phase, i - 3))
            steps.extend(filler)

        steps.append(("setup",))
        steps.append(("norm", "norm_mix_g"))
        steps += proj("q") + proj("k")
        steps.append(("memscale",))
        steps += proj("v") + proj("u")
        steps.append(("conv",))
        steps += proj("y")
        steps.append(("norm", "norm_mem_g"))
        steps.append(("rggate",))
        ck, cv = proj("ck"), proj("cv")
        steps += [ck[0], ("rg1",), ck[1], ("rg2",), cv[0], cv[1], ("mix", 1)]
        attend("dil", 8)
        steps.append(("mix", 0))
        steps += proj("wout", js=range(4))
        steps.append(("norm", "norm_cross_g"))
        steps += proj("cq")
        attend("cross", 4)
        steps += proj("co", n=0)
        steps.append(("norm", "norm_mlp_g"))
        steps += proj("up", js=range(16))
        steps += proj("down", js=range(16))
        steps.append(("finalnorm",))
        assert pieces == N_PIECES_1
        for l in range(L2):
            steps.append(("norm", f"ln_mix_{l}"))
            steps += proj("a", l) + proj("b", l)
            steps.append(("aturn", l))
            steps += proj("hg", l, (0,)) + proj("kr", l, (0,), KT * 32 + 96)
            c = proj("c", l)
            steps += [c[0], ("znorm", l), c[1]]
            steps.append(("bturn", l))
            steps += proj("f", l)
            steps.append(("zturn", l))
            steps += proj("e", l)
            steps.append(("fnet", l))
            gates = [("gate", l, g, half, piece(by="pool")) for g in range(4) for half in range(2)]
            attend(f"mla{l}", 4, gates[:4])
            attend(f"diff{l}", 4, gates[4:])
            pairs = lambda kind, i: [(kind, l, i, hp) for hp in range(2)]
            steps += pairs("decay", 0)
            steps.append(("merge", l, 0, piece(0)))
            steps.append(("diffnorm", l))
            steps += pairs("query", 0) + pairs("decay", 1)
            steps.append(("merge", l, 1, piece(0)))
            steps.append(("diffout", l))
            steps += pairs("query", 1)
            gates = [("gate", l, g, half, piece()) for g in range(4, 8) for half in range(2)]
            for i in range(len(LEVELS) + 1):
                if i + 2 < len(LEVELS):
                    steps += pairs("decay", i + 2)
                steps += pairs("level", i)
                if i + 2 < len(LEVELS):
                    steps += pairs("query", i + 2)
                if i != 7 and len(gates) > 1:
                    steps.append(gates.pop(0))
            steps.append(("hval", l))
            steps += gates
            steps.append(("merge", l, 2, piece(0)))
            steps.append(("hout", l))
            steps.append(("merge", l, 3, piece(0)))
            steps += proj("wout", l, range(4))
            steps.append(("norm", f"ln_ffn_{l}"))
            steps += proj("gu", l, range(22))
            steps += proj("wd", l, range(11))
        assert pieces == NP, pieces
        norms = [s[1] for s in steps if s[0] == "norm"]
        stats = [s[1] if s[0] == "norm" else "final" for s in steps if s[0] in ("norm", "finalnorm")]

        side_order = [(l, what) for l in range(L2) for what in ("a", "b", "z", "do", "ho")]

        def wait_h(eng, name, tt):
            if name == "ln_mix_0":
                eng.wait_ge(s_hn, tt + 1)
            elif name not in ("norm_mix_g", "norm_mem_g"):
                wait_drained(eng, {"norm_cross_g": "wout.3", "norm_mlp_g": f"co.1.{tt}", "final": f"down.{tt}1", "ln_mix_1": f"wd0.{tt}1",
                                   "ln_ffn_0": "wout0.3", "ln_ffn_1": "wout1.3"}[name])

        def job_of(name, l, j):
            return f"{name}{'' if l is None else l}.{j}"

        def product_of(name, l, j):
            return j if name == "up" else 16 + 11 * l + j // 2

        block = ctx.enter_context(nc.Block())

        @block.tensor
        def _(pe):
            rot = {"g": 0, "m": 0}
            banks = {"g": (0, 1, 2), "m": (3, 4, 5, 6, 7)}

            def fill(name, group):
                if isinstance(group, int):
                    b = group
                else:
                    b = banks[group][rot[group] % len(banks[group])]
                    rot[group] += 1
                if uses[b]:
                    pe.wait_ge(drained[b], uses[b])
                jobs[name] = (b, uses[b])
                uses[b] += 1
                return psum[b]

            def full(ins, name):
                ins.then_inc(filled[jobs[name][0]], 1)

            reads = 0

            def loaded(p):
                pe.wait_ge(piece_loaded[p % RING], 16 * (p // RING + 1))
                return raw(p)

            def mm(out, lhsT, rhs, first, last):
                return nc.tensor.matmul(out, lhsT, rhs, start=first, stop=last)

            def gemm(job, group, p, form, n=256):
                q = split_of[p]
                bank = fill(job, group)
                hi, lo = (w[:, q % SPLITS, 0:KT * n].rearrange("p (k c) -> p k c", k=KT) for w in (w_hi, w_lo))
                pe.wait_ge(s_whi, 2 * q + 1)
                for half in range(2):
                    cut = slice(half * P, (half + 1) * P)
                    for i, (w, x) in enumerate(((hi, x_hi), (hi, x_lo), (lo, x_hi))):
                        if half == 0 and i == 2:
                            wait_low(pe, q)
                        for k in range(KT):
                            if half == i == 0 and k == KT // 2:
                                pe.wait_ge(s_whi, 2 * (q + 1))
                            lhsT, rhs = (w[:, k, cut], x[:, k, :]) if form == "feat" else (x[:, k, cut], w[:, k, :])
                            ins = mm(bank[:, half * 256:half * 256 + n], lhsT, rhs, i == k == 0, i == 2 and k == KT - 1)
                full(ins, job)
                last_job[p] = job

            def plain(name, group, src, w, kts, n, p=None):
                for tt in range(TT):
                    bank = fill(f"{name}.{tt}", group)
                    for i, k in enumerate(kts):
                        ins = mm(bank[:, 0:n], src[:, k, tt * P:(tt + 1) * P], w[:, i, :], i == 0, i == len(kts) - 1)
                    full(ins, f"{name}.{tt}")
                if p is not None:
                    last_job[p] = f"{name}.{TT - 1}"

            def turns(name, src, tiles, group="m"):
                for j in range(0, tiles, 2):
                    job = f"{name}.{j // 2}"
                    bank = fill(job, group)
                    for jj in range(min(2, tiles - j)):
                        for tt in range(TT):
                            piece = src(j + jj, tt)
                            ins = nc.tensor.transpose(bank[0:piece.shape[1], jj * S + tt * P:jj * S + (tt + 1) * P], piece, ident)
                    full(ins, job)

            def score_operands(phase, hd, j):
                if phase == "dil":
                    q, k = at(A_Q1, 2, 2, S), at(A_K1, 2, 2, S)
                    p0 = 32 * (hd % 4)
                    return [(lambda qt, f=f: q[p0:p0 + 32, hd // 4, f, qt * P:(qt + 1) * P], k[p0:p0 + 32, hd // 4, f, :]) for f in range(2)]
                if phase == "cross":
                    q, k = at(A_CQ, 4, S), at(A_CK, 4, S)
                    return [(lambda qt: q[:, hd, qt * P:(qt + 1) * P], k[:, hd, :])]
                if phase[:3] == "mla":
                    z = at(A_QKT, 8, S)
                    return [(lambda qt: z[0:96, hd, qt * P:(qt + 1) * P], z[0:96, 4 + hd, :])]
                z = at(A_DT, 4, S)
                hh = 2 * hd + j
                p0 = 32 * (hh % 4)
                return [(lambda qt: z[p0:p0 + 32, hh // 4, qt * P:(qt + 1) * P], z[p0:p0 + 32, 2 + hh // 4, :])]

            for step in steps:
                kind = step[0]
                if kind == "setup":
                    pe.wait_ge(s_const, 16)
                elif kind == "norm":
                    name = step[1]
                    pe.wait_ge(s_scaled, norms.index(name) + 1)
                    src = at(A_MEM, TT, D) if name == "norm_mem_g" else xs
                    turns(name, lambda k, tt: src[:, tt, k * P:(k + 1) * P], KT)
                elif kind == "proj":
                    _, name, l, j, p = step
                    job = job_of(name, l, j)
                    before = {"q": "norm_mix_g", "ck": "norm_mem_g", "cq": "norm_cross_g", "a": f"ln_mix_{l}", "up": "norm_mlp_g",
                              "gu": f"ln_ffn_{l}"}.get(name)
                    if before and j == 0:
                        for i in range(KT // 2):
                            wait_drained(pe, f"{before}.{i}")
                    if name == "wout" and j == 0:
                        if l is None:
                            pe.wait_ge(s_xlo, 2)
                        else:
                            pe.wait_ge(s_mlo, 4 * (l + 1))
                    if name in ("q", "k", "u", "y", "ck", "cq", "e", "f"):
                        gemm(job, "g", p, "feat")
                    elif name in ("v", "cv", "wout", "a", "b", "c", "hg"):
                        gemm(job, "g", p, "tok")
                    elif name in ("up", "gu"):
                        gemm(job, "m", p, "feat")
                    elif name == "co":
                        if j == 0:
                            for hd in range(4):
                                wait_drained(pe, f"value.cross{hd}")
                        plain(job, "g", at(A_CO, 4, S), loaded(p).rearrange("p (k c) -> p k c", k=4), range(4), 512, p)
                    elif name == "kr":
                        q = split_of[p]
                        bank = fill(job, "g")
                        pe.wait_ge(s_whi, 2 * (q + 1))
                        wait_low(pe, q)
                        for i, (w, x) in enumerate(((w_hi, x_hi), (w_hi, x_lo), (w_lo, x_hi))):
                            for k in range(KT):
                                ins = mm(bank[:, 0:S], w[:, q % SPLITS, 32 * k:32 * k + P], x[:, k, :], i == k == 0, i == 2 and k == KT - 1)
                        full(ins, job)
                        w = loaded(p)
                        cT = at(A_CT, 4, S)
                        for i in range(2):
                            wait_drained(pe, f"aturn{l}.{i}")
                        plain(f"uq{l}", "m", cT, w[:, 256:256 + 1152].rearrange("p (k c) -> p k c", k=3), range(3), 384)
                        plain(f"ukv{l}", "m", cT, w[:, 1408:1920].rearrange("p (k c) -> p k c", k=1), [3], 512, p)
                        wait_drained(pe, job)
                        bank = fill(f"krt{l}", "g")
                        for tt in range(TT):
                            ins = nc.tensor.transpose(bank[:, 32 * tt:32 * tt + 32], at(A_KR, S)[0:32, tt * P:(tt + 1) * P], ident[0:32, 0:32])
                        full(ins, f"krt{l}")
                    elif name in ("down", "wd"):
                        tag = job_of(name, l, "")
                        count = 16 if name == "down" else 11
                        q = split_of[p]
                        hi, lo = (w[:, q % SPLITS, :].rearrange("p (k c) -> p k c", k=2) for w in (w_hi, w_lo))
                        if j == 0:
                            acc = {(tt, c): fill(f"{tag}{tt}{c}", 2 * tt + c) for tt in range(TT) for c in range(2)}
                        pe.wait_ge(s_plo, (j if name == "down" else product_of("gu", l, 2 * j)) + 1)
                        pe.wait_ge(s_whi, 2 * (q + 1))
                        passes = ((hi, hid_hi), (hi, hid_lo), (lo, hid_hi))

                        def accumulate(tt, c, i):
                            w, x = passes[i]
                            for k in range(2):
                                ins = mm(acc[tt, c][:, :], x[:, 2 * j + k, tt * P:(tt + 1) * P], w[:, k, 512 * c:512 * c + 512],
                                         i == j == k == 0, i == 2 and k == 1 and j == count - 1)
                            return ins

                        if j < count - 1:
                            for i in range(3):
                                if i == 2:
                                    wait_low(pe, q)
                                for tt in range(TT):
                                    for c in range(2):
                                        ins = accumulate(tt, c, i)
                            ins.then_inc(s_read, 1)
                            reads += 1
                            last_job[p] = reads
                        else:
                            wait_low(pe, q)
                            for tt in range(TT):
                                for c in range(2):
                                    for i in range(3):
                                        ins = accumulate(tt, c, i)
                                    full(ins, f"{tag}{tt}{c}")
                            last_job[p] = f"{tag}11"
                elif kind == "rggate":
                    pe.wait_ge(s_rgw, 16)
                    pe.wait_ge(s_conv, 1)
                    rgw = at(A_RGW, 2, 4, 2, P)
                    uc = at(A_UC, 4, S)
                    for z in range(2):
                        for ct in range(4):
                            name = f"rg.{z}{ct}"
                            bank = fill(name, "m")
                            for ax in range(2):
                                ins = mm(bank[:, ax * S:(ax + 1) * S], rgw[:, z, ct, ax, :], uc[:, ct, :], True, True)
                            full(ins, name)
                elif kind == "score":
                    phase, hd = step[1:]
                    _, a0, count = ATT[phase, hd]
                    if hd == 0:
                        for name in {"dil": ["rope"], "cross": ["cq.0", "cq.1", "ck.0", "ck.1"], "mla": [f"zturn{phase[-1]}.{j}" for j in range(4)],
                                     "dif": [f"bturn{phase[-1]}.{j}" for j in range(2)]}[phase[:3] if phase != "cross" else phase]:
                            if name == "rope":
                                pe.wait_ge(s_rope, 1)
                                for i in range(2):
                                    wait_drained(pe, f"v.{i}")
                            else:
                                wait_drained(pe, name)
                    for j in range(count):
                        name = f"score{a0 + j}"
                        bank = fill(name, "m")
                        ops = score_operands(phase, hd, j)
                        for qt in range(TT):
                            for f, (lhs, rhs) in enumerate(ops):
                                ins = mm(bank[:, qt * S:(qt + 1) * S], lhs(qt), rhs, f == 0, f == len(ops) - 1)
                        full(ins, name)
                elif kind == "turn":
                    phase, hd = step[1:]
                    n, a0, count = ATT[phase, hd]
                    pe.wait_ge(s_prob, n + 1)
                    name = f"turn{n}"
                    bank = fill(name, "m")
                    base = A_SC1 if phase in ("dil", "cross") else A_SC
                    prob = at(base + 512 * (a0 % 4), TT, S)
                    for kt in range(TT):
                        for qt in range(TT):
                            ins = nc.tensor.transpose(bank[:, kt * S + qt * P:kt * S + (qt + 1) * P], prob[:, qt, kt * P:(kt + 1) * P], ident)
                    full(ins, name)
                elif kind == "value":
                    phase, hd = step[1:]
                    n, a0, count = ATT[phase, hd]
                    wait_drained(pe, f"turn{n}")
                    base = A_SC1 if phase in ("dil", "cross") else A_SC
                    pT = at(base + 2048 + 512 * (n % 2), TT, S)
                    if phase == "dil" or phase[:3] == "mla":
                        v = at(A_V1, TT, 512) if phase == "dil" else at(A_VM, TT, 256)
                        name = f"value.{phase}{hd // 2}"
                        if hd % 2 == 0:
                            bank = fill(name, "m")
                        else:
                            bank = psum[jobs[name][0]]
                        p0 = 64 * (hd % 2)
                        for kt in range(TT):
                            ins = mm(bank[p0:p0 + 64, 0:S], v[:, kt, 64 * hd:64 * hd + 64], pT[:, kt, :], kt == 0, kt == TT - 1)
                        if hd % 2:
                            full(ins, name)
                        else:
                            ins.then_inc(s_even, 1)
                    elif phase == "cross":
                        v = at(A_CV, TT, 512)
                        if hd == 0:
                            for tt in range(TT):
                                wait_drained(pe, f"cv.{tt}")
                        name = f"value.cross{hd}"
                        bank = fill(name, "m")
                        for kt in range(TT):
                            ins = mm(bank[:, 0:S], v[:, kt, P * hd:P * hd + P], pT[:, kt, :], kt == 0, kt == TT - 1)
                        full(ins, name)
                    else:
                        v = at(A_VC, TT, 512)
                        if hd == 0:
                            for tt in range(TT):
                                wait_drained(pe, f"c{phase[4]}.{tt}")
                        name = f"value.{phase}{hd}"
                        bank = fill(name, "m")
                        for qt in range(TT):
                            for kt in range(TT):
                                ins = mm(bank[:, qt * P:(qt + 1) * P], pT[:, kt, qt * P:(qt + 1) * P], v[:, kt, P * (hd // 2):P * (hd // 2) + P],
                                         kt == 0, kt == TT - 1)
                        full(ins, name)
                elif kind == "aturn":
                    l = step[1]
                    pe.wait_ge(s_tok, side_order.index((l, "a")) + 1)
                    za = at(A_ZA, TT, 512)
                    turns(f"aturn{l}", lambda k, tt: za[:, tt, k * P:(k + 1) * P], 4)
                elif kind == "bturn":
                    l = step[1]
                    pe.wait_ge(s_tok, side_order.index((l, "b")) + 1)
                    zb = at(A_ZB, TT, 512)
                    turns(f"bturn{l}", lambda k, tt: zb[:, tt, k * P:(k + 1) * P], 4)
                elif kind == "zturn":
                    l = step[1]
                    pe.wait_ge(s_tok, side_order.index((l, "z")) + 1)
                    z = at(A_Z, TT, 8, 96)
                    turns(f"zturn{l}", lambda k, tt: z[:, tt, k, :], 8)
                elif kind == "diffout":
                    l = step[1]
                    pe.wait_ge(s_tok, side_order.index((l, "do")) + 1)
                    do = at(A_DO, TT, 256)
                    turns(f"diffout{l}", lambda k, tt: do[:, tt, k * P:(k + 1) * P], 2)
                elif kind == "hout":
                    l = step[1]
                    pe.wait_ge(s_tok, side_order.index((l, "ho")) + 1)
                    ho = at(A_HO, TT, 256)
                    turns(f"hout{l}", lambda k, tt: ho[:, tt, k * P:(k + 1) * P], 2)
                elif kind == "fnet":
                    l = step[1]
                    fT, ab = at(A_FT, 2, S), at(A_AB, TT, 2, S)
                    dftd = const[:, C_DFTD:C_DFTD + 2 * P]
                    dc = const[:, C_DFTC:C_DFTC + TT * S].rearrange("p (s t) -> p s t", s=TT)
                    ds = const[:, C_DFTS:C_DFTS + TT * S].rearrange("p (s t) -> p s t", s=TT)
                    wait_drained(pe, f"e{l}.0")
                    for st in range(TT):
                        bank = fill(f"fab{l}.{st}", "m")
                        for ft in range(2):
                            ins = mm(bank[:, ft * S:(ft + 1) * S], fT[:, ft, st * P:(st + 1) * P], dftd, True, True)
                        full(ins, f"fab{l}.{st}")
                    for st in range(TT):
                        wait_drained(pe, f"fab{l}.{st}")
                    bank = fill(f"fy{l}", "m")
                    for ft in range(2):
                        for st in range(TT):
                            mm(bank[:, ft * S:(ft + 1) * S], ab[:, st, ft, 0:P], dc[:, st, :], st == 0, False)
                            ins = mm(bank[:, ft * S:(ft + 1) * S], ab[:, st, ft, P:2 * P], ds[:, st, :], False, st == TT - 1)
                    full(ins, f"fy{l}")
                elif kind == "gate":
                    _, l, g, half, p = step
                    gemm(f"gate{l}.{g}{half}", "g", p, "feat")
                elif kind == "merge":
                    _, l, br, p = step
                    if br == 0:
                        for j in range(2):
                            wait_drained(pe, f"value.mla{l}{j}")
                    elif br == 1:
                        wait_drained(pe, f"fy{l}")
                    elif br == 2:
                        wait_drained(pe, f"diffout{l}.0")
                    else:
                        wait_drained(pe, f"hout{l}.0")
                    w = loaded(p).rearrange("p (k c) -> p k c", k=2)
                    for j in range(4):
                        job = f"merge{l}.{br}{j}"
                        bank = fill(job, "g")
                        for jj in range(2):
                            for k in range(2):
                                c0 = (2 * j + jj) * P
                                ins = mm(bank[:, jj * S:(jj + 1) * S], w[:, k, c0:c0 + P], oT[:, 2 * br + k, :], k == 0, k == 1)
                        full(ins, job)
                    last_job[p] = job
                elif kind == "level":
                    _, l, i, hp = step
                    job = f"level{l}.{i}{hp}"
                    if i < len(LEVELS):
                        idx = (l * len(LEVELS) + i) * 2 + hp
                        pe.wait_ge(s_Ql, idx + 1)
                        pe.wait_ge(s_Kl, idx + 1)
                        q = at(A_QL + 512 * (idx % 4), 2, S)
                        k = at(A_KL + 512 * (idx % 4), 2, S)
                        q0 = 0
                    else:
                        q, k, q0 = at(A_HQ, 4, S), at(A_KK, 4, S), 2 * hp
                        pe.wait_ge(s_hkk, l + 1)
                        wait_drained(pe, f"e{l}.1")
                    bank = fill(job, "m")
                    for hh in range(2):
                        for st in range(TT):
                            t0 = 1 - st if i == 0 else st
                            ins = mm(bank[:, (2 * hh + st) * P:(2 * hh + st + 1) * P], k[:, q0 + hh, st * P:(st + 1) * P],
                                     q[:, q0 + hh, t0 * P:(t0 + 1) * P], True, True)
                    full(ins, job)
                elif kind == "hval":
                    l = step[1]
                    sT, v = at(A_ST, 4, TT, S), at(A_VC, TT, 512)
                    for hp in range(2):
                        wait_drained(pe, f"level{l}.{len(LEVELS)}{hp}")
                        job = f"hval{l}.{hp}"
                        bank = fill(job, "m")
                        for tt in range(TT):
                            for hh in range(2):
                                for st in range(TT):
                                    ins = mm(bank[:, (2 * tt + hh) * P:(2 * tt + hh + 1) * P], sT[:, 2 * hp + hh, st, tt * P:(tt + 1) * P],
                                             v[:, st, 256 + hp * P:256 + (hp + 1) * P], st == 0, st == TT - 1)
                        full(ins, job)

        @block.sync
        def _(sp):
            sp.dma_start(h[:], x_d.rearrange("(t p) d -> p t d", p=P)).then_inc(s_x, 16)
            sp.dma_start(vec[:], vec_d).then_inc(s_vec, 16)
            sp.dma_start(const[:], const_d).then_inc(s_const, 16)

            def load_piece(p):
                if p >= RING:
                    old = p - RING
                    if old in split_of:
                        wait_low(sp, split_of[old])
                    if old not in split_of or split[split_of[old]][1] < PIECE:
                        wait_read(sp, old)
                sp.dma_start(raw(p), pieces_d[p]).then_inc(piece_loaded[p % RING], 16)

            load_piece(0)
            sp.dma_start(at(A_ROPE, S).bitcast(I32), pos_d).then_inc(s_pos, 16)
            load_piece(1)
            load_piece(2)
            sp.dma_start(at(A_MEM, TT, D), mem_d.rearrange("(t p) d -> p t d", p=P)).then_inc(s_mem, 16)
            sp.dma_start(at(A_RGW, 16 * P), rgw_d).then_inc(s_rgw, 16)
            sp.dma_start(row[:], row_d).then_inc(s_row, 16)
            for p in range(RING, NP):
                load_piece(p)
            for tt in range(TT):
                wait_drained(sp, f"wd1.{tt}1")
                sp.dma_start(out_d[tt * P:(tt + 1) * P, :], h[:, tt, :]).then_inc(s_out, 16)
            sp.wait_ge(s_out, 16 * TT)

        @block.gpsimd
        def _(pool):
            n_link = 0

            def link(ins):
                nonlocal n_link
                n_link += 1
                ins.then_inc(pool_link, 1)
                pool.wait_ge(pool_link, n_link)

            up = at(A_U, 4, UPAD)
            link(nc.gpsimd.memset(up[:, :, 0:2], 0.0))
            nc.gpsimd.memset(up[:, :, S + 2:S + 3], 0.0).then_inc(s_zero1, 1)
            done = 0

            def split_ahead(p):
                nonlocal done
                while done < min(split_of[p] + 2, len(split)):
                    q, (pp, n) = done, split[done]
                    done += 1
                    if low[q][0] != "pool":
                        continue
                    for half in range(2):
                        cut = slice(half * n // 2, (half + 1) * n // 2)
                        pool.wait_ge(s_whi, 2 * q + half + 1)
                        ins = nc.gpsimd.tensor_tensor(w_lo[:, q % SPLITS, cut], raw(pp)[:, cut], w_hi[:, q % SPLITS, cut].bitcast(F32), ALU.subtract)
                        if half == 0:
                            link(ins)
                        else:
                            ins.then_inc(s_wlo_pool, 1)

            for step in steps:
                kind = step[0]
                if kind in ("proj", "gate") and step[-1] in split_of:
                    split_ahead(step[-1])
                if kind == "decay":
                    _, l, i, hp = step
                    idx = (l * len(LEVELS) + i) * 2 + hp
                    half = LEVELS[i]
                    if i < 2 and hp == 0 and i == 0:
                        wait_filled(pool, f"score{ATT[f'diff{l}', 3][1] + 1}")
                    if idx >= 4:
                        prev = idx - 4
                        wait_filled(pool, f"level{prev // (2 * len(LEVELS))}.{prev // 2 % len(LEVELS)}{prev % 2}")
                    if idx:
                        pool.wait_ge(s_Kl, idx)
                    k = at(A_KL + 512 * (idx % 4), 2 * S)
                    link(nc.gpsimd.memset(k, 0.0))
                    pool.wait_ge(s_Xl, idx + 1)
                    x = at(A_X + 512 * (idx % 4), 2 * S).rearrange("p (b w c) -> p b w c", w=2, c=half)
                    kk = at(A_KK, 4 * S)[:, hp * 512:(hp + 1) * 512].rearrange("p (b w c) -> p b w c", w=2, c=half)
                    kl = k.rearrange("p (b w c) -> p b w c", w=2, c=half)
                    link(nc.gpsimd.tensor_tensor(kl[0:64, :, 0, :], kk[0:64, :, 0, :], x[0:64, :, 0, :], ALU.mult))
                    nc.gpsimd.tensor_tensor(kl[64:128, :, 1, :], kk[64:128, :, 1, :], x[64:128, :, 1, :], ALU.mult).then_inc(s_Kl, 1)

        @block.scalar
        def _(act):
            n_link = 0

            def link(ins):
                nonlocal n_link
                n_link += 1
                ins.then_inc(act_link, 1)
                act.wait_ge(act_link, n_link)

            def copy(out, in_, scale=1.0):
                return nc.scalar.activation(out, in_, ACT.Copy, scale=scale)

            def bank2(bank):
                return bank[:].rearrange("p (a t) -> p a t", a=2)

            done = 0

            def split_ahead(p):
                nonlocal done
                while done < min(split_of[p] + 2, len(split)):
                    q, (pp, n) = done, split[done]
                    done += 1
                    act.wait_ge(piece_loaded[pp % RING], 16 * (pp // RING + 1))
                    if q >= SPLITS:
                        wait_read(act, split[q - SPLITS][0])
                    for half in range(2):
                        cut = slice(half * n // 2, (half + 1) * n // 2)
                        copy(w_hi[:, q % SPLITS, cut], raw(pp)[:, cut]).then_inc(s_whi, 1)

            for step in steps:
                kind = step[0]
                p = step[-1] if kind in ("proj", "gate") else None
                if p in split_of:
                    split_ahead(p)
                if kind in ("norm", "finalnorm", "memscale"):
                    name = {"norm": step[-1], "finalnorm": "final", "memscale": "norm_mem_g"}[kind]
                    src = at(A_MEM, TT, D) if kind == "memscale" else h
                    if name == "norm_mix_g":
                        act.wait_ge(s_x, 16)
                    elif kind == "memscale":
                        act.wait_ge(s_mem, 16)
                    ss = col("ss." + name, TT)
                    for tt in range(TT) if kind != "norm" or name != "norm_mem_g" else ():
                        wait_h(act, name, tt)
                        ins = nc.scalar.activation(junk[:], src[:, tt, :], ACT.Square, accum_out=ss[:, tt:tt + 1])
                        if tt < TT - 1:
                            link(ins)
                        else:
                            ins.then_inc(s_sumsq, 1)
                    if kind == "norm":
                        if name == "norm_mix_g":
                            act.wait_ge(s_vec, 16)
                        if name == "norm_mix_g":
                            split_ahead(0)
                        gi = V_GAIN + GAINS.index(name) * KT
                        for k in range(KT):
                            bank = bank2(wait_filled(act, f"{name}.{k // 2}"))
                            ins = copy(x_hi[:, k, :], bank[:, k % 2, :], vec[:, gi + k:gi + k + 1])
                            if k % 2:
                                ins.then_inc(s_nhi, 1)
                    if name == "norm_mix_g":
                        act.wait_ge(s_ang, 1)
                        cs = at(A_ROPE, 2 * S)
                        nc.scalar.activation(cs, cs, ACT.Sin).then_inc(s_trig, 1)
                elif kind == "proj":
                    _, name, l, j, _ = step
                    job = job_of(name, l, j)
                    if name in ("v", "cv", "b", "c"):
                        dst = at({"v": A_V1, "cv": A_CV, "b": A_ZB, "c": A_VC}[name], TT, 512)
                        drains(copy(dst[:, :, 256 * j:256 * j + 256], bank2(wait_filled(act, job))), job)
                    elif name == "u":
                        up = at(A_U, 4, UPAD)
                        drains(copy(up[:, 2 * j:2 * j + 2, 2:2 + S], bank2(wait_filled(act, job))), job)
                    elif name == "y":
                        yg = at(A_YG, 4, S)
                        drains(nc.scalar.activation(yg[:, 2 * j:2 * j + 2, :], bank2(wait_filled(act, job)), ACT.Gelu_apprx_tanh), job)
                    elif name in ("ck", "cq"):
                        if name == "ck":
                            act.wait_ge(s_rope, 1)
                        dst = at(A_CK if name == "ck" else A_CQ, 4, S)
                        drains(copy(dst[:, 2 * j:2 * j + 2, :], bank2(wait_filled(act, job))), job)
                    elif name == "a":
                        za = at(A_ZA, TT, 512)
                        if l and j == 0:
                            wait_filled(act, "hval0.1")
                        ss = col(f"ss.a{l}", 3 * TT).rearrange("p (s t) -> p s t", t=TT)
                        bank = bank2(wait_filled(act, job))
                        copy(za[:, :, 256 * j:256 * j + 256], bank)
                        for tt in range(TT):
                            jk = junk[:, 512 * tt + 256 * j:512 * tt + 256 * j + 256]
                            if j == 0:
                                ins = nc.scalar.activation(jk, bank[:, tt, :], ACT.Square, scale=384.0 ** -0.5, accum_out=ss[:, 0, tt:tt + 1])
                            else:
                                nc.scalar.activation(jk[:, 0:128], bank[:, tt, 0:128], ACT.Square, scale=384.0 ** -0.5, accum_out=ss[:, 1, tt:tt + 1])
                                ins = nc.scalar.activation(jk[:, 128:256], bank[:, tt, 128:256], ACT.Square, scale=128.0 ** -0.5, accum_out=ss[:, 2, tt:tt + 1])
                        drains(ins, job)
                    elif name == "hg":
                        drains(nc.scalar.activation(at(A_SG, TT, 256), bank2(wait_filled(act, job)), ACT.Tanh, scale=0.5), job)
                    elif name == "kr":
                        z = at(A_Z, TT, 8, 96)
                        drains(copy(at(A_KR, S)[0:32, :], wait_filled(act, job)[0:32, 0:S]), job)
                        for tt in range(TT):
                            bank = wait_filled(act, f"uq{l}.{tt}")
                            drains(copy(z[:, tt, 0:4, :], bank[:, 0:384].rearrange("p (h d) -> p h d", h=4)), f"uq{l}.{tt}")
                        vm = at(A_VM, TT, 256)
                        for tt in range(TT):
                            bank = wait_filled(act, f"ukv{l}.{tt}")
                            copy(z[:, tt, 4:8, 0:64], bank[:, 0:256].rearrange("p (h d) -> p h d", h=4))
                            drains(copy(vm[:, tt, :], bank[:, 256:512]), f"ukv{l}.{tt}")
                        bank = wait_filled(act, f"krt{l}")[:, 0:64].rearrange("p (t d) -> p t d", t=TT)
                        drains(copy(z[:, :, 4:8, 64:96], bank[:, :, None, :].broadcast_to([P, TT, 4, 32])), f"krt{l}")
                    elif name == "f":
                        kk = at(A_KK, 4, S)
                        drains(nc.scalar.activation(kk[:, 2 * j:2 * j + 2, :], bank2(wait_filled(act, job)), ACT.Sigmoid), job)
                        if j == 1:
                            act.wait_ge(s_f, l + 1)
                            nc.scalar.activation(at(A_F, 4 * S), at(A_F, 4 * S), ACT.Ln).then_inc(s_lf, 1)
                    elif name == "e" and j == 0:
                        if l:
                            wait_filled(act, "wd0.11")
                        drains(copy(at(A_FT, 2, S), bank2(wait_filled(act, job))), job)
                    elif name == "e":
                        hq = at(A_HQ, 4, S)
                        bank = wait_filled(act, job)
                        for hd in range(4):
                            for d in range(2):
                                src = bank[64 * (hd % 2):64 * (hd % 2) + 64, S * (hd // 2):S * (hd // 2) + S]
                                ins = copy(hq[64 * d:64 * d + 64, hd, :], src)
                        drains(ins, job)
                    elif name == "gu" and j % 2 == 0:
                        m = product_of(name, l, j)
                        act.wait_ge(s_plo, m - 1)
                        drains(nc.scalar.activation(product[:, m % 2, :], wait_filled(act, job)[:], ACT.Silu), job)
                    elif name == "up" or name == "gu":
                        m = product_of(name, l, j)
                        k = 2 * (j if name == "up" else j // 2)
                        if name == "up":
                            if m >= 2:
                                act.wait_ge(s_plo, m - 1)
                            nc.scalar.activation(product[:, m % 2, :], wait_filled(act, job)[:], ACT.Relu).then_inc(s_relu, 1)
                        wait_drained(act, job)
                        copy(hid_hi[:, k:k + 2, :], product[:, m % 2, :].rearrange("p (a t) -> p a t", a=2)).then_inc(s_phi, 1)
                elif kind == "mix":
                    k = 4 * step[1]
                    if k:
                        act.wait_ge(s_rec, 1)
                        wait_filled(act, "cv.1")
                    else:
                        for i in range(4):
                            wait_drained(act, f"value.dil{i}")
                    copy(x_hi[:, k:k + 4, :], oT[:, k:k + 4, :]).then_inc(s_xhi, 1)
                elif kind == "rggate":
                    r, ii = at(A_RG_R, 2, 4, S), at(A_RG_I, 2, 4, S)
                    for z in range(2):
                        for ct in range(4):
                            name = f"rg.{z}{ct}"
                            bank = bank2(wait_filled(act, name))
                            b0 = V_RGB + (z * 4 + ct) * 2
                            nc.scalar.activation(r[:, z, ct, :], bank[:, 0, :], ACT.Sigmoid, bias=vec[:, b0:b0 + 1])
                            drains(nc.scalar.activation(ii[:, z, ct, :], bank[:, 1, :], ACT.Sigmoid, bias=vec[:, b0 + 1:b0 + 2]), name)
                    act.wait_ge(s_sp, 1)
                    nc.scalar.activation(col("sp.x", 8), col("sp.na", 8), ACT.Exp).then_inc(s_spe, 1)
                    act.wait_ge(s_lb, 1)
                    nc.scalar.activation(col("lb.x", 8), col("lb.e", 8), ACT.Exp).then_inc(s_lbe, 1)
                elif kind == "rg1":
                    act.wait_ge(s_rgy, 1)
                    nc.scalar.activation(at(A_RG_T, 2048), at(A_RG_R, 2048), ACT.Tanh)
                    nc.scalar.activation(at(A_RG_A, 2048), at(A_RG_R, 2048), ACT.Exp, scale=-1.0).then_inc(s_rgta, 1)
                elif kind == "rg2":
                    act.wait_ge(s_rgw2, 1)
                    nc.scalar.activation(at(A_RG_T, 2048), at(A_RG_T, 2048), ACT.Sqrt).then_inc(s_rgs, 1)
                elif kind == "score":
                    phase, hd = step[1:]
                    n, a0, count = ATT[phase, hd]
                    masked = phase == "dil"
                    scale = {"dil": 1.0, "cro": 128.0 ** -0.5, "mla": 96.0 ** -0.5, "dif": 32.0 ** -0.5}[phase[:3]]
                    base = A_SC1 if phase in ("dil", "cross") else A_SC
                    if phase[:4] == "diff" and hd == 0:
                        act.wait_ge(s_lam, int(phase[4]) + 1)
                        nc.scalar.activation(col(f"lam.e{phase[4]}", 2), col(f"lam.d{phase[4]}", 2), ACT.Exp).then_inc(s_lame, 1)
                    for j in range(count):
                        a = a0 + j
                        sc = at(base + 512 * (a % 4), TT, S)
                        act.wait_ge(s_max, a + 1)
                        if not masked:
                            if a >= 4:
                                n4 = ATT[HEAD_OF_UNIT[a - 4]][0]
                                wait_filled(act, f"turn{n4}")
                            src = bank2(wait_filled(act, f"score{a}"))
                        else:
                            src = sc
                        nm, sm = col(f"nmax{a % 16}", TT), col(f"sum{a % 16}", TT)
                        for qt in range(TT):
                            ins = nc.scalar.activation(sc[:, qt, :], src[:, qt, :], ACT.Exp, bias=nm[:, qt:qt + 1], scale=scale, accum_out=sm[:, qt:qt + 1])
                        if masked:
                            ins.then_inc(s_exp, 1)
                        else:
                            drains(ins, f"score{a}")
                elif kind == "turn":
                    phase, hd = step[1:]
                    n, a0, count = ATT[phase, hd]
                    base = A_SC1 if phase in ("dil", "cross") else A_SC
                    pT = at(base + 2048 + 512 * (n % 2), 512)
                    if n >= 2:
                        ph, h2, _ = HEADS[n - 2]
                        if ph in ("cross", "diff0", "diff1"):
                            wait_filled(act, f"value.{ph}{h2}")
                        elif h2 % 2:
                            wait_filled(act, f"value.{ph}{h2 // 2}")
                        else:
                            act.wait_ge(s_even, EVEN[n - 2])
                    drains(copy(pT, wait_filled(act, f"turn{n}")[:]), f"turn{n}")
                elif kind == "value":
                    phase, hd = step[1:]
                    if phase == "cross":
                        name = f"value.cross{hd}"
                        drains(copy(at(A_CO, 4, S)[:, hd, :], wait_filled(act, name)[:, 0:S]), name)
                    elif phase[:4] == "diff":
                        name = f"value.{phase}{hd}"
                        do = at(A_DO, TT, 4, 64)
                        bank = wait_filled(act, name)[:, 0:256].rearrange("p (q c) -> p q c", q=2)
                        drains(copy(do[:, :, hd, :], bank[:, :, 64 * (hd % 2):64 * (hd % 2) + 64]), name)
                    elif hd % 2:
                        name = f"value.{phase}{hd // 2}"
                        drains(copy(oT[:, hd // 2, :], wait_filled(act, name)[:, 0:S]), name)
                elif kind == "aturn":
                    l = step[1]
                    cT = at(A_CT, 4, S)
                    for j in range(2):
                        bank = bank2(wait_filled(act, f"aturn{l}.{j}"))
                        for jj in range(2):
                            k = 2 * j + jj
                            ins = copy(cT[:, k, :], bank[:, jj, :], vec[:, V_QA + 4 * l + k:V_QA + 4 * l + k + 1])
                        drains(ins, f"aturn{l}.{j}")
                elif kind == "bturn":
                    l = step[1]
                    dT = at(A_DT, 4, S)
                    for j in range(2):
                        drains(copy(dT[:, 2 * j:2 * j + 2, :], bank2(wait_filled(act, f"bturn{l}.{j}"))), f"bturn{l}.{j}")
                elif kind == "zturn":
                    l = step[1]
                    z = at(A_QKT, 8, S)
                    for j in range(4):
                        bank = bank2(wait_filled(act, f"zturn{l}.{j}"))
                        drains(copy(z[0:96, 2 * j:2 * j + 2, :], bank[0:96, :, :]), f"zturn{l}.{j}")
                elif kind == "fnet":
                    l = step[1]
                    ab = at(A_AB, TT, 2, S)
                    for st in range(TT):
                        drains(copy(ab[:, st, :, :], bank2(wait_filled(act, f"fab{l}.{st}"))), f"fab{l}.{st}")
                    drains(copy(oT[:, 2:4, :], bank2(wait_filled(act, f"fy{l}"))), f"fy{l}")
                elif kind == "gate":
                    _, l, g, half, _ = step
                    gate = at(A_GATE, 16, S)
                    k = (4 * g + 2 * half) % 16
                    if g >= 4:
                        act.wait_ge(s_merged, l + 1)
                    drains(nc.scalar.activation(gate[:, k:k + 2, :], bank2(wait_filled(act, f"gate{l}.{g}{half}")), ACT.Tanh, scale=0.5), f"gate{l}.{g}{half}")
                elif kind == "merge" and step[2] == 3:
                    l = step[1]
                    for j in range(4):
                        act.wait_ge(s_msum, 4 * l + j + 1)
                        copy(x_hi[:, 2 * j:2 * j + 2, :], merged[:, 2 * j:2 * j + 2, :]).then_inc(s_mhi, 1)
                elif kind in ("diffout", "hout"):
                    l = step[1]
                    k = 4 if kind == "diffout" else 6
                    drains(copy(oT[:, k:k + 2, :], bank2(wait_filled(act, f"{kind}{l}.0"))), f"{kind}{l}.0")
                elif kind == "decay":
                    _, l, i, hp = step
                    idx = (l * len(LEVELS) + i) * 2 + hp
                    act.wait_ge(s_Dl, idx + 1)
                    x = at(A_X + 512 * (idx % 4), 512)
                    nc.scalar.activation(x, x, ACT.Exp).then_inc(s_Xl, 1)
                elif kind == "hval":
                    l = step[1]
                    ho = at(A_HO, TT, 4, 64)
                    for hp in range(2):
                        name = f"hval{l}.{hp}"
                        bank = wait_filled(act, name)[:].rearrange("p (t h c) -> p t h c", t=2, h=2)
                        copy(ho[:, :, 2 * hp, :], bank[:, :, 0, 0:64])
                        drains(copy(ho[:, :, 2 * hp + 1, :], bank[:, :, 1, 64:128]), name)

        @block.vector
        def _(dve):
            n_link = 0
            v = nc.vector

            def link(ins):
                nonlocal n_link
                n_link += 1
                ins.then_inc(dve_link, 1)
                dve.wait_ge(dve_link, n_link)

            def bank2(bank):
                return bank[:].rearrange("p (a t) -> p a t", a=2)

            def rsqrt(x, y, t, n):
                link(v.tensor_scalar(t.bitcast(I32), x.bitcast(I32), 1, None, ALU.logical_shift_right))
                link(v.tensor_scalar(y.bitcast(I32), t.bitcast(I32), -1.0, float(RSQRT_MAGIC), ALU.mult, ALU.add))
                for _ in range(3):
                    link(v.tensor_tensor(t, y, y, ALU.mult))
                    link(v.scalar_tensor_tensor(t, t, -0.5, x, ALU.mult, ALU.mult))
                    link(v.scalar_tensor_tensor(y, t, 1.5, y, ALU.add, ALU.mult))

            def heads_norm(zv, groups, n, scratch):
                sq = scratch[:, 0:groups * n].rearrange("p (a g n) -> p a g n", a=TT, n=n)
                ss, rs, t = col("hn.ss", 32)[:, 0:groups], col("hn.rs", 32)[:, 0:groups], col("hn.t", 32)[:, 0:groups]
                link(v.tensor_tensor(sq, zv, zv, ALU.mult))
                link(v.tensor_reduce(ss, sq.rearrange("p a g n -> p (a g) n"), AX_X, ALU.add))
                link(v.tensor_scalar(ss, ss, 1.0 / n, EPS, ALU.mult, ALU.add))
                rsqrt(ss, rs, t, groups)
                return rs

            def rope32(x1, x2, heads):
                c = const[:, C_COS:C_COS + TT * 16].rearrange("p (a d) -> p a d", a=TT)[:, :, None, :].broadcast_to([P, TT, heads, 16])
                s = const[:, C_SIN:C_SIN + TT * 16].rearrange("p (a d) -> p a d", a=TT)[:, :, None, :].broadcast_to([P, TT, heads, 16])
                n = TT * heads * 16
                t = [scratch_xs[:, i * n:(i + 1) * n].rearrange("p (a g d) -> p a g d", a=TT, d=16) for i in range(4)]
                v.tensor_tensor(t[0], x1, c, ALU.mult)
                v.tensor_tensor(t[1], x2, s, ALU.mult)
                v.tensor_tensor(t[2], x1, s, ALU.mult)
                link(v.tensor_tensor(t[3], x2, c, ALU.mult))
                v.tensor_tensor(x1, t[0], t[1], ALU.subtract)
                return v.tensor_tensor(x2, t[2], t[3], ALU.add)

            scratch_xs = xs[:].rearrange("p a b -> p (a b)")
            def level_decay(l, i, hp):
                idx, half = (l * len(LEVELS) + i) * 2 + hp, LEVELS[i]
                nb = S // (2 * half)
                E, F = at(A_E, 4, S + 1), at(A_F, 4, S)
                if idx >= 4:
                    dve.wait_ge(s_Kl, idx - 3)
                    dve.wait_ge(s_Ql, idx - 3)
                x = at(A_X + 512 * (idx % 4), 2 * S).rearrange("p (g b w c) -> p g b w c", g=2, w=2, c=half)
                f5 = F[:, 2 * hp:2 * hp + 2, :].rearrange("p g (b w c) -> p g b w c", w=2, c=half)
                mid = E[:, 2 * hp:2 * hp + 2, half:S:2 * half][:, :, :, None].broadcast_to([P, 2, nb, half])
                v.tensor_tensor(x[:, :, :, 0, :], mid, f5[:, :, :, 0, :], ALU.subtract)
                v.tensor_tensor(x[:, :, :, 1, :], f5[:, :, :, 1, :], mid, ALU.subtract).then_inc(s_Dl, 1)

            def level_query(l, i, hp):
                idx = (l * len(LEVELS) + i) * 2 + hp
                dve.wait_ge(s_Xl, idx + 1)
                if idx >= 4:
                    prev = idx - 4
                    wait_filled(dve, f"level{prev // (2 * len(LEVELS))}.{prev // 2 % len(LEVELS)}{prev % 2}")
                q = at(A_HQ, 4 * S)[:, hp * 512:(hp + 1) * 512]
                v.tensor_tensor(at(A_QL + 512 * (idx % 4), 2 * S), q, at(A_X + 512 * (idx % 4), 2 * S), ALU.mult).then_inc(s_Ql, 1)

            def level_place(l, i, hp):
                job = f"level{l}.{i}{hp}"
                bank = wait_filled(dve, job)[:].rearrange("p (g s c) -> p g s c", g=2, s=2)
                sT = at(A_ST + 1024 * hp, 2, 4, P)
                if i == 0:
                    drains(v.tensor_copy(sT[:, :, 1:3, :], bank), job)
                elif i == 1:
                    drains(v.tensor_copy(sT[:, :, 0:4:3, :], bank), job)
                else:
                    if i == 2:
                        wait_drained(dve, f"level{l}.1{hp}")
                    else:
                        wait_drained(dve, f"level{l}.{i - 1}{hp}")
                    m0 = C_MASK + (i - 2) * P
                    mask = const[:, m0:m0 + P].bitcast(I32)[:, None, None, :].broadcast_to([P, 2, 2, P])
                    drains(v.copy_predicated(sT[:, :, 0:4:3, :], mask, bank), job)
            def split_ahead(p):
                nonlocal done
                while done < min(split_of[p] + 2, len(split)):
                    q, (pp, n) = done, split[done]
                    done += 1
                    if low[q][0] != "dve":
                        continue
                    dve.wait_ge(s_whi, 2 * (q + 1))
                    v.tensor_tensor(w_lo[:, q % SPLITS, 0:n], raw(pp)[:, 0:n], w_hi[:, q % SPLITS, 0:n].bitcast(F32), ALU.subtract).then_inc(s_wlo, 1)

            def product_low(m):
                k = 2 * (m if m < 16 else (m - 16) % 11)
                dve.wait_ge(s_phi, m + 1)
                v.tensor_tensor(hid_lo[:, k:k + 2, :], product[:, m % 2, :].rearrange("p (a t) -> p a t", a=2),
                                hid_hi[:, k:k + 2, :].bitcast(F32), ALU.subtract).then_inc(s_plo, 1)

            def merged_low(l, j):
                dve.wait_ge(s_mhi, 4 * l + j + 1)
                v.tensor_tensor(x_lo[:, 2 * j:2 * j + 2, :], merged[:, 2 * j:2 * j + 2, :], x_hi[:, 2 * j:2 * j + 2, :].bitcast(F32),
                                ALU.subtract).then_inc(s_mlo, 1)

            done = 0
            for step in steps:
                kind = step[0]
                p = step[-1] if kind in ("proj", "gate") else None
                if p in split_of:
                    split_ahead(p)
                if kind in ("norm", "finalnorm", "memscale"):
                    name = {"norm": step[-1], "finalnorm": "final", "memscale": "norm_mem_g"}[kind]
                    ss, rs, t = col("ss." + name, TT), col("rs." + name, TT), col("nt", TT)
                    if kind != "norm" or name != "norm_mem_g":
                        dve.wait_ge(s_sumsq, stats.index(name) + 1)
                        link(v.tensor_scalar(ss, ss, 1.0 / D, EPS, ALU.mult, ALU.add))
                        rsqrt(ss, rs, t, TT)
                    if kind == "finalnorm":
                        dve.wait_ge(s_row, 16)
                        for tt in range(TT):
                            ins = v.scalar_tensor_tensor(h[:, tt, :], h[:, tt, :], rs[:, tt:tt + 1], row[:, R_FINAL:R_FINAL + D], ALU.mult, ALU.mult)
                            ins.then_inc(s_hn, 1)
                        continue
                    src = at(A_MEM, TT, D) if name == "norm_mem_g" else h
                    dst = src if name == "norm_mem_g" else xs
                    if kind == "memscale" or name != "norm_mem_g":
                        v.tensor_scalar(dst[:, 0, :], src[:, 0, :], rs[:, 0:1], None, ALU.mult)
                        v.tensor_scalar(dst[:, 1, :], src[:, 1, :], rs[:, 1:2], None, ALU.mult).then_inc(s_scaled, 1)
                    if kind == "memscale":
                        continue
                    if name == "norm_mix_g":
                        dve.wait_ge(s_vec, 16)
                        split_ahead(0)
                    gi = V_GAIN + GAINS.index(name) * KT
                    for k in range(KT):
                        if k % 2 == 0:
                            dve.wait_ge(s_nhi, norms.index(name) * KT // 2 + k // 2 + 1)
                        bank = bank2(wait_filled(dve, f"{name}.{k // 2}"))
                        ins = v.scalar_tensor_tensor(x_lo[:, k, :], bank[:, k % 2, :], vec[:, gi + k:gi + k + 1], x_hi[:, k, :].bitcast(F32), ALU.mult, ALU.subtract)
                        if k % 2:
                            drains(ins, f"{name}.{k // 2}")
                    if name == "norm_mix_g":
                        dve.wait_ge(s_pos, 16)
                        dve.wait_ge(s_const, 16)
                        r4 = at(A_ROPE, 4, S)
                        ang, n = r4[:, 2, :], r4[:, 3, :]
                        link(v.tensor_copy(n, r4[:, 0, :].bitcast(I32)))
                        link(v.tensor_scalar(ang, n, const[:, C_FREQ:C_FREQ + 1], None, ALU.mult))
                        for f, (quarter, shift) in enumerate(((0.25, 0.5 * np.pi), (0.0, 0.0))):
                            out = r4[:, f, :]
                            link(v.tensor_scalar(n, ang, float(1.0 / (2.0 * np.pi)), quarter, ALU.mult, ALU.add))
                            link(v.tensor_scalar(n, n, ROUND, None, ALU.add))
                            link(v.tensor_scalar(n, n, ROUND, None, ALU.subtract))
                            link(v.scalar_tensor_tensor(out, n, -TWO_PI_HI, ang, ALU.mult, ALU.add))
                            link(v.scalar_tensor_tensor(out, n, -TWO_PI_MID, out, ALU.mult, ALU.add))
                            link(v.scalar_tensor_tensor(out, n, -TWO_PI_LO, out, ALU.mult, ALU.add))
                            link(v.tensor_scalar(out, out, shift, 3.1415925, ALU.add, ALU.min))
                            ins = v.tensor_scalar(out, out, -3.1415925, None, ALU.max)
                            if f == 0:
                                link(ins)
                            else:
                                ins.then_inc(s_ang, 1)
                        l0, l1 = vec_lb[:, 0, :], vec_lb[:, 1, :]
                        m, e = col("lb.m", 4), col("lb.e", 8)
                        link(v.tensor_tensor(m, l0, l1, ALU.max))
                        v.tensor_tensor(e[:, 0:4], l0, m, ALU.subtract)
                        v.tensor_tensor(e[:, 4:8], l1, m, ALU.subtract).then_inc(s_lb, 1)
                        lam = vec[:, V_LAM:V_LAM + 8]
                        na = col("sp.na", 8)
                        link(v.tensor_scalar(na, lam, -1.0, None, ALU.mult))
                        v.tensor_tensor(na, na, lam, ALU.min).then_inc(s_sp, 1)
                elif kind == "proj":
                    _, name, l, j, _ = step
                    job = job_of(name, l, j)
                    if name in ("q", "k"):
                        if name == "q" and j == 0:
                            dve.wait_ge(s_trig, 1)
                        cs = at(A_ROPE, 2, S)
                        C = cs[:, None, 0, :].broadcast_to([P, 2, S])
                        Sn = cs[:, None, 1, :].broadcast_to([P, 2, S])
                        tmp = at(A_SC1, 4, S)
                        dst = at(A_Q1 if name == "q" else A_K1, 2, 2, S)
                        bank = bank2(wait_filled(dve, job))
                        v.tensor_tensor(tmp[:, 0:2, :], bank, C, ALU.mult)
                        drains(v.tensor_tensor(tmp[:, 2:4, :], bank, Sn, ALU.mult), job)
                        wait_drained(dve, job)
                        v.tensor_tensor(dst[:, j, 0, :], tmp[:, 0, :], tmp[:, 3, :], ALU.subtract)
                        ins = v.tensor_tensor(dst[:, j, 1, :], tmp[:, 2, :], tmp[:, 1, :], ALU.add)
                        if j == 1 and name == "k":
                            ins.then_inc(s_rope, 1)
                        else:
                            link(ins)
                    elif name == "wout":
                        gain = 1.0 if l is None else 0.5
                        hh = h[:, :, 256 * j:256 * j + 256]
                        drains(v.scalar_tensor_tensor(hh, bank2(wait_filled(dve, job)), gain, hh, ALU.mult, ALU.add), job)
                    elif name == "co":
                        for tt in range(TT):
                            hh = h[:, tt, 512 * j:512 * j + 512]
                            drains(v.tensor_tensor(hh, wait_filled(dve, f"{job}.{tt}")[:], hh, ALU.add), f"{job}.{tt}")
                    elif (name, j) in (("down", 15), ("wd", 10)):
                        for tt in range(TT):
                            for c in range(2):
                                job = job_of(name, l, f"{tt}{c}")
                                hh = h[:, tt, 512 * c:512 * c + 512]
                                drains(v.tensor_tensor(hh, wait_filled(dve, job)[:], hh, ALU.add), job)
                    elif (name, j) in (("down", 0), ("wd", 0)):
                        product_low(15 if name == "down" else product_of("gu", l, 21))
                    elif name == "up":
                        m = product_of(name, l, j)
                        dve.wait_ge(s_relu, m + 1)
                        drains(v.tensor_tensor(product[:, m % 2, :], wait_filled(dve, job)[:], product[:, m % 2, :], ALU.mult), job)
                        if j:
                            product_low(m - 1)
                    elif name == "gu" and j % 2:
                        m = product_of(name, l, j)
                        wait_drained(dve, job_of(name, l, j - 1))
                        bank = wait_filled(dve, job)
                        drains(v.tensor_tensor(product[:, m % 2, :], bank[:], product[:, m % 2, :], ALU.mult), job)
                        if j > 1:
                            product_low(m - 1)
                    elif name == "a" and j == 1:
                        za = at(A_ZA, TT, 512)
                        s3, rs, t = col(f"ss.a{l}", 3 * TT), col(f"rs.a{l}", 2 * TT), col("hn.t", 32)[:, 0:2 * TT]
                        for i in range(2):
                            wait_drained(dve, f"a{l}.{i}")
                        link(v.tensor_tensor(s3[:, TT:2 * TT], s3[:, 0:TT], s3[:, TT:2 * TT], ALU.add))
                        ss = s3[:, TT:3 * TT]
                        link(v.tensor_scalar(ss, ss, EPS, None, ALU.add))
                        rsqrt(ss, rs, t, 2 * TT)
                        for tt in range(TT):
                            v.tensor_scalar(za[:, tt, 0:384], za[:, tt, 0:384], rs[:, tt:tt + 1], None, ALU.mult)
                            ins = v.tensor_scalar(za[:, tt, 384:512], za[:, tt, 384:512], rs[:, TT + tt:TT + tt + 1], None, ALU.mult)
                        ins.then_inc(s_tok, 1)
                        if l == 0:
                            dve.wait_ge(s_lbe, 1)
                            e, sm, p = col("lb.x", 8), col("lb.s", 4), col("lb.p", 8)
                            link(v.tensor_tensor(sm, e[:, 0:4], e[:, 4:8], ALU.add))
                            link(v.reciprocal(sm, sm))
                            v.tensor_tensor(p[:, 0:4], e[:, 0:4], sm, ALU.mult)
                            link(v.tensor_tensor(p[:, 4:8], e[:, 4:8], sm, ALU.mult))
                            lb, om = col("lb.lb", 8), col("lb.om", 8)
                            v.tensor_tensor(lb[:, 0:4], p[:, 0:4], p[:, 0:4], ALU.subtract)
                            link(v.tensor_tensor(sm, p[:, 0:4], p[:, 4:8], ALU.add))
                            link(v.tensor_tensor(lb[:, 4:8], sm, p[:, 0:4], ALU.subtract))
                            link(v.tensor_scalar(om, lb, -1.0, 1.0, ALU.mult, ALU.add))
                            dve.wait_ge(s_row, 16)
                            for ll in range(L2):
                                r0 = R_LAYER + ll * R_PER + R_LQ
                                lq = row[:, r0:r0 + 128].rearrange("p (a d) -> p a d", a=4)
                                prod = scratch_xs[:, 0:64].rearrange("p (a d) -> p a d", a=2)
                                link(v.tensor_tensor(prod, lq[:, 0:2, :], lq[:, 2:4, :], ALU.mult))
                                ins = v.tensor_reduce(col(f"lam.d{ll}", 2), prod, AX_X, ALU.add)
                                ins.then_inc(s_lam, 1)
                                dve.wait_ge(s_lam, ll + 1)
                    elif name == "b" and j == 1:
                        zb = at(A_ZB, TT, 16, 32)
                        for i in range(2):
                            wait_drained(dve, f"b{l}.{i}")
                        rs = heads_norm(zb, 32, 32, scratch_xs)
                        link(v.tensor_tensor(zb, zb, rs.rearrange("p (a g) -> p a g", a=TT)[:, :, :, None].broadcast_to([P, TT, 16, 32]), ALU.mult))
                        r0 = R_LAYER + l * R_PER + R_DQN
                        g = row[:, r0:r0 + 64].rearrange("p (a d) -> p a d", a=2)[:, :, None, :].broadcast_to([P, 2, 8, 32])
                        for tt in range(TT):
                            z4 = zb[:, tt, :, :].rearrange("p (a g) d -> p a g d", a=2)
                            ins = v.tensor_tensor(z4, z4, g, ALU.mult)
                        link(ins)
                        rope32(zb[:, :, :, 0:16], zb[:, :, :, 16:32], 16).then_inc(s_tok, 1)
                    elif name == "f" and j == 1:
                        kk, F = at(A_KK, 4, S), at(A_F, 4, S)
                        E = at(A_E, 4, S + 1)
                        lb, om = col("lb.lb", 8), col("lb.om", 8)
                        for i in range(2):
                            wait_drained(dve, f"f{l}.{i}")
                        for hd in range(4):
                            c = 4 * l + hd
                            ins = v.tensor_scalar(kk[:, hd, :], kk[:, hd, :], om[:, c:c + 1], lb[:, c:c + 1], ALU.mult, ALU.add)
                        link(ins)
                        v.tensor_scalar(F, kk, 2.0 ** -63, None, ALU.max).then_inc(s_f, 1)
                        v.tensor_scalar(kk, kk, -1.0, 1.0, ALU.mult, ALU.add).then_inc(s_hkk, 1)
                        v.memset(E[:, :, 0:1], 0.0)
                        ones = scratch_xs[:, 0:S]
                        dve.wait_ge(s_tok, side_order.index((l, "z")) + 1)
                        link(v.memset(ones, 1.0))
                        dve.wait_ge(s_lf, l + 1)
                        for hd in range(4):
                            ins = v.tensor_tensor_scan(E[:, hd, 1:S + 1], ones, F[:, hd, :], 0.0, ALU.mult, ALU.add)
                        link(ins)
                        v.tensor_copy(F[0:64, :, :], E[0:64, :, 1:S + 1])
                        link(v.tensor_copy(F[64:128, :, :], E[64:128, :, 0:S]))
                elif kind == "znorm":
                    l = step[1]
                    z = at(A_Z, TT, 8, 96)
                    wait_drained(dve, f"krt{l}")
                    for tt in range(TT):
                        for n in ("uq", "ukv"):
                            wait_drained(dve, f"{n}{l}.{tt}")
                    dve.wait_ge(s_tok, side_order.index((l, "b")) + 1)
                    rs = heads_norm(z, 16, 96, scratch_xs)
                    link(v.tensor_tensor(z, z, rs.rearrange("p (a g) -> p a g", a=TT)[:, :, :, None].broadcast_to([P, TT, 8, 96]), ALU.mult))
                    r0 = R_LAYER + l * R_PER + R_QN
                    g = row[:, r0:r0 + 192].rearrange("p (a d) -> p a d", a=2)[:, :, None, :].broadcast_to([P, 2, 4, 96])
                    for tt in range(TT):
                        z4 = z[:, tt, :, :].rearrange("p (a g) d -> p a g d", a=2)
                        ins = v.tensor_tensor(z4, z4, g, ALU.mult)
                    link(ins)
                    rope32(z[:, :, :, 64:80], z[:, :, :, 80:96], 8).then_inc(s_tok, 1)
                elif kind == "mix":
                    k = 4 * step[1]
                    dve.wait_ge(s_xhi, 2 - step[1])
                    v.tensor_tensor(x_lo[:, k:k + 4, :], oT[:, k:k + 4, :], x_hi[:, k:k + 4, :].bitcast(F32), ALU.subtract).then_inc(s_xlo, 1)
                elif kind == "conv":
                    for j in range(2):
                        wait_drained(dve, f"u.{j}")
                    dve.wait_ge(s_zero1, 1)
                    up, uc = at(A_U, 4, UPAD), at(A_UC, 4, S)
                    cw = vec[:, V_CONVW:V_CONVW + 16]
                    for tap in range(4):
                        for ct in range(4):
                            w = cw[:, 4 * ct + tap:4 * ct + tap + 1]
                            src = up[:, ct, tap:tap + S]
                            if tap == 0:
                                ins = v.tensor_scalar(uc[:, ct, :], src, w, vec[:, V_CONVB + ct:V_CONVB + ct + 1], ALU.mult, ALU.add)
                            else:
                                ins = v.scalar_tensor_tensor(uc[:, ct, :], src, w, uc[:, ct, :], ALU.mult, ALU.add)
                        if tap < 3:
                            link(ins)
                        else:
                            ins.then_inc(s_conv, 1)
                elif kind == "rg1":
                    dve.wait_ge(s_spe, 1)
                    x, s1, s2, acc = col("sp.x", 8), col("sp.s", 8), col("sp.s2", 8), col("sp.acc", 8)
                    link(v.tensor_scalar(s1, x, 2.0, None, ALU.add))
                    link(v.reciprocal(s1, s1))
                    link(v.tensor_tensor(s1, s1, x, ALU.mult))
                    link(v.tensor_tensor(s2, s1, s1, ALU.mult))
                    link(v.memset(acc, 1.0 / 19.0))
                    for n in range(17, 0, -2):
                        link(v.tensor_tensor(acc, acc, s2, ALU.mult))
                        link(v.tensor_scalar(acc, acc, 1.0 / n, None, ALU.add))
                    link(v.tensor_tensor(acc, acc, s1, ALU.mult))
                    link(v.tensor_scalar(s2, vec[:, V_LAM:V_LAM + 8], -1.0, 0.0, ALU.mult, ALU.max))
                    link(v.tensor_scalar(s2, s2, RG_C, None, ALU.mult))
                    link(v.scalar_tensor_tensor(acc, acc, 2.0 * RG_C, s2, ALU.mult, ALU.add))
                    r = at(A_RG_R, 8, S)
                    wait_drained(dve, "rg.13")
                    v.tensor_tensor(r, r, acc[:, :, None].broadcast_to([P, 8, S]), ALU.mult).then_inc(s_rgy, 1)
                    ii = at(A_RG_I, 2, 4, S)
                    uc = at(A_UC, 4, S)
                    for z in range(2):
                        link(v.tensor_tensor(ii[:, z], ii[:, z], uc, ALU.mult))
                    dve.wait_ge(s_rgta, 1)
                    r, t, a = at(A_RG_R, 2048), at(A_RG_T, 2048), at(A_RG_A, 2048)
                    link(v.tensor_tensor(r, a, a, ALU.mult))
                    v.scalar_tensor_tensor(t, r, 1.0, t, ALU.add, ALU.mult).then_inc(s_rgw2, 1)
                elif kind == "rg2":
                    t, ii = at(A_RG_T, 2048), at(A_RG_I, 2048)
                    dve.wait_ge(s_rgs, 1)
                    link(v.tensor_tensor(ii, ii, t, ALU.mult))
                    a4, b4, h4 = at(A_RG_A, 2, 4, S), at(A_RG_I, 2, 4, S), at(A_RG_R, 2, 4, S)
                    for ct in range(4):
                        v.tensor_tensor_scan(h4[:, 0, ct, :], a4[:, 0, ct, :], b4[:, 0, ct, :], 0.0, ALU.mult, ALU.add)
                        ins = v.tensor_tensor_scan(h4[:, 1, ct, ::-1], a4[:, 1, ct, ::-1], b4[:, 1, ct, ::-1], 0.0, ALU.mult, ALU.add)
                    link(ins)
                    link(v.tensor_tensor(h4[:, 0], h4[:, 0], h4[:, 1], ALU.add))
                    v.tensor_tensor(oT[:, 4:8, :], h4[:, 0], at(A_YG, 4, S), ALU.mult).then_inc(s_rec, 1)
                elif kind == "score":
                    phase, hd = step[1:]
                    n, a0, count = ATT[phase, hd]
                    scale = {"dil": 64.0 ** -0.5, "cro": 128.0 ** -0.5, "mla": 96.0 ** -0.5, "dif": 32.0 ** -0.5}[phase[:3]]
                    if phase[:4] == "diff" and hd == 0:
                        l = int(phase[4])
                        dve.wait_ge(s_lame, l + 1)
                        e, nl = col(f"lam.e{l}", 2), col(f"lam.n{l}", 1)
                        link(v.tensor_tensor(nl, e[:, 1:2], e[:, 0:1], ALU.subtract))
                        link(v.tensor_scalar(nl, nl, LAMBDA_INIT[l], None, ALU.subtract))
                    for j in range(count):
                        a = a0 + j
                        bank = bank2(wait_filled(dve, f"score{a}"))
                        nm = col(f"nmax{a % 16}", TT)
                        if phase == "dil":
                            if a >= 4:
                                wait_filled(dve, f"turn{ATT[HEAD_OF_UNIT[a - 4]][0]}")
                            sc = at(A_SC1 + 512 * (a % 4), TT, S)
                            drains(v.scalar_tensor_tensor(sc, bank, scale, logc, ALU.mult, ALU.add), f"score{a}")
                            wait_drained(dve, f"score{a}")
                            v.tensor_reduce(nm, sc, AX_X, ALU.max, negate=True).then_inc(s_max, 1)
                        else:
                            mx = col(f"max{a % 4}", TT)
                            link(v.tensor_reduce(mx, bank, AX_X, ALU.max, negate=True))
                            v.tensor_scalar(nm, mx, scale, None, ALU.mult).then_inc(s_max, 1)
                elif kind == "prob":
                    phase, hd = step[1:]
                    n, a0, count = ATT[phase, hd]
                    base = A_SC1 if phase in ("dil", "cross") else A_SC
                    for j in range(count):
                        a = a0 + j
                        if phase == "dil":
                            dve.wait_ge(s_exp, a + 1)
                        else:
                            wait_drained(dve, f"score{a}")
                        ins = v.reciprocal(col(f"rsum{a % 16}", TT), col(f"sum{a % 16}", TT))
                    link(ins)
                    p0 = at(base + 512 * (a0 % 4), TT, S)
                    rs = col(f"rsum{a0 % 16}", TT)
                    if count == 1:
                        v.tensor_scalar(p0[:, 0, :], p0[:, 0, :], rs[:, 0:1], None, ALU.mult)
                        v.tensor_scalar(p0[:, 1, :], p0[:, 1, :], rs[:, 1:2], None, ALU.mult).then_inc(s_prob, 1)
                    else:
                        p1 = at(base + 512 * ((a0 + 1) % 4), TT, S)
                        rs1 = col(f"rsum{(a0 + 1) % 16}", TT)
                        v.tensor_scalar(rs1, rs1, col(f"lam.n{phase[4]}", 1), None, ALU.mult)
                        v.tensor_scalar(p0[:, 0, :], p0[:, 0, :], rs[:, 0:1], None, ALU.mult)
                        link(v.tensor_scalar(p0[:, 1, :], p0[:, 1, :], rs[:, 1:2], None, ALU.mult))
                        v.scalar_tensor_tensor(p0[:, 0, :], p1[:, 0, :], rs1[:, 0:1], p0[:, 0, :], ALU.mult, ALU.add)
                        v.scalar_tensor_tensor(p0[:, 1, :], p1[:, 1, :], rs1[:, 1:2], p0[:, 1, :], ALU.mult, ALU.add).then_inc(s_prob, 1)
                elif kind in ("diffnorm", "hval"):
                    l = step[1]
                    if kind == "diffnorm":
                        o = at(A_DO, TT, 4, 64)
                        for hd in range(4):
                            wait_drained(dve, f"value.diff{l}{hd}")
                        factor, g0 = 1.0 - LAMBDA_INIT[l], R_SUB
                    else:
                        o = at(A_HO, TT, 4, 64)
                        for hp in range(2):
                            wait_drained(dve, f"hval{l}.{hp}")
                        factor, g0 = 0.5, R_ON
                    rs = heads_norm(o, 8, 64, at(A_SCR, 512))
                    link(v.tensor_scalar(rs, rs, factor, None, ALU.mult))
                    link(v.tensor_tensor(o, o, rs.rearrange("p (a g) -> p a g", a=TT)[:, :, :, None].broadcast_to([P, TT, 4, 64]), ALU.mult))
                    r0 = R_LAYER + l * R_PER + g0
                    g = row[:, r0:r0 + 64][:, None, None, :].broadcast_to([P, TT, 4, 64])
                    ins = v.tensor_tensor(o, o, g, ALU.mult)
                    if kind == "hval":
                        link(ins)
                        ins = v.scalar_tensor_tensor(at(A_HO, 512), at(A_SG, 512), 1.0, at(A_HO, 512), ALU.add, ALU.mult)
                    ins.then_inc(s_tok, 1)
                elif kind == "decay":
                    _, l, i, hp = step
                    if i == 0 and hp == 0:
                        wait_filled(dve, f"value.mla{l}1")
                        wait_drained(dve, f"e{l}.1")
                    level_decay(l, i, hp)
                elif kind == "query":
                    level_query(*step[1:])
                elif kind == "level":
                    level_place(*step[1:])
                elif kind == "merge":
                    _, l, br, _ = step
                    gate = at(A_GATE, 16, S)
                    tmp = junk[:].bitcast(F32)[:, 0:512].rearrange("p (a t) -> p a t", a=2)
                    for j in range(4):
                        job = f"merge{l}.{br}{j}"
                        k = (8 * br + 2 * j) % 16
                        g = (8 * br + 2 * j) // 4
                        wait_drained(dve, f"gate{l}.{g}{(8 * br + 2 * j) // 2 % 2}")
                        bank = bank2(wait_filled(dve, job))
                        gk, mk = gate[:, k:k + 2, :], merged[:, 2 * j:2 * j + 2, :]
                        if br == 0:
                            drains(v.scalar_tensor_tensor(mk, gk, 1.0, bank, ALU.add, ALU.mult), job)
                        else:
                            drains(v.scalar_tensor_tensor(tmp, gk, 1.0, bank, ALU.add, ALU.mult), job)
                            wait_drained(dve, job)
                            ins = v.tensor_tensor(mk, mk, tmp, ALU.add)
                            if br == 3:
                                ins.then_inc(s_msum, 1)
                                dve.wait_ge(s_msum, 4 * l + j + 1)
                                if j:
                                    merged_low(l, j - 1)
                            elif j == 3 and br == 1:
                                ins.then_inc(s_merged, 1)
                                dve.wait_ge(s_merged, l + 1)
                            else:
                                link(ins)
                    if br == 3:
                        merged_low(l, 3)




def constants():
    c = np.zeros((P, C_SIZE), np.float64)
    p = np.arange(P)
    c[:, C_IDENT:C_IDENT + P] = np.eye(P)
    i, j = np.arange(S)[:, None], np.arange(S)[None, :]
    count = np.zeros((S, S))
    for window, dil in ((128, 1), (512, 4), (2048, 16)):
        count += ((i - j) % dil == 0) & (np.abs(i - j) // dil <= window // (2 * dil))
    logc = np.where(count > 0, np.log(np.maximum(count, 1)), -1e30)
    c[:, C_LOGC:C_LOGC + TT * S] = logc.reshape(TT, P, S).transpose(1, 0, 2).reshape(P, -1)
    c[:, C_FREQ] = 10000.0 ** (-(p % 32) / 32.0)
    ang = np.arange(S)[:, None] / 10000.0 ** (np.arange(0, 32, 2) / 32.0)[None, :]
    for off, f in ((C_COS, np.cos), (C_SIN, np.sin)):
        c[:, off:off + TT * 16] = f(ang).reshape(TT, P, 16).transpose(1, 0, 2).reshape(P, -1)
    d = np.arange(64)
    ph = 2 * np.pi * d[:, None] * d[None, :] / 64
    for g in range(2):
        c[64 * g:64 * g + 64, C_DFTD + 64 * g:C_DFTD + 64 * g + 64] = np.cos(ph) / 8.0
        c[64 * g:64 * g + 64, C_DFTD + P + 64 * g:C_DFTD + P + 64 * g + 64] = np.sin(ph) / 8.0
    ph = 2 * np.pi * ((i * j) % S) / S
    c[:, C_DFTC:C_DFTC + TT * S] = (np.cos(ph) / 16.0).reshape(TT, P, S).transpose(1, 0, 2).reshape(P, -1)
    c[:, C_DFTS:C_DFTS + TT * S] = (-np.sin(ph) / 16.0).reshape(TT, P, S).transpose(1, 0, 2).reshape(P, -1)
    for n, half in enumerate(MASKED):
        same = p[:, None] // (2 * half) == p[None, :] // (2 * half) if half else np.eye(P, dtype=bool)
        c[:, C_MASK + n * P:C_MASK + (n + 1) * P] = same
    return c.astype(np.float32)




def fold(w):
    k = w.shape[0] // P
    return w.reshape(k, P, -1).transpose(1, 0, 2).reshape(P, -1)


def pack_pieces(a):
    pieces = []

    def put(*parts):
        parts = [fold(p) for p in parts]
        n = sum(p.shape[1] for p in parts)
        pieces.append(np.concatenate(parts + ([np.zeros((P, PIECE - n), np.float32)] if n < PIECE else []), axis=1))

    def columns(w, n=256):
        for c in range(0, w.shape[1], n):
            put(w[:, c:c + n])

    def rows(w, n=256):
        for r in range(0, w.shape[0], n):
            put(w[r:r + n])

    w = a["w_in"][0]
    halves = np.concatenate([np.concatenate([64 * hd + 32 * f + np.arange(32) for hd in range(4 * g, 4 * g + 4)]) for g in range(2) for f in range(2)])
    columns(w[:, halves])
    columns(w[:, 512 + halves])
    columns(w[:, 1024:2560])
    columns(a["w_ck"][0])
    columns(a["w_cv"][0])
    columns(a["w_out"][0])
    columns(a["w_cq"][0])
    columns(a["w_co"][0], 512)
    columns(a["w_mlp_in"][0])
    rows(a["w_mlp_out"][0])
    for l in range(L2):
        w = a["w_in_2"][l]
        o = np.cumsum([0, 384, 128, 32, 256, 256, 256, 256, 256, 256, 256, 256, 256, 4096])
        c_q, c_kv, k_rope, fnet, dq, dk, dv, hq, hi, hff, hfb, hg, gate = (w[:, o[i]:o[i + 1]] for i in range(13))
        columns(np.concatenate([c_q, c_kv, dq, dk, hg], 1))
        ukv = a["mla_w_ukv_2"][l].reshape(P, 4, 2, 64).transpose(0, 2, 1, 3).reshape(P, 512)
        put(k_rope, a["mla_w_uq_2"][l], ukv)
        columns(np.concatenate([dv, hi], 1))
        columns(np.stack([hff.reshape(D, 4, 64), hfb.reshape(D, 4, 64)], 2).reshape(D, 512))
        columns(np.concatenate([fnet, hq], 1))
        br = a["w_branch_2"][l]
        columns(gate[:, 0:2048])
        put(br[0])
        put(br[1])
        columns(gate[:, 2048:4096])
        put(br[2])
        put(br[3])
        columns(a["w_out_2"][l])
        gu = a["w_gate_up_2"][l].reshape(D, 2, 11, 256).transpose(0, 2, 1, 3).reshape(D, -1)
        columns(gu)
        rows(a["w_down_2"][l])
    return np.ascontiguousarray(np.stack(pieces))


def pack_vectors(a):
    gains = [a[n][0] for n in GAINS[:4]] + [a["ln_mix_2"][l] for l in range(L2)] + [a["ln_ffn_2"][l] for l in range(L2)]
    parts = [g.reshape(KT, P).T for g in gains]
    parts.append(a["conv_w"][0].reshape(4, 4, P).transpose(2, 1, 0).reshape(P, 16))
    parts.append(a["conv_b"][0].reshape(4, P).T)
    ab, xb = (a[n][0].reshape(2, 4, P).transpose(2, 0, 1) for n in ("rg_a_b", "rg_x_b"))
    parts.append(np.stack([ab, xb], 3).reshape(P, 16))
    parts.append(a["rg_lambda"][0].reshape(2, 4, P).transpose(2, 0, 1).reshape(P, 8))
    for l in range(L2):
        parts.append(a["mla_g_qa_2"][l].reshape(3, P).T)
        parts.append(a["mla_g_kva_2"][l].reshape(P, 1))
    lb = a["hgrn_lb_logits_2"].reshape(2, L2, 4, 64).transpose(0, 3, 1, 2).reshape(P, L2 * 4)
    parts.append(lb)
    out = np.ascontiguousarray(np.concatenate(parts, 1))
    assert out.shape == (P, V_SIZE), out.shape
    return out


def pack_rows(a):
    r = [a["norm_final_g"]]
    for l in range(L2):
        r += [a[n + "_2"][l] for n in ("mla_g_qn", "mla_g_kn", "diff_g_qn", "diff_g_kn", "diff_g_sub", "hgrn_g_on",
                                       "diff_lq1", "diff_lq2", "diff_lk1", "diff_lk2")]
    r = np.concatenate(r)
    assert r.shape == (R_SIZE,)
    return np.ascontiguousarray(np.broadcast_to(r, (P, R_SIZE)))


def pack_rg(a):
    out = np.zeros((P, 2, 4, 2, P), np.float32)
    for ax, n in enumerate(("rg_a_w", "rg_x_w")):
        w = a[n][0]
        for z in range(2):
            for g in range(8):
                p0 = 64 * (g % 2)
                out[p0:p0 + 64, z, g // 2, ax, p0:p0 + 64] = w[z, g]
    return out.reshape(P, 16 * P)


def kernel(**inputs):
    import concourse.bacc as bacc
    from concourse.bass_utils import run_bass_kernel_spmd

    a = {n: np.asarray(x) for n, x in inputs.items()}
    arrays = {
        "x": np.ascontiguousarray(a["x"][0]),
        "mem": np.ascontiguousarray(a["mem"][0]),
        "positions": np.ascontiguousarray(np.broadcast_to(a["positions"][0], (P, S))),
        "constants": constants(),
        "vectors": pack_vectors(a),
        "rows": pack_rows(a),
        "rg_weights": pack_rg(a),
        "weight_pieces": pack_pieces(a),
    }
    nc = bacc.Bacc("TRN2", target_bir_lowering=False, num_devices=1)
    args = [nc.dram_tensor(n, v.shape, mybir.dt.from_np(v.dtype), kind="ExternalInput").ap() for n, v in arrays.items()]
    args.append(nc.dram_tensor("out", (S, D), F32, kind="ExternalOutput").ap())
    build(nc, *args)
    r = run_bass_kernel_spmd(nc, [arrays], core_ids=[0])
    return r.results[0]["out"].reshape(1, S, D)
```

```python
from contextlib import ExitStack

import numpy as np
import concourse.bass as bass
from concourse import mybir

ALU = mybir.AluOpType
ACT = mybir.ActivationFunctionType
F32 = mybir.dt.float32
F32R = mybir.dt.float32r
BF16 = mybir.dt.bfloat16
I32 = mybir.dt.int32
AX_X = mybir.AxisListType.X

P = 128
D = 1024
S = 256
TT = S // P
KT = D // P
L2 = 2
EPS = 1e-6
PIECE = 2048
RING = 3
SPLITS = 2
RG_C = 8.0
LEVELS = (128, 64, 32, 16, 8, 4, 2, 1)
MASKED = (32, 16, 8, 4, 2, 1, 0)
N_PIECES_1 = 54
N_PIECES_2 = 69
NP = N_PIECES_1 + L2 * N_PIECES_2
LAMBDA_INIT = [0.8 - 0.6 * float(np.exp(-0.3 * l)) for l in range(L2)]
RSQRT_MAGIC = 0x5F3759DF
TWO_PI_HI = 6.28125
TWO_PI_MID = 0.0019350051879882812
TWO_PI_LO = 2.0 * np.pi - TWO_PI_HI - TWO_PI_MID
ROUND = 1.5 * 2.0 ** 23

C_IDENT = 0
C_FREQ = C_IDENT + P
C_LOGC = C_FREQ + 1
C_COS = C_LOGC + TT * S
C_SIN = C_COS + TT * 16
C_DFTD = C_SIN + TT * 16 + 1
C_DFTC = C_DFTD + 2 * P
C_DFTS = C_DFTC + TT * S
C_MASK = C_DFTS + TT * S
C_SIZE = C_MASK + len(MASKED) * P

GAINS = ("norm_mix_g", "norm_cross_g", "norm_mem_g", "norm_mlp_g", "ln_mix_0", "ln_mix_1", "ln_ffn_0", "ln_ffn_1", "norm_final_g")
V_GAIN = 0
V_CONVW = V_GAIN + len(GAINS) * KT
V_CONVB = V_CONVW + 16
V_RGB = V_CONVB + 4
V_LAM = V_RGB + 16
V_QA = V_LAM + 8
V_LB = V_QA + 4 * L2
V_SIZE = V_LB + 4 * L2

R_FINAL = 0
R_LAYER = D
R_QN, R_DQN, R_SUB, R_ON, R_LQ = 0, 192, 256, 320, 384
R_PER = 512
R_SIZE = R_LAYER + L2 * R_PER

A_HID_HI, A_HID_LO = 0, 8192
A_PROD = 16384
A_RG_R, A_RG_I, A_RG_T, A_RG_A = 0, 2048, 4096, 6144
A_MEM = 0
A_Q1 = 8192
A_K1 = A_Q1 + 1024
A_V1 = A_K1 + 1024
A_CQ = A_K1
A_CO = A_Q1
A_U = A_V1 + 1024
UPAD = S + 3
A_UC = A_U + 4 * UPAD
A_YG = A_UC + 1024
A_RGW = A_YG + 1024
A_ROPE = A_RGW + 16 * P
A_CK = A_ROPE
A_CV = A_ROPE + 1024
A_SC1 = A_ROPE + 2048
A_GATE = 0
A_FT, A_AB = 0, 512
A_VC = 4096
A_SG = A_VC + 1024
A_HO = A_SG + 512
A_DO = A_HO + 512
A_HQ = A_DO + 512
A_KK = A_HQ + 1024
A_E = A_KK + 1024
A_F = A_E + 4 * (S + 1)
A_ZB = A_F + 1024
A_DT = A_ZB + 1024
A_SC = A_DT + 1024
A_VM = A_SC + 6 * 512
A_ZA = A_VM + 512
A_CT = A_ZA + 1024
A_Z = A_CT + 1024
A_QKT = A_Z + 1536
A_ST = A_ZA
A_X = A_ST + 2048
A_KL = A_ZB
A_QL = A_SC
A_SCR = A_SC + 2048
A_KR = 0
ARENA = A_QKT + 2048
assert A_X + 2048 <= ARENA and A_SC1 + 6 * 512 <= ARENA



def attention_plan():
    heads = [("dil", h, 1) for h in range(8)] + [("cross", h, 1) for h in range(4)]
    for l in range(L2):
        heads += [(f"mla{l}", h, 1) for h in range(4)]
        heads += [(f"diff{l}", h, 2) for h in range(4)]
    plan, unit = {}, 0
    for n, (phase, h, k) in enumerate(heads):
        plan[phase, h] = (n, unit, k)
        unit += k
    return heads, plan


HEADS, ATT = attention_plan()
EVEN = {n: sum(1 for m in HEADS[:n + 1] if m[0][:3] in ("dil", "mla") and m[1] % 2 == 0) for n in range(len(HEADS))}
HEAD_OF_UNIT = [(phase, h) for phase, h, k in HEADS for _ in range(k)]


def build(nc, x_d, mem_d, pos_d, const_d, vec_d, row_d, rgw_d, pieces_d, out_d):
    with ExitStack() as ctx:
        def sb(name, shape, dt=F32):
            return ctx.enter_context(nc.sbuf_tensor(name, shape, dt))

        def sem(name):
            return ctx.enter_context(nc.semaphore(name))

        ring = sb("ring", [P, RING, PIECE])
        w_hi = sb("w_hi", [P, SPLITS, PIECE], F32R)
        w_lo = sb("w_lo", [P, SPLITS, PIECE], F32R)
        const = sb("const", [P, C_SIZE])
        vec = sb("vec", [P, V_SIZE])
        row = sb("row", [P, R_SIZE])
        h = sb("h", [P, TT, D])
        xs = sb("xs", [P, TT, D])
        x_hi = sb("x_hi", [P, KT, S], F32R)
        x_lo = sb("x_lo", [P, KT, S], F32R)
        oT = sb("oT", [P, KT, S])
        W = sb("W", [P, ARENA])
        arena0 = nc.sbuf_base - 4 * ARENA
        hid_hi = nc.alloc_sbuf_tensor_at("hid_hi", [P, 32, S], F32R, offset=arena0 + 4 * A_HID_HI)
        hid_lo = nc.alloc_sbuf_tensor_at("hid_lo", [P, 32, S], F32R, offset=arena0 + 4 * A_HID_LO)
        junk = sb("junk", [P, D], BF16)
        stat = sb("stat", [P, 448])
        rrow = sb("rrow", [P, S])
        psum = [ctx.enter_context(nc.psum_tensor(f"bank{b}", [P, 512], F32)) for b in range(8)]

        def at(off, *dims):
            n = int(np.prod(dims))
            v = W[:, off:off + n]
            if len(dims) == 1:
                return v
            names = "abcd"[:len(dims)]
            return v.rearrange(f"p ({' '.join(names)}) -> p {' '.join(names)}", **dict(zip(names[1:], dims[1:])))

        merged = xs[:].rearrange("p a b -> p (a b)").rearrange("p (k t) -> p k t", k=KT)
        product = at(A_PROD, 2, 512)
        ident = const[:, C_IDENT:C_IDENT + P]
        logc = const[:, C_LOGC:C_LOGC + TT * S].rearrange("p (a k) -> p a k", a=TT)
        vec_lb = vec[:, V_LB:V_LB + 4 * L2].rearrange("p (l h) -> p l h", l=L2)

        cols = {}

        def col(name, n):
            if name not in cols:
                at0 = sum(k for _, k in cols.values())
                assert at0 + n <= 448, at0
                cols[name] = (at0, n)
            at0, n = cols[name]
            return stat[:, at0:at0 + n]

        s_ident = sem("identity_loaded")
        s_x = [sem(f"x_loaded{tt}") for tt in range(TT)]
        s_mem, s_pos, s_const, s_vec, s_row, s_rgw = (sem(n) for n in (
            "mem_loaded", "positions_loaded", "const_loaded", "vec_loaded", "row_loaded", "rgw_loaded"))
        piece_loaded = [sem(f"piece_loaded{i}") for i in range(RING)]
        s_weight_high, s_weight_low, s_weight_low_pool = sem("weights_high"), sem("weights_low"), sem("weights_low_pool")
        s_norm_high, s_norm_high_dve = sem("norm_high"), sem("norm_high_dve")
        s_sig, s_gate, s_silu = sem("sigmoid"), sem("gate_ready"), sem("silu")
        s_relu, s_hidden_high, s_hidden_low = sem("relu"), sem("hidden_high"), sem("hidden_low")
        s_mix_high, s_mix_low = sem("mix_high"), sem("mix_low")
        s_merged_sum, s_merged_high, s_merged_low = sem("merged_sum"), sem("merged_high"), sem("merged_low")
        filled = [sem(f"filled{b}") for b in range(8)]
        drained = [sem(f"drained{b}") for b in range(8)]
        jobs = {}
        uses = [0] * 8
        last_job = [None] * NP
        dve_link, act_link, pool_link = sem("dve_link"), sem("act_link"), sem("pool_link")
        s_sumsq, s_rs = sem("sumsq_ready"), sem("rstd_ready")
        s_max, s_exp, s_prob = sem("max_ready"), sem("exp_ready"), sem("prob_ready")
        s_conv, s_rec = sem("conv_ready"), sem("rec_ready")
        s_rg_exponent, s_rg_tanh_exp, s_rg_square, s_rg_root = sem("rg_exponent"), sem("rg_tanh_exp"), sem("rg_square"), sem("rg_root")
        s_softplus_in = sem("softplus_in")
        s_softplus_exp = sem("softplus_exp")
        s_angles, s_trig, s_rope = sem("angles_ready"), sem("cos_sin_ready"), sem("rope_done")
        s_even, s_read = sem("even_value_done"), sem("piece_read")
        s_token_side = sem("token_side_ready")
        s_bound_in, s_bound_exp, s_f, s_log_f, s_hgrn_k = (sem(n) for n in ("lb_in", "lb_exp", "f_ready", "log_f_ready", "hgrn_k_ready"))
        s_decay_log, s_decay, s_query, s_key = (sem(n) for n in ("decay_log", "decay", "level_queries", "level_keys"))
        s_lambda_in, s_lambda_exp = sem("lambda_in"), sem("lambda_exp")
        s_merged = sem("merged_ready")
        s_pads_zeroed = sem("pads_zeroed")
        s_h_normed, s_out = sem("h_normed"), sem("out_stored")

        def wait_filled(eng, name):
            b, use = jobs[name]
            eng.wait_ge(filled[b], use + 1)
            return psum[b]

        def wait_drained(eng, name):
            b, use = jobs[name]
            eng.wait_ge(drained[b], use + 1)

        def drains(ins, name):
            ins.then_inc(drained[jobs[name][0]], 1)

        def raw(p):
            return ring[:, p % RING, :]

        def wait_read(eng, p):
            if isinstance(last_job[p], int):
                eng.wait_ge(s_read, last_job[p])
            else:
                wait_filled(eng, last_job[p])

        steps = []
        split = []
        split_of = {}
        low = []
        s_low = {"dve": s_weight_low, "pool": s_weight_low_pool}

        def piece(n=PIECE, by="dve"):
            nonlocal pieces
            if n:
                split_of[pieces] = len(split)
                split.append((pieces, n))
                low.append((by, 1 + sum(b == by for b, _ in low)))
            pieces += 1
            return pieces - 1

        pieces = 0

        def proj(name, l=None, js=range(2), n=PIECE):
            by = "pool" if name in ("v", "u", "y", "ck", "cv", "b", "hg", "kr", "c", "e", "f") else "dve"
            return [("proj", name, l, j, piece(n, by)) for j in js]

        def wait_low(eng, q):
            by, n = low[q]
            eng.wait_ge(s_low[by], n)

        def attend(heads, filler=(), first=0, long=False):
            filler, count = list(filler), len(heads)
            for i in range(count + 3):
                turn = [("turn", *heads[i - 2])] if 2 <= i <= count + 1 else []
                if i < count:
                    steps.append(("score", *heads[i]))
                if long:
                    steps.extend(turn)
                if 1 <= i <= count:
                    steps.append(("prob", *heads[i - 1]))
                if filler and i >= first:
                    steps.append(filler.pop(0))
                if not long:
                    steps.extend(turn)
                if 3 <= i:
                    steps.append(("value", *heads[i - 3]))
            steps.extend(filler)

        steps.append(("setup",))
        steps.append(("norm", "norm_mix_g"))
        steps += proj("q") + proj("k")
        steps.append(("memscale",))
        steps += proj("v") + proj("u")
        steps.append(("conv",))
        steps += proj("y")
        steps.append(("norm", "norm_mem_g"))
        ck, cv = proj("ck"), proj("cv")
        steps += [ck[0], ("rggate", 0), ck[1], ("rggate", 1), ("softplus",), ("rgA",), cv[0], ("rgT",), ("rgB",), cv[1]]
        attend([("dil", n) for n in range(8)], [("rgS",)] + [("rgC", n) for n in range(4)] + [("mix", 1)])
        steps.append(("mix", 0))
        steps += proj("wout", js=range(4))
        steps.append(("norm", "norm_cross_g"))
        steps += proj("cq")
        attend([("cross", n) for n in range(4)])
        steps += proj("co", n=0)
        steps.append(("norm", "norm_mlp_g"))
        steps += proj("up", js=range(16))
        steps += proj("down", js=range(16))
        assert pieces == N_PIECES_1
        for l in range(L2):
            steps.append(("norm", f"ln_mix_{l}"))
            steps += proj("a", l) + proj("b", l)
            steps.append(("aturn", l))
            steps += proj("hg", l, (0,)) + proj("kr", l, (0,), KT * 32 + 96)
            c = proj("c", l)
            steps += [c[0], ("znorm", l), c[1]]
            steps.append(("bturn", l))
            steps += proj("f", l)
            steps.append(("zturn", l))
            e = proj("e", l)
            steps += [e[0], ("logf", l), e[1], ("fnet", l)]
            gates = [("gate", l, g, half, piece(by="pool" if g < 1 else "dve")) for g in range(4) for half in range(2)]
            attend([(f"mla{l}", n) for n in range(4)] + [(f"diff{l}", n) for n in range(4)], gates, 3, True)
            pairs = lambda kind, i: [(kind, l, i, hp) for hp in range(2)]
            steps += pairs("decay", 0)
            steps.append(("merge", l, 0, piece(0)))
            steps += pairs("query", 0) + pairs("decay", 1)
            steps.append(("merge", l, 1, piece(0)))
            steps += pairs("query", 1)
            gates = [("gate", l, g, half, piece()) for g in range(4, 8) for half in range(2)]
            for i in range(len(LEVELS) + 1):
                if i + 2 < len(LEVELS):
                    steps += pairs("decay", i + 2)
                steps += pairs("level", i)
                if i + 2 < len(LEVELS):
                    steps += pairs("query", i + 2)
                if i != 7 and len(gates) > 1:
                    steps.append(gates.pop(0))
                if i == 8:
                    steps += [("diffnorm", l)]
            steps.append(("hval", l))
            steps += gates
            steps.append(("diffout", l))
            steps.append(("merge", l, 2, piece(0)))
            steps.append(("hout", l))
            steps.append(("merge", l, 3, piece(0)))
            steps += proj("wout", l, range(4))
            steps.append(("norm", f"ln_ffn_{l}"))
            steps += proj("gu", l, range(22))
            steps += proj("wd", l, range(11))
        assert pieces == NP, pieces
        norms = [s[1] for s in steps if s[0] == "norm"]
        piece_after = {s[1]: next(t[-1] for t in steps[i:] if t[0] == "proj") for i, s in enumerate(steps) if s[0] == "norm"}
        stats = [n for s in steps if s[0] == "norm" for n in (["final"] if s[1] == "ln_mix_0" else []) + [s[1]]]

        side_order = [(l, what) for l in range(L2) for what in ("a", "b", "z", "do", "ho")]

        def norm_input(name):
            def drained_by(job):
                b, use = jobs[job]
                return drained[b], use + 1

            if name == "norm_mem_g":
                return [(0, tt, 0, D, s_mem, 16) for tt in range(TT)]
            if name == "norm_mix_g":
                return [(0, tt, 0, D, s_x[tt], 16) for tt in range(TT)]
            if name == "ln_mix_0":
                return [(0, tt, 0, D, s_h_normed, tt + 1) for tt in range(TT)]
            if name == "norm_mlp_g":
                return [(j, tt, 512 * j, 512, *drained_by(f"co.{j}.{tt}")) for j in range(2) for tt in range(TT)]
            if name in ("final", "ln_mix_1"):
                tag = "down" if name == "final" else "wd0"
                return [(c, tt, 512 * c, 512, *drained_by(f"{tag}.{tt}{c}")) for tt in range(TT) for c in range(2)]
            tag = {"norm_cross_g": "wout", "ln_ffn_0": "wout0", "ln_ffn_1": "wout1"}[name]
            return [(j, tt, 256 * j, 256, *drained_by(f"{tag}.{j}")) for j in range(4) for tt in range(TT)]

        def job_of(name, l, j):
            return f"{name}{'' if l is None else l}.{j}"

        def product_of(name, l, j):
            return j if name == "up" else 16 + 11 * l + j // 2

        block = ctx.enter_context(nc.Block())

        @block.tensor
        def _(pe):
            rot = {"g": 0, "m": 0}
            banks = {"g": (0, 1, 2), "m": (3, 4, 5, 6, 7)}

            def fill(name, group):
                if isinstance(group, int):
                    b = group
                else:
                    b = banks[group][rot[group] % len(banks[group])]
                    rot[group] += 1
                if uses[b]:
                    pe.wait_ge(drained[b], uses[b])
                jobs[name] = (b, uses[b])
                uses[b] += 1
                return psum[b]

            def full(ins, name):
                ins.then_inc(filled[jobs[name][0]], 1)

            reads = 0

            def loaded(p):
                pe.wait_ge(piece_loaded[p % RING], 16 * (p // RING + 1))
                return raw(p)

            def mm(out, lhsT, rhs, first, last):
                return nc.tensor.matmul(out, lhsT, rhs, start=first, stop=last)

            def gemm(job, group, p, form, n=256, parts=None):
                q = split_of[p]
                bank = fill(job, group)
                hi, lo = (w[:, q % SPLITS, 0:KT * n].rearrange("p (k c) -> p k c", k=KT) for w in (w_hi, w_lo))
                pe.wait_ge(s_weight_high, 2 * q + 1)
                passes = [(hi, x_hi), (hi, x_lo), (lo, x_hi)] if parts is None else [(hi, x_hi), (lo, x_hi), (hi, x_lo)]
                for half in range(2):
                    cut = slice(half * P, (half + 1) * P)
                    for i, (w, x) in enumerate(passes):
                        if half == 0 and w is lo:
                            wait_low(pe, q)
                        for k in range(KT):
                            if half == 0 and i != 1 and parts and k % 2 == 0:
                                pe.wait_ge(*parts(k // 2)[i // 2])
                            if half == i == 0 and k == KT // 2:
                                pe.wait_ge(s_weight_high, 2 * (q + 1))
                            lhsT, rhs = (w[:, k, cut], x[:, k, :]) if form == "feat" else (x[:, k, cut], w[:, k, :])
                            ins = mm(bank[:, half * 256:half * 256 + n], lhsT, rhs, i == k == 0, i == 2 and k == KT - 1)
                full(ins, job)
                last_job[p] = job

            def plain(name, group, src, w, kts, n, p=None):
                for tt in range(TT):
                    bank = fill(f"{name}.{tt}", group)
                    for i, k in enumerate(kts):
                        ins = mm(bank[:, 0:n], src[:, k, tt * P:(tt + 1) * P], w[:, i, :], i == 0, i == len(kts) - 1)
                    full(ins, f"{name}.{tt}")
                if p is not None:
                    last_job[p] = f"{name}.{TT - 1}"

            def turns(name, src, tiles, group="m"):
                for j in range(0, tiles, 2):
                    job = f"{name}.{j // 2}"
                    bank = fill(job, group)
                    for jj in range(min(2, tiles - j)):
                        for tt in range(TT):
                            piece = src(j + jj, tt)
                            ins = nc.tensor.transpose(bank[0:piece.shape[1], jj * S + tt * P:jj * S + (tt + 1) * P], piece, ident)
                    full(ins, job)

            def score_operands(phase, hd, j):
                if phase == "dil":
                    q, k = at(A_Q1, 2, 2, S), at(A_K1, 2, 2, S)
                    p0 = 32 * (hd % 4)
                    return [(lambda qt, f=f: q[p0:p0 + 32, hd // 4, f, qt * P:(qt + 1) * P], k[p0:p0 + 32, hd // 4, f, :]) for f in range(2)]
                if phase == "cross":
                    q, k = at(A_CQ, 4, S), at(A_CK, 4, S)
                    return [(lambda qt: q[:, hd, qt * P:(qt + 1) * P], k[:, hd, :])]
                if phase[:3] == "mla":
                    z = at(A_QKT, 8, S)
                    return [(lambda qt: z[0:96, hd, qt * P:(qt + 1) * P], z[0:96, 4 + hd, :])]
                z = at(A_DT, 4, S)
                hh = 2 * hd + j
                p0 = 32 * (hh % 4)
                return [(lambda qt: z[p0:p0 + 32, hh // 4, qt * P:(qt + 1) * P], z[p0:p0 + 32, 2 + hh // 4, :])]

            for step in steps:
                kind = step[0]
                if kind == "setup":
                    pe.wait_ge(s_ident, 16)
                elif kind == "norm":
                    name = step[1]
                    src = at(A_MEM, TT, D) if name == "norm_mem_g" else h
                    for j in range(KT // 2):
                        for _, tt, c0, n, s_in, value in norm_input("final" if name == "ln_mix_0" else name):
                            if c0 < 256 * (j + 1) and c0 + n > 256 * j:
                                pe.wait_ge(s_in, value)
                        turns(f"{name}.{j}", lambda k, tt: src[:, tt, (2 * j + k) * P:(2 * j + k + 1) * P], 2)
                elif kind == "proj":
                    _, name, l, j, p = step
                    job = job_of(name, l, j)
                    before = {"q": "norm_mix_g", "ck": "norm_mem_g", "cq": "norm_cross_g", "a": f"ln_mix_{l}", "up": "norm_mlp_g",
                              "gu": f"ln_ffn_{l}"}.get(name)
                    before = before if j == 0 else None
                    parts = None
                    if before:
                        def parts(i):
                            b, use = jobs[f"{before}.{i}.0"]
                            return ((s_norm_high, s_norm_high_dve)[i % 2], 2 * norms.index(before) + i // 2 + 1), (drained[b], use + 1)
                    elif name == "wout" and j == 0 and l is None:
                        def parts(i):
                            return (s_mix_high, 2), (s_mix_low, 2)
                    elif name == "wout" and j == 0:
                        def parts(i):
                            return (s_merged_high, 4 * l + i + 1), (s_merged_low, 4 * l + i + 1)
                    if name in ("q", "k", "u", "y", "ck", "cq", "e", "f"):
                        gemm(job, "g", p, "feat", parts=parts)
                    elif name in ("v", "cv", "wout", "a", "b", "c", "hg"):
                        gemm(job, "g", p, "tok", parts=parts)
                    elif name in ("up", "gu"):
                        gemm(job, "m", p, "feat", parts=parts)
                    elif name == "co":
                        if j == 0:
                            for hd in range(4):
                                wait_drained(pe, f"value.cross{hd}")
                        plain(job, "g", at(A_CO, 4, S), loaded(p).rearrange("p (k c) -> p k c", k=4), range(4), 512, p)
                    elif name == "kr":
                        q = split_of[p]
                        bank = fill(job, "g")
                        pe.wait_ge(s_weight_high, 2 * (q + 1))
                        wait_low(pe, q)
                        for i, (w, x) in enumerate(((w_hi, x_hi), (w_hi, x_lo), (w_lo, x_hi))):
                            for k in range(KT):
                                ins = mm(bank[:, 0:S], w[:, q % SPLITS, 32 * k:32 * k + P], x[:, k, :], i == k == 0, i == 2 and k == KT - 1)
                        full(ins, job)
                        w = loaded(p)
                        cT = at(A_CT, 4, S)
                        for i in range(2):
                            wait_drained(pe, f"aturn{l}.{i}")
                        plain(f"uq{l}", "m", cT, w[:, 256:256 + 1152].rearrange("p (k c) -> p k c", k=3), range(3), 384)
                        plain(f"ukv{l}", "m", cT, w[:, 1408:1920].rearrange("p (k c) -> p k c", k=1), [3], 512, p)
                        wait_drained(pe, job)
                        bank = fill(f"krt{l}", "g")
                        for tt in range(TT):
                            ins = nc.tensor.transpose(bank[:, 32 * tt:32 * tt + 32], at(A_KR, S)[0:32, tt * P:(tt + 1) * P], ident[0:32, 0:32])
                        full(ins, f"krt{l}")
                    elif name in ("down", "wd"):
                        tag = job_of(name, l, "")
                        count = 16 if name == "down" else 11
                        q = split_of[p]
                        hi, lo = (w[:, q % SPLITS, :].rearrange("p (k c) -> p k c", k=2) for w in (w_hi, w_lo))
                        if j == 0:
                            acc = {(tt, c): fill(f"{tag}{tt}{c}", 2 * tt + c) for tt in range(TT) for c in range(2)}
                        pe.wait_ge(s_hidden_low, (j if name == "down" else product_of("gu", l, 2 * j)) + 1)
                        pe.wait_ge(s_weight_high, 2 * (q + 1))
                        passes = ((hi, hid_hi), (hi, hid_lo), (lo, hid_hi))

                        def accumulate(tt, c, i):
                            w, x = passes[i]
                            for k in range(2):
                                ins = mm(acc[tt, c][:, :], x[:, 2 * j + k, tt * P:(tt + 1) * P], w[:, k, 512 * c:512 * c + 512],
                                         i == j == k == 0, i == 2 and k == 1 and j == count - 1)
                            return ins

                        if j < count - 1:
                            for i in range(3):
                                if i == 2:
                                    wait_low(pe, q)
                                for tt in range(TT):
                                    for c in range(2):
                                        ins = accumulate(tt, c, i)
                            ins.then_inc(s_read, 1)
                            reads += 1
                            last_job[p] = reads
                        else:
                            wait_low(pe, q)
                            for tt in range(TT):
                                for c in range(2):
                                    for i in range(3):
                                        ins = accumulate(tt, c, i)
                                    full(ins, f"{tag}{tt}{c}")
                            last_job[p] = f"{tag}11"
                    if name == "a":
                        before = f"ln_mix_{l}" if j == 1 else None
                    if before and name != "up":
                        pe.wait_ge(s_rs, stats.index(before) + 1)
                        rs = col("rs." + before, TT)
                        bank = fill(f"{before}.rstd", "m")
                        for tt in range(TT):
                            ins = mm(bank[:, tt * P:(tt + 1) * P], rs[:, tt:tt + 1].broadcast_to([P, P]), ident, True, True)
                        full(ins, f"{before}.rstd")
                elif kind == "rggate":
                    pe.wait_ge(s_rgw, 16)
                    pe.wait_ge(s_conv, 1)
                    rgw = at(A_RGW, 2, 4, 2, P)
                    uc = at(A_UC, 4, S)
                    z = step[1]
                    for ct in range(4):
                        name = f"rg.{z}{ct}"
                        bank = fill(name, "m")
                        for ax in range(2):
                            ins = mm(bank[:, ax * S:(ax + 1) * S], rgw[:, z, ct, ax, :], uc[:, ct, :], True, True)
                        full(ins, name)
                elif kind == "score":
                    phase, hd = step[1:]
                    _, a0, count = ATT[phase, hd]
                    if hd == 0:
                        for name in {"dil": ["rope"], "cross": ["cq.0", "cq.1", "ck.0", "ck.1"], "mla": [f"zturn{phase[-1]}.{j}" for j in range(4)],
                                     "dif": [f"bturn{phase[-1]}.{j}" for j in range(2)]}[phase[:3] if phase != "cross" else phase]:
                            if name == "rope":
                                pe.wait_ge(s_rope, 1)
                                for i in range(2):
                                    wait_drained(pe, f"v.{i}")
                            else:
                                wait_drained(pe, name)
                    for j in range(count):
                        name = f"score{a0 + j}"
                        bank = fill(name, "m")
                        ops = score_operands(phase, hd, j)
                        for qt in range(TT):
                            for f, (lhs, rhs) in enumerate(ops):
                                ins = mm(bank[:, qt * S:(qt + 1) * S], lhs(qt), rhs, f == 0, f == len(ops) - 1)
                        full(ins, name)
                elif kind == "turn":
                    phase, hd = step[1:]
                    n, a0, count = ATT[phase, hd]
                    pe.wait_ge(s_prob, n + 1)
                    name = f"turn{n}"
                    bank = fill(name, "m")
                    base = A_SC1 if phase in ("dil", "cross") else A_SC
                    prob = at(base + 512 * (a0 % 4), TT, S)
                    for kt in range(TT):
                        for qt in range(TT):
                            ins = nc.tensor.transpose(bank[:, kt * S + qt * P:kt * S + (qt + 1) * P], prob[:, qt, kt * P:(kt + 1) * P], ident)
                    full(ins, name)
                elif kind == "value":
                    phase, hd = step[1:]
                    n, a0, count = ATT[phase, hd]
                    wait_drained(pe, f"turn{n}")
                    base = A_SC1 if phase in ("dil", "cross") else A_SC
                    pT = at(base + 2048 + 512 * (n % 2), TT, S)
                    if phase == "dil" or phase[:3] == "mla":
                        v = at(A_V1, TT, 512) if phase == "dil" else at(A_VM, TT, 256)
                        name = f"value.{phase}{hd // 2}"
                        if hd % 2 == 0:
                            bank = fill(name, "m")
                        else:
                            bank = psum[jobs[name][0]]
                        p0 = 64 * (hd % 2)
                        for kt in range(TT):
                            ins = mm(bank[p0:p0 + 64, 0:S], v[:, kt, 64 * hd:64 * hd + 64], pT[:, kt, :], kt == 0, kt == TT - 1)
                        if hd % 2:
                            full(ins, name)
                        else:
                            ins.then_inc(s_even, 1)
                    elif phase == "cross":
                        v = at(A_CV, TT, 512)
                        if hd == 0:
                            for tt in range(TT):
                                wait_drained(pe, f"cv.{tt}")
                        name = f"value.cross{hd}"
                        bank = fill(name, "m")
                        for kt in range(TT):
                            ins = mm(bank[:, 0:S], v[:, kt, P * hd:P * hd + P], pT[:, kt, :], kt == 0, kt == TT - 1)
                        full(ins, name)
                    else:
                        v = at(A_VC, TT, 512)
                        if hd == 0:
                            for tt in range(TT):
                                wait_drained(pe, f"c{phase[4]}.{tt}")
                        name = f"value.{phase}{hd}"
                        bank = fill(name, "g")
                        for qt in range(TT):
                            for kt in range(TT):
                                ins = mm(bank[:, qt * P:(qt + 1) * P], pT[:, kt, qt * P:(qt + 1) * P], v[:, kt, P * (hd // 2):P * (hd // 2) + P],
                                         kt == 0, kt == TT - 1)
                        full(ins, name)
                elif kind == "aturn":
                    l = step[1]
                    pe.wait_ge(s_token_side, side_order.index((l, "a")) + 1)
                    za = at(A_ZA, TT, 512)
                    turns(f"aturn{l}", lambda k, tt: za[:, tt, k * P:(k + 1) * P], 4)
                elif kind == "bturn":
                    l = step[1]
                    pe.wait_ge(s_token_side, side_order.index((l, "b")) + 1)
                    zb = at(A_ZB, TT, 512)
                    turns(f"bturn{l}", lambda k, tt: zb[:, tt, k * P:(k + 1) * P], 4)
                elif kind == "zturn":
                    l = step[1]
                    pe.wait_ge(s_token_side, side_order.index((l, "z")) + 1)
                    z = at(A_Z, TT, 8, 96)
                    turns(f"zturn{l}", lambda k, tt: z[:, tt, k, :], 8)
                elif kind == "diffout":
                    l = step[1]
                    pe.wait_ge(s_token_side, side_order.index((l, "do")) + 1)
                    do = at(A_DO, TT, 256)
                    turns(f"diffout{l}", lambda k, tt: do[:, tt, k * P:(k + 1) * P], 2)
                elif kind == "hout":
                    l = step[1]
                    pe.wait_ge(s_token_side, side_order.index((l, "ho")) + 1)
                    ho = at(A_HO, TT, 256)
                    turns(f"hout{l}", lambda k, tt: ho[:, tt, k * P:(k + 1) * P], 2)
                elif kind == "fnet":
                    l = step[1]
                    fT, ab = at(A_FT, 2, S), at(A_AB, TT, 2, S)
                    dftd = const[:, C_DFTD:C_DFTD + 2 * P]
                    dc = const[:, C_DFTC:C_DFTC + TT * S].rearrange("p (s t) -> p s t", s=TT)
                    ds = const[:, C_DFTS:C_DFTS + TT * S].rearrange("p (s t) -> p s t", s=TT)
                    wait_drained(pe, f"e{l}.0")
                    for st in range(TT):
                        bank = fill(f"fab{l}.{st}", "m")
                        for ft in range(2):
                            ins = mm(bank[:, ft * S:(ft + 1) * S], fT[:, ft, st * P:(st + 1) * P], dftd, True, True)
                        full(ins, f"fab{l}.{st}")
                    for st in range(TT):
                        wait_drained(pe, f"fab{l}.{st}")
                    bank = fill(f"fy{l}", "m")
                    for ft in range(2):
                        for st in range(TT):
                            mm(bank[:, ft * S:(ft + 1) * S], ab[:, st, ft, 0:P], dc[:, st, :], st == 0, False)
                            ins = mm(bank[:, ft * S:(ft + 1) * S], ab[:, st, ft, P:2 * P], ds[:, st, :], False, st == TT - 1)
                    full(ins, f"fy{l}")
                elif kind == "gate":
                    _, l, g, half, p = step
                    gemm(f"gate{l}.{g}{half}", "g", p, "feat")
                elif kind == "merge":
                    _, l, br, p = step
                    if br == 0:
                        for j in range(2):
                            wait_drained(pe, f"value.mla{l}{j}")
                    elif br == 1:
                        wait_drained(pe, f"fy{l}")
                    elif br == 2:
                        wait_drained(pe, f"diffout{l}.0")
                    else:
                        wait_drained(pe, f"hout{l}.0")
                    w = loaded(p).rearrange("p (k c) -> p k c", k=2)
                    for j in range(4):
                        job = f"merge{l}.{br}{j}"
                        bank = fill(job, "g")
                        for jj in range(2):
                            for k in range(2):
                                c0 = (2 * j + jj) * P
                                ins = mm(bank[:, jj * S:(jj + 1) * S], w[:, k, c0:c0 + P], oT[:, 2 * br + k, :], k == 0, k == 1)
                        full(ins, job)
                    last_job[p] = job
                elif kind == "level":
                    _, l, i, hp = step
                    job = f"level{l}.{i}{hp}"
                    if i < len(LEVELS):
                        idx = (l * len(LEVELS) + i) * 2 + hp
                        pe.wait_ge(s_query, idx + 1)
                        pe.wait_ge(s_key, idx + 1)
                        q = at(A_QL + 512 * (idx % 4), 2, S)
                        k = at(A_KL + 512 * (idx % 4), 2, S)
                        q0 = 0
                    else:
                        q, k, q0 = at(A_HQ, 4, S), at(A_KK, 4, S), 2 * hp
                        pe.wait_ge(s_hgrn_k, l + 1)
                        wait_drained(pe, f"e{l}.1")
                    bank = fill(job, "m")
                    for hh in range(2):
                        for st in range(TT):
                            t0 = 1 - st if i == 0 else st
                            ins = mm(bank[:, (2 * hh + st) * P:(2 * hh + st + 1) * P], k[:, q0 + hh, st * P:(st + 1) * P],
                                     q[:, q0 + hh, t0 * P:(t0 + 1) * P], True, True)
                    full(ins, job)
                elif kind == "hval":
                    l = step[1]
                    sT, v = at(A_ST, 4, TT, S), at(A_VC, TT, 512)
                    for hp in range(2):
                        wait_drained(pe, f"level{l}.{len(LEVELS)}{hp}")
                        job = f"hval{l}.{hp}"
                        bank = fill(job, "m")
                        for tt in range(TT):
                            for hh in range(2):
                                for st in range(TT):
                                    ins = mm(bank[:, (2 * tt + hh) * P:(2 * tt + hh + 1) * P], sT[:, 2 * hp + hh, st, tt * P:(tt + 1) * P],
                                             v[:, st, 256 + hp * P:256 + (hp + 1) * P], st == 0, st == TT - 1)
                        full(ins, job)

        @block.sync
        def _(sp):
            sp.dma_start(at(A_ROPE, S).bitcast(I32), pos_d).then_inc(s_pos, 16)
            sp.dma_start(const[:, 0:C_LOGC], const_d[:, 0:C_LOGC]).then_inc(s_ident, 16)
            for tt in range(TT):
                sp.dma_start(h[:, tt, :], x_d[tt * P:(tt + 1) * P, :]).then_inc(s_x[tt], 16)
            sp.dma_start(vec[:], vec_d).then_inc(s_vec, 16)

            def load_piece(p):
                if p >= RING:
                    old = p - RING
                    if old in split_of:
                        wait_low(sp, split_of[old])
                    if old not in split_of or split[split_of[old]][1] < PIECE:
                        wait_read(sp, old)
                sp.dma_start(raw(p), pieces_d[p]).then_inc(piece_loaded[p % RING], 16)

            load_piece(0)
            sp.dma_start(const[:, C_LOGC:], const_d[:, C_LOGC:]).then_inc(s_const, 16)
            load_piece(1)
            load_piece(2)
            sp.dma_start(at(A_MEM, TT, D), mem_d.rearrange("(t p) d -> p t d", p=P)).then_inc(s_mem, 16)
            sp.dma_start(at(A_RGW, 16 * P), rgw_d).then_inc(s_rgw, 16)
            sp.dma_start(row[:], row_d).then_inc(s_row, 16)
            for p in range(RING, NP):
                load_piece(p)
            for tt in range(TT):
                wait_drained(sp, f"wd1.{tt}1")
                sp.dma_start(out_d[tt * P:(tt + 1) * P, :], h[:, tt, :]).then_inc(s_out, 16)
            sp.wait_ge(s_out, 16 * TT)

        @block.gpsimd
        def _(pool):
            n_link = 0

            def link(ins):
                nonlocal n_link
                n_link += 1
                ins.then_inc(pool_link, 1)
                pool.wait_ge(pool_link, n_link)

            up = at(A_U, 4, UPAD)
            link(nc.gpsimd.memset(up[:, :, 0:2], 0.0))
            nc.gpsimd.memset(up[:, :, S + 2:S + 3], 0.0).then_inc(s_pads_zeroed, 1)
            done = 0

            def split_ahead(p):
                nonlocal done
                while done < min(split_of[p] + 2, len(split)):
                    q, (pp, n) = done, split[done]
                    done += 1
                    if low[q][0] != "pool":
                        continue
                    for half in range(2):
                        cut = slice(half * n // 2, (half + 1) * n // 2)
                        pool.wait_ge(s_weight_high, 2 * q + half + 1)
                        ins = nc.gpsimd.tensor_tensor(w_lo[:, q % SPLITS, cut], raw(pp)[:, cut], w_hi[:, q % SPLITS, cut].bitcast(F32), ALU.subtract)
                        if half == 0:
                            link(ins)
                        else:
                            ins.then_inc(s_weight_low_pool, 1)

            for step in steps:
                kind = step[0]
                if kind in ("proj", "gate") and step[-1] in split_of:
                    split_ahead(step[-1])
                if kind == "decay":
                    _, l, i, hp = step
                    idx = (l * len(LEVELS) + i) * 2 + hp
                    half = LEVELS[i]
                    if i == hp == 0:
                        wait_filled(pool, f"score{ATT[f'diff{l}', 3][1] + 1}")
                    if idx >= 4:
                        prev = idx - 4
                        wait_filled(pool, f"level{prev // (2 * len(LEVELS))}.{prev // 2 % len(LEVELS)}{prev % 2}")
                    if idx:
                        pool.wait_ge(s_key, idx)
                    k = at(A_KL + 512 * (idx % 4), 2 * S)
                    link(nc.gpsimd.memset(k, 0.0))
                    pool.wait_ge(s_decay, idx + 1)
                    x = at(A_X + 512 * (idx % 4), 2 * S).rearrange("p (b w c) -> p b w c", w=2, c=half)
                    kk = at(A_KK, 4 * S)[:, hp * 512:(hp + 1) * 512].rearrange("p (b w c) -> p b w c", w=2, c=half)
                    kl = k.rearrange("p (b w c) -> p b w c", w=2, c=half)
                    link(nc.gpsimd.tensor_tensor(kl[0:64, :, 0, :], kk[0:64, :, 0, :], x[0:64, :, 0, :], ALU.mult))
                    nc.gpsimd.tensor_tensor(kl[64:128, :, 1, :], kk[64:128, :, 1, :], x[64:128, :, 1, :], ALU.mult).then_inc(s_key, 1)

        @block.scalar
        def _(act):
            n_link = 0

            def link(ins):
                nonlocal n_link
                n_link += 1
                ins.then_inc(act_link, 1)
                act.wait_ge(act_link, n_link)

            def copy(out, in_, scale=1.0):
                return nc.scalar.activation(out, in_, ACT.Copy, scale=scale)

            def bank2(bank):
                return bank[:].rearrange("p (a t) -> p a t", a=2)

            done = 0

            def split_ahead(p, ahead=1):
                nonlocal done
                while done < min(split_of[p] + 1 + ahead, len(split)):
                    q, (pp, n) = done, split[done]
                    done += 1
                    act.wait_ge(piece_loaded[pp % RING], 16 * (pp // RING + 1))
                    if q >= SPLITS:
                        wait_read(act, split[q - SPLITS][0])
                    for half in range(2):
                        cut = slice(half * n // 2, (half + 1) * n // 2)
                        copy(w_hi[:, q % SPLITS, cut], raw(pp)[:, cut]).then_inc(s_weight_high, 1)

            scaled_gates = []

            def gate_tanh():
                while scaled_gates:
                    l, g, half = scaled_gates.pop()
                    k = (4 * g + 2 * half) % 16
                    gate = at(A_GATE, 16, S)[:, k:k + 2, :]
                    wait_drained(act, f"gate{l}.{g}{half}")
                    nc.scalar.activation(gate, gate, ACT.Tanh, scale=0.5).then_inc(s_gate, 1)

            for step in steps:
                kind = step[0]
                p = step[-1] if kind in ("proj", "gate") else None
                if step[:2] == ("proj", "cq") and step[3] == 1:
                    split_ahead(p, 0)
                    cq1 = p
                elif step[:4] == ("proj", "co", None, 0):
                    split_ahead(cq1)
                elif p in split_of:
                    split_ahead(p)
                if kind in ("norm", "memscale"):
                    name = step[1] if kind == "norm" else "norm_mem_g"
                    if kind == "norm":
                        if name == "norm_mix_g":
                            act.wait_ge(s_vec, 16)
                        gi = V_GAIN + GAINS.index(name) * KT
                        gain = col("gain.final", KT) if name == "ln_mix_0" else vec[:, gi:gi + KT]
                        for j in (0, 2):
                            bank = bank2(wait_filled(act, f"{name}.{j}.0"))
                            for k in (2 * j, 2 * j + 1):
                                ins = copy(x_hi[:, k, :], bank[:, k % 2, :], gain[:, k:k + 1])
                            ins.then_inc(s_norm_high, 1)
                        if name == "norm_mix_g":
                            act.wait_ge(s_angles, 1)
                            cs = at(A_ROPE, 2 * S)
                            nc.scalar.activation(cs, cs, ACT.Sin).then_inc(s_trig, 1)
                            split_ahead(0, 0)
                        elif name == "ln_mix_0":
                            split_ahead(piece_after[name])
                    src = at(A_MEM, TT, D) if kind == "memscale" else h
                    for stat_name in ["final"] * (name == "ln_mix_0") + [name] * (kind == "memscale" or name != "norm_mem_g"):
                        inputs = norm_input(stat_name)
                        ss = col("ss." + stat_name, 4 * TT)
                        for i, (part, tt, c0, n, s_in, value) in enumerate(inputs):
                            act.wait_ge(s_in, value)
                            ins = nc.scalar.activation(junk[:, 0:n], src[:, tt, c0:c0 + n], ACT.Square, accum_out=ss[:, TT * part + tt:TT * part + tt + 1])
                            if i < len(inputs) - 1:
                                link(ins)
                            else:
                                ins.then_inc(s_sumsq, 1)
                        if stat_name == "final":
                            act.wait_ge(s_sumsq, stats.index("final") + 1)
                    if kind == "memscale":
                        act.wait_ge(s_softplus_in, 1)
                        nc.scalar.activation(col("sp.x", 8), col("sp.na", 8), ACT.Exp).then_inc(s_softplus_exp, 1)
                        act.wait_ge(s_bound_in, 1)
                        nc.scalar.activation(col("lb.x", 8), col("lb.e", 8), ACT.Exp).then_inc(s_bound_exp, 1)
                elif kind == "proj":
                    _, name, l, j, _ = step
                    job = job_of(name, l, j)
                    def high_part(m):
                        wait_drained(act, f"up.{m}" if m < 16 else f"gu{(m - 16) // 11}.{(m - 16) % 11 * 2 + 1}")
                        k = 2 * (m if m < 16 else (m - 16) % 11)
                        copy(hid_hi[:, k:k + 2, :], product[:, m % 2, :].rearrange("p (a t) -> p a t", a=2)).then_inc(s_hidden_high, 1)

                    before = {"v": "norm_mix_g", "cv": "norm_mem_g"}.get(name, f"ln_mix_{l}")
                    if name in ("v", "cv", "a", "b", "c", "hg", "kr"):
                        act.wait_ge(s_rs, stats.index(before) + 1)
                    rs = col("rs." + before, TT) if name in ("v", "cv", "a", "b", "c", "kr") else None
                    if name in ("v", "cv", "b", "c"):
                        dst = at({"v": A_V1, "cv": A_CV, "b": A_ZB, "c": A_VC}[name], TT, 512)
                        if name == "cv":
                            act.wait_ge(s_rope, 1)
                        bank = bank2(wait_filled(act, job))
                        for tt in range(TT):
                            ins = copy(dst[:, tt, 256 * j:256 * j + 256], bank[:, tt, :], rs[:, tt:tt + 1])
                        drains(ins, job)
                    elif name == "y":
                        wait_drained(act, job)
                        yg = at(A_YG, 4, S)[:, 2 * j:2 * j + 2, :]
                        nc.scalar.activation(yg, yg, ACT.Gelu_apprx_tanh)
                    elif name == "a" and j == 1:
                        za = at(A_ZA, TT, 512)
                        if l:
                            wait_filled(act, "hval0.1")
                        ss = col(f"ss.a{l}", 3 * TT).rearrange("p (s t) -> p s t", t=TT)
                        rsq, rskv = col(f"rsq{l}", TT), col(f"rskv{l}", TT)
                        for half in range(2):
                            bank = bank2(wait_filled(act, f"a{l}.{half}"))
                            for tt in range(TT):
                                copy(za[:, tt, 256 * half:256 * half + 256], bank[:, tt, :], rs[:, tt:tt + 1])
                            for tt in range(TT):
                                jk = junk[:, 512 * tt + 256 * half:512 * tt + 256 * half + 256]
                                if half == 0:
                                    ins = nc.scalar.activation(jk, bank[:, tt, :], ACT.Square, scale=rsq[:, tt:tt + 1], accum_out=ss[:, 0, tt:tt + 1])
                                else:
                                    nc.scalar.activation(jk[:, 0:128], bank[:, tt, 0:128], ACT.Square, scale=rsq[:, tt:tt + 1], accum_out=ss[:, 1, tt:tt + 1])
                                    ins = nc.scalar.activation(jk[:, 128:256], bank[:, tt, 128:256], ACT.Square, scale=rskv[:, tt:tt + 1], accum_out=ss[:, 2, tt:tt + 1])
                            drains(ins, f"a{l}.{half}")
                    elif name == "hg":
                        bank = bank2(wait_filled(act, job))
                        for tt in range(TT):
                            ins = nc.scalar.activation(at(A_SG, TT, 256)[:, tt, :], bank[:, tt, :], ACT.Tanh, scale=col(f"rsh{l}", TT)[:, tt:tt + 1])
                        drains(ins, job)
                    elif name == "kr":
                        z = at(A_Z, TT, 8, 96)
                        drains(copy(at(A_KR, S)[0:32, :], wait_filled(act, job)[0:32, 0:S]), job)
                        for tt in range(TT):
                            bank = wait_filled(act, f"uq{l}.{tt}")
                            drains(copy(z[:, tt, 0:4, :], bank[:, 0:384].rearrange("p (h d) -> p h d", h=4)), f"uq{l}.{tt}")
                        vm = at(A_VM, TT, 256)
                        for tt in range(TT):
                            bank = wait_filled(act, f"ukv{l}.{tt}")
                            copy(z[:, tt, 4:8, 0:64], bank[:, 0:256].rearrange("p (h d) -> p h d", h=4))
                            drains(copy(vm[:, tt, :], bank[:, 256:512]), f"ukv{l}.{tt}")
                        bank = wait_filled(act, f"krt{l}")[:, 0:64].rearrange("p (t d) -> p t d", t=TT)
                        for tt in range(TT):
                            ins = copy(z[:, tt, 4:8, 64:96], bank[:, tt, None, :].broadcast_to([P, 4, 32]), rs[:, tt:tt + 1])
                        drains(ins, f"krt{l}")
                    elif name == "f":
                        kk = at(A_KK, 4, S)[:, 2 * j:2 * j + 2, :]
                        wait_drained(act, job)
                        nc.scalar.activation(kk, kk, ACT.Sigmoid).then_inc(s_sig, 1)
                    elif name in ("up", "gu") and (name == "up" or j % 2 == 0):
                        m = product_of(name, l, j)
                        if j:
                            high_part(m - 1)
                        if name == "up":
                            if m >= 2:
                                act.wait_ge(s_hidden_low, m - 1)
                            nc.scalar.activation(product[:, m % 2, :], wait_filled(act, job)[:], ACT.Relu).then_inc(s_relu, 1)
                        else:
                            wait_drained(act, job)
                            nc.scalar.activation(product[:, m % 2, :], product[:, m % 2, :], ACT.Silu).then_inc(s_silu, 1)
                    elif name in ("down", "wd") and j == 0:
                        high_part(15 if name == "down" else product_of("gu", l, 21))
                elif kind == "logf":
                    l = step[1]
                    act.wait_ge(s_f, l + 1)
                    nc.scalar.activation(at(A_F, 4 * S), at(A_F, 4 * S), ACT.Ln).then_inc(s_log_f, 1)
                elif kind == "mix":
                    k = 4 * step[1]
                    if k:
                        act.wait_ge(s_rec, 1)
                        wait_filled(act, "cv.1")
                    else:
                        for i in range(4):
                            wait_drained(act, f"value.dil{i}")
                    copy(x_hi[:, k:k + 4, :], oT[:, k:k + 4, :]).then_inc(s_mix_high, 1)
                elif kind == "rggate":
                    r, ii = at(A_RG_R, 2, 4, S), at(A_RG_I, 2, 4, S)
                    z = step[1]
                    for ct in range(4):
                        name = f"rg.{z}{ct}"
                        bank = bank2(wait_filled(act, name))
                        b0 = V_RGB + (z * 4 + ct) * 2
                        nc.scalar.activation(r[:, z, ct, :], bank[:, 0, :], ACT.Sigmoid, bias=vec[:, b0:b0 + 1])
                        drains(nc.scalar.activation(ii[:, z, ct, :], bank[:, 1, :], ACT.Sigmoid, bias=vec[:, b0 + 1:b0 + 2]), name)
                elif kind == "rgT":
                    act.wait_ge(s_rg_exponent, 1)
                    nc.scalar.activation(at(A_RG_T, 2048), at(A_RG_R, 2048), ACT.Tanh)
                    nc.scalar.activation(at(A_RG_A, 2048), at(A_RG_R, 2048), ACT.Exp, scale=-1.0).then_inc(s_rg_tanh_exp, 1)
                elif kind == "rgS":
                    act.wait_ge(s_rg_square, 1)
                    nc.scalar.activation(at(A_RG_T, 2048), at(A_RG_T, 2048), ACT.Sqrt).then_inc(s_rg_root, 1)
                elif kind == "score":
                    phase, hd = step[1:]
                    n, a0, count = ATT[phase, hd]
                    masked = phase == "dil"
                    scale = {"dil": 1.0, "cro": 128.0 ** -0.5, "mla": 96.0 ** -0.5, "dif": 32.0 ** -0.5}[phase[:3]]
                    base = A_SC1 if phase in ("dil", "cross") else A_SC
                    if phase[:4] == "diff" and hd == 0:
                        act.wait_ge(s_lambda_in, int(phase[4]) + 1)
                        nc.scalar.activation(col(f"lam.e{phase[4]}", 2), col(f"lam.d{phase[4]}", 2), ACT.Exp).then_inc(s_lambda_exp, 1)
                    for j in range(count):
                        a = a0 + j
                        sc = at(base + 512 * (a % 4), TT, S)
                        act.wait_ge(s_max, a + 1)
                        if not masked:
                            if a >= 4:
                                n4 = ATT[HEAD_OF_UNIT[a - 4]][0]
                                wait_filled(act, f"turn{n4}")
                            src = bank2(wait_filled(act, f"score{a}"))
                        else:
                            src = sc
                        nm, sm = col(f"nmax{a % 16}", TT), col(f"sum{a % 16}", TT)
                        for qt in range(TT):
                            ins = nc.scalar.activation(sc[:, qt, :], src[:, qt, :], ACT.Exp, bias=nm[:, qt:qt + 1], scale=scale, accum_out=sm[:, qt:qt + 1])
                        if masked:
                            ins.then_inc(s_exp, 1)
                        else:
                            drains(ins, f"score{a}")
                elif kind == "turn":
                    phase, hd = step[1:]
                    n, a0, count = ATT[phase, hd]
                    base = A_SC1 if phase in ("dil", "cross") else A_SC
                    pT = at(base + 2048 + 512 * (n % 2), 512)
                    if n >= 2:
                        ph, h2, _ = HEADS[n - 2]
                        if ph in ("cross", "diff0", "diff1"):
                            wait_filled(act, f"value.{ph}{h2}")
                        elif h2 % 2:
                            wait_filled(act, f"value.{ph}{h2 // 2}")
                        else:
                            act.wait_ge(s_even, EVEN[n - 2])
                    drains(copy(pT, wait_filled(act, f"turn{n}")[:]), f"turn{n}")
                elif kind == "value":
                    phase, hd = step[1:]
                    if phase == "cross":
                        name = f"value.cross{hd}"
                        drains(copy(at(A_CO, 4, S)[:, hd, :], wait_filled(act, name)[:, 0:S]), name)
                    elif phase[:4] == "diff":
                        name = f"value.{phase}{hd}"
                        do = at(A_DO, TT, 4, 64)
                        bank = wait_filled(act, name)[:, 0:256].rearrange("p (q c) -> p q c", q=2)
                        drains(copy(do[:, :, hd, :], bank[:, :, 64 * (hd % 2):64 * (hd % 2) + 64]), name)
                    elif hd % 2:
                        name = f"value.{phase}{hd // 2}"
                        drains(copy(oT[:, hd // 2, :], wait_filled(act, name)[:, 0:S]), name)
                elif kind == "aturn":
                    l = step[1]
                    cT = at(A_CT, 4, S)
                    for j in range(2):
                        bank = bank2(wait_filled(act, f"aturn{l}.{j}"))
                        for jj in range(2):
                            k = 2 * j + jj
                            ins = copy(cT[:, k, :], bank[:, jj, :], vec[:, V_QA + 4 * l + k:V_QA + 4 * l + k + 1])
                        drains(ins, f"aturn{l}.{j}")
                elif kind == "bturn":
                    l = step[1]
                    dT = at(A_DT, 4, S)
                    for j in range(2):
                        drains(copy(dT[:, 2 * j:2 * j + 2, :], bank2(wait_filled(act, f"bturn{l}.{j}"))), f"bturn{l}.{j}")
                elif kind == "zturn":
                    l = step[1]
                    z = at(A_QKT, 8, S)
                    for j in range(4):
                        bank = bank2(wait_filled(act, f"zturn{l}.{j}"))
                        drains(copy(z[0:96, 2 * j:2 * j + 2, :], bank[0:96, :, :]), f"zturn{l}.{j}")
                elif kind == "fnet":
                    l = step[1]
                    ab = at(A_AB, TT, 2, S)
                    for st in range(TT):
                        drains(copy(ab[:, st, :, :], bank2(wait_filled(act, f"fab{l}.{st}"))), f"fab{l}.{st}")
                    drains(copy(oT[:, 2:4, :], bank2(wait_filled(act, f"fy{l}"))), f"fy{l}")
                elif kind == "gate":
                    _, l, g, half, _ = step
                    gate_tanh()
                    scaled_gates.append((l, g, half))
                elif kind == "merge" and step[2] in (0, 2):
                    gate_tanh()
                elif kind == "merge" and step[2] == 3:
                    l = step[1]
                    for j in range(4):
                        act.wait_ge(s_merged_sum, 4 * l + j + 1)
                        copy(x_hi[:, 2 * j:2 * j + 2, :], merged[:, 2 * j:2 * j + 2, :]).then_inc(s_merged_high, 1)
                elif kind in ("diffout", "hout"):
                    l = step[1]
                    k = 4 if kind == "diffout" else 6
                    drains(copy(oT[:, k:k + 2, :], bank2(wait_filled(act, f"{kind}{l}.0"))), f"{kind}{l}.0")
                elif kind == "decay":
                    _, l, i, hp = step
                    idx = (l * len(LEVELS) + i) * 2 + hp
                    act.wait_ge(s_decay_log, idx + 1)
                    x = at(A_X + 512 * (idx % 4), 512)
                    nc.scalar.activation(x, x, ACT.Exp).then_inc(s_decay, 1)
                elif kind == "hval":
                    l = step[1]
                    ho = at(A_HO, TT, 4, 64)
                    for hp in range(2):
                        name = f"hval{l}.{hp}"
                        bank = wait_filled(act, name)[:].rearrange("p (t h c) -> p t h c", t=2, h=2)
                        copy(ho[:, :, 2 * hp, :], bank[:, :, 0, 0:64])
                        drains(copy(ho[:, :, 2 * hp + 1, :], bank[:, :, 1, 64:128]), name)

        @block.vector
        def _(dve):
            n_link = 0
            v = nc.vector

            def link(ins):
                nonlocal n_link
                n_link += 1
                ins.then_inc(dve_link, 1)
                dve.wait_ge(dve_link, n_link)

            def bank2(bank):
                return bank[:].rearrange("p (a t) -> p a t", a=2)

            def rsqrt(x, y, t, n, s_done=None):
                link(v.tensor_scalar(t.bitcast(I32), x.bitcast(I32), 1, None, ALU.logical_shift_right))
                link(v.tensor_scalar(y.bitcast(I32), t.bitcast(I32), -1.0, float(RSQRT_MAGIC), ALU.mult, ALU.add))
                for i in range(3):
                    link(v.tensor_tensor(t, y, y, ALU.mult))
                    link(v.scalar_tensor_tensor(t, t, -0.5, x, ALU.mult, ALU.mult))
                    ins = v.scalar_tensor_tensor(y, t, 1.5, y, ALU.add, ALU.mult)
                    if i < 2 or s_done is None:
                        link(ins)
                    else:
                        ins.then_inc(s_done, 1)

            def heads_norm(zv, groups, n, scratch):
                sq = scratch[:, 0:groups * n].rearrange("p (a g n) -> p a g n", a=TT, n=n)
                ss, rs, t = col("hn.ss", 32)[:, 0:groups], col("hn.rs", 32)[:, 0:groups], col("hn.t", 32)[:, 0:groups]
                link(v.tensor_tensor(sq, zv, zv, ALU.mult))
                link(v.tensor_reduce(ss, sq.rearrange("p a g n -> p (a g) n"), AX_X, ALU.add))
                link(v.tensor_scalar(ss, ss, 1.0 / n, EPS, ALU.mult, ALU.add))
                rsqrt(ss, rs, t, groups)
                return rs

            def rope32(x1, x2, heads):
                c = const[:, C_COS:C_COS + TT * 16].rearrange("p (a d) -> p a d", a=TT)[:, :, None, :].broadcast_to([P, TT, heads, 16])
                s = const[:, C_SIN:C_SIN + TT * 16].rearrange("p (a d) -> p a d", a=TT)[:, :, None, :].broadcast_to([P, TT, heads, 16])
                n = TT * heads * 16
                t = [scratch_xs[:, i * n:(i + 1) * n].rearrange("p (a g d) -> p a g d", a=TT, d=16) for i in range(4)]
                v.tensor_tensor(t[0], x1, c, ALU.mult)
                v.tensor_tensor(t[1], x2, s, ALU.mult)
                v.tensor_tensor(t[2], x1, s, ALU.mult)
                link(v.tensor_tensor(t[3], x2, c, ALU.mult))
                v.tensor_tensor(x1, t[0], t[1], ALU.subtract)
                return v.tensor_tensor(x2, t[2], t[3], ALU.add)

            scratch_xs = xs[:].rearrange("p a b -> p (a b)")
            def level_decay(l, i, hp):
                idx, half = (l * len(LEVELS) + i) * 2 + hp, LEVELS[i]
                nb = S // (2 * half)
                E, F = at(A_E, 4, S + 1), at(A_F, 4, S)
                if idx >= 4:
                    dve.wait_ge(s_key, idx - 3)
                    dve.wait_ge(s_query, idx - 3)
                x = at(A_X + 512 * (idx % 4), 2 * S).rearrange("p (g b w c) -> p g b w c", g=2, w=2, c=half)
                f5 = F[:, 2 * hp:2 * hp + 2, :].rearrange("p g (b w c) -> p g b w c", w=2, c=half)
                mid = E[:, 2 * hp:2 * hp + 2, half:S:2 * half][:, :, :, None].broadcast_to([P, 2, nb, half])
                v.tensor_tensor(x[:, :, :, 0, :], mid, f5[:, :, :, 0, :], ALU.subtract)
                v.tensor_tensor(x[:, :, :, 1, :], f5[:, :, :, 1, :], mid, ALU.subtract).then_inc(s_decay_log, 1)

            def level_query(l, i, hp):
                idx = (l * len(LEVELS) + i) * 2 + hp
                dve.wait_ge(s_decay, idx + 1)
                if i == 0:
                    wait_drained(dve, f"value.diff{l}3")
                if idx >= 4:
                    prev = idx - 4
                    wait_filled(dve, f"level{prev // (2 * len(LEVELS))}.{prev // 2 % len(LEVELS)}{prev % 2}")
                q = at(A_HQ, 4 * S)[:, hp * 512:(hp + 1) * 512]
                v.tensor_tensor(at(A_QL + 512 * (idx % 4), 2 * S), q, at(A_X + 512 * (idx % 4), 2 * S), ALU.mult).then_inc(s_query, 1)

            def level_place(l, i, hp):
                job = f"level{l}.{i}{hp}"
                bank = wait_filled(dve, job)[:].rearrange("p (g s c) -> p g s c", g=2, s=2)
                sT = at(A_ST + 1024 * hp, 2, 4, P)
                if i == 0:
                    drains(v.tensor_copy(sT[:, :, 1:3, :], bank), job)
                elif i == 1:
                    drains(v.tensor_copy(sT[:, :, 0:4:3, :], bank), job)
                else:
                    if i == 2:
                        wait_drained(dve, f"level{l}.1{hp}")
                    else:
                        wait_drained(dve, f"level{l}.{i - 1}{hp}")
                    m0 = C_MASK + (i - 2) * P
                    mask = const[:, m0:m0 + P].bitcast(I32)[:, None, None, :].broadcast_to([P, 2, 2, P])
                    drains(v.copy_predicated(sT[:, :, 0:4:3, :], mask, bank), job)
            def split_ahead(p, ahead=1):
                nonlocal done
                while done < min(split_of[p] + 1 + ahead, len(split)):
                    q, (pp, n) = done, split[done]
                    done += 1
                    if low[q][0] != "dve":
                        continue
                    dve.wait_ge(s_weight_high, 2 * (q + 1))
                    v.tensor_tensor(w_lo[:, q % SPLITS, 0:n], raw(pp)[:, 0:n], w_hi[:, q % SPLITS, 0:n].bitcast(F32), ALU.subtract).then_inc(s_weight_low, 1)

            def product_low(m):
                k = 2 * (m if m < 16 else (m - 16) % 11)
                dve.wait_ge(s_hidden_high, m + 1)
                v.tensor_tensor(hid_lo[:, k:k + 2, :], product[:, m % 2, :].rearrange("p (a t) -> p a t", a=2),
                                hid_hi[:, k:k + 2, :].bitcast(F32), ALU.subtract).then_inc(s_hidden_low, 1)

            def merged_low(l, j):
                dve.wait_ge(s_merged_high, 4 * l + j + 1)
                v.tensor_tensor(x_lo[:, 2 * j:2 * j + 2, :], merged[:, 2 * j:2 * j + 2, :], x_hi[:, 2 * j:2 * j + 2, :].bitcast(F32),
                                ALU.subtract).then_inc(s_merged_low, 1)

            done = 0
            for step in steps:
                kind = step[0]
                p = step[-1] if kind in ("proj", "gate") else None
                if step[:2] == ("proj", "cq") and step[3] == 1:
                    split_ahead(p, 0)
                    cq1 = p
                elif step[:4] == ("proj", "co", None, 0):
                    split_ahead(cq1)
                elif p in split_of:
                    split_ahead(p)
                if kind == "setup":
                    dve.wait_ge(s_pos, 16)
                    dve.wait_ge(s_ident, 16)
                    r4 = at(A_ROPE, 4, S)
                    ang, n = r4[:, 2, :], r4[:, 3, :]
                    link(v.tensor_copy(n, r4[:, 0, :].bitcast(I32)))
                    link(v.tensor_scalar(ang, n, const[:, C_FREQ:C_FREQ + 1], None, ALU.mult))
                    for f, (quarter, shift) in enumerate(((0.25, 0.5 * np.pi), (0.0, 0.0))):
                        out = r4[:, f, :]
                        link(v.tensor_scalar(n, ang, float(1.0 / (2.0 * np.pi)), quarter, ALU.mult, ALU.add))
                        link(v.tensor_scalar(n, n, ROUND, None, ALU.add))
                        link(v.tensor_scalar(n, n, ROUND, None, ALU.subtract))
                        link(v.scalar_tensor_tensor(out, n, -TWO_PI_HI, ang, ALU.mult, ALU.add))
                        link(v.scalar_tensor_tensor(out, n, -TWO_PI_MID, out, ALU.mult, ALU.add))
                        link(v.scalar_tensor_tensor(out, n, -TWO_PI_LO, out, ALU.mult, ALU.add))
                        link(v.tensor_scalar(out, out, shift, 3.1415925, ALU.add, ALU.min))
                        ins = v.tensor_scalar(out, out, -3.1415925, None, ALU.max)
                        if f == 0:
                            link(ins)
                        else:
                            ins.then_inc(s_angles, 1)
                elif kind in ("norm", "memscale"):
                    name = step[1] if kind == "norm" else "norm_mem_g"
                    if kind == "norm":
                        if name == "norm_mix_g":
                            dve.wait_ge(s_vec, 16)
                        gi = V_GAIN + GAINS.index(name) * KT
                        gain = col("gain.final", KT) if name == "ln_mix_0" else vec[:, gi:gi + KT]
                        ni = norms.index(name)
                        for j in (1, 3):
                            bank = bank2(wait_filled(dve, f"{name}.{j}.0"))
                            for k in (2 * j, 2 * j + 1):
                                ins = v.tensor_scalar(x_hi[:, k, :], bank[:, k % 2, :], gain[:, k:k + 1], None, ALU.mult)
                            ins.then_inc(s_norm_high_dve, 1)
                        for j in range(KT // 2):
                            dve.wait_ge((s_norm_high, s_norm_high_dve)[j % 2], 2 * ni + j // 2 + 1)
                            bank = bank2(wait_filled(dve, f"{name}.{j}.0"))
                            for k in (2 * j, 2 * j + 1):
                                ins = v.scalar_tensor_tensor(x_lo[:, k, :], bank[:, k % 2, :], gain[:, k:k + 1], x_hi[:, k, :].bitcast(F32), ALU.mult, ALU.subtract)
                            drains(ins, f"{name}.{j}.0")
                        if name == "norm_mix_g":
                            split_ahead(0, 0)
                        elif name == "ln_mix_0":
                            split_ahead(piece_after[name])
                    for stat_name in ["final"] * (name == "ln_mix_0") + [name] * (kind == "memscale" or name != "norm_mem_g"):
                        s4, rs, t = col("ss." + stat_name, 4 * TT), col("rs." + stat_name, TT), col("nt", TT)
                        parts = 1 + max(x[0] for x in norm_input(stat_name))
                        ss = s4[:, 0:TT]
                        dve.wait_ge(s_sumsq, stats.index(stat_name) + 1)
                        if parts == 2:
                            link(v.tensor_tensor(ss, s4[:, 0:TT], s4[:, TT:2 * TT], ALU.add))
                        elif parts == 4:
                            link(v.tensor_tensor(s4[:, 0:4], s4[:, 0:4], s4[:, 4:8], ALU.add))
                            link(v.tensor_tensor(ss, s4[:, 0:TT], s4[:, TT:2 * TT], ALU.add))
                        link(v.tensor_scalar(ss, ss, 1.0 / D, EPS, ALU.mult, ALU.add))
                        if stat_name[:6] != "ln_mix":
                            rsqrt(ss, rs, t, TT, s_rs)
                        else:
                            rsqrt(ss, rs, t, TT)
                            if name == "ln_mix_0":
                                link(v.tensor_tensor(rs, rs, col("rs.final", TT), ALU.mult))
                            v.tensor_scalar(col(f"rsq{name[-1]}", TT), rs, 384.0 ** -0.5, None, ALU.mult)
                            v.tensor_scalar(col(f"rskv{name[-1]}", TT), rs, 128.0 ** -0.5, None, ALU.mult)
                            v.tensor_scalar(col(f"rsh{name[-1]}", TT), rs, 0.5, None, ALU.mult).then_inc(s_rs, 1)
                        if name == "norm_mlp_g":
                            dve.wait_ge(s_rs, stats.index(name) + 1)
                            link(v.tensor_tensor(col("rs2", TT), rs, rs, ALU.mult))
                        if stat_name == "final":
                            dve.wait_ge(s_rs, stats.index(stat_name) + 1)
                            dve.wait_ge(s_row, 16)
                            for tt in range(TT):
                                v.scalar_tensor_tensor(h[:, tt, :], h[:, tt, :], rs[:, tt:tt + 1], row[:, R_FINAL:R_FINAL + D], ALU.mult, ALU.mult).then_inc(s_h_normed, 1)
                    if kind == "memscale":
                        continue
                    if name == "norm_mix_g":
                        split_ahead(0)
                        gf, gn = (V_GAIN + GAINS.index(n) * KT for n in ("norm_final_g", "ln_mix_0"))
                        link(v.tensor_tensor(col("gain.final", KT), vec[:, gf:gf + KT], vec[:, gn:gn + KT], ALU.mult))
                        l0, l1 = vec_lb[:, 0, :], vec_lb[:, 1, :]
                        m, e = col("lb.m", 4), col("lb.e", 8)
                        link(v.tensor_tensor(m, l0, l1, ALU.max))
                        v.tensor_tensor(e[:, 0:4], l0, m, ALU.subtract)
                        v.tensor_tensor(e[:, 4:8], l1, m, ALU.subtract).then_inc(s_bound_in, 1)
                        lam = vec[:, V_LAM:V_LAM + 8]
                        na = col("sp.na", 8)
                        link(v.tensor_scalar(na, lam, -1.0, None, ALU.mult))
                        v.tensor_tensor(na, na, lam, ALU.min).then_inc(s_softplus_in, 1)
                elif kind == "proj":
                    _, name, l, j, _ = step
                    job = job_of(name, l, j)
                    before = {"q": "norm_mix_g", "ck": "norm_mem_g", "cq": "norm_cross_g", "a": f"ln_mix_{l}", "gu": f"ln_ffn_{l}"}.get(name)
                    if before and j == (name == "a"):
                        drains(v.tensor_copy(rrow[:], wait_filled(dve, f"{before}.rstd")[:, 0:S]), f"{before}.rstd")
                        wait_drained(dve, f"{before}.rstd")
                    scaled = rrow[:, None, :].broadcast_to([P, 2, S])

                    def scale(out):
                        drains(v.tensor_tensor(out, bank2(wait_filled(dve, job)), scaled, ALU.mult), job)

                    if name in ("q", "k"):
                        cs = at(A_ROPE, 2, S)
                        if name == "q" and j == 0:
                            dve.wait_ge(s_trig, 1)
                            link(v.tensor_tensor(cs, cs, scaled, ALU.mult))
                        C = cs[:, None, 0, :].broadcast_to([P, 2, S])
                        Sn = cs[:, None, 1, :].broadcast_to([P, 2, S])
                        tmp = at(A_SC1, 4, S)
                        dst = at(A_Q1 if name == "q" else A_K1, 2, 2, S)
                        bank = bank2(wait_filled(dve, job))
                        v.tensor_tensor(tmp[:, 0:2, :], bank, C, ALU.mult)
                        drains(v.tensor_tensor(tmp[:, 2:4, :], bank, Sn, ALU.mult), job)
                        wait_drained(dve, job)
                        v.tensor_tensor(dst[:, j, 0, :], tmp[:, 0, :], tmp[:, 3, :], ALU.subtract)
                        ins = v.tensor_tensor(dst[:, j, 1, :], tmp[:, 2, :], tmp[:, 1, :], ALU.add)
                        if j == 1 and name == "k":
                            ins.then_inc(s_rope, 1)
                        else:
                            link(ins)
                    elif name == "u":
                        scale(at(A_U, 4, UPAD)[:, 2 * j:2 * j + 2, 2:2 + S])
                    elif name == "y":
                        scale(at(A_YG, 4, S)[:, 2 * j:2 * j + 2, :])
                    elif name in ("ck", "cq"):
                        scale(at(A_CK if name == "ck" else A_CQ, 4, S)[:, 2 * j:2 * j + 2, :])
                    elif name == "e" and j == 0:
                        scale(at(A_FT, 2, S))
                    elif name == "e":
                        hq = at(A_HQ, 2, 2, S)
                        bank = bank2(wait_filled(dve, job))
                        for o in range(2):
                            for d in range(2):
                                ins = v.tensor_tensor(hq[64 * d:64 * d + 64, :, o, :], bank[64 * o:64 * o + 64, :, :], scaled[64 * o:64 * o + 64], ALU.mult)
                        drains(ins, job)
                    elif name == "gu" and j % 2 == 0:
                        m = product_of(name, l, j)
                        dve.wait_ge(s_hidden_low, m - 1)
                        scale(product[:, m % 2, :].rearrange("p (a t) -> p a t", a=2))
                    elif name == "wout":
                        gain = 1.0 if l is None else 0.5
                        hh = h[:, :, 256 * j:256 * j + 256]
                        drains(v.scalar_tensor_tensor(hh, bank2(wait_filled(dve, job)), gain, hh, ALU.mult, ALU.add), job)
                    elif name == "co":
                        for tt in range(TT):
                            hh = h[:, tt, 512 * j:512 * j + 512]
                            drains(v.tensor_tensor(hh, wait_filled(dve, f"{job}.{tt}")[:], hh, ALU.add), f"{job}.{tt}")
                    elif (name, j) in (("down", 15), ("wd", 10)):
                        for tt in range(TT):
                            for c in range(2):
                                job = job_of(name, l, f"{tt}{c}")
                                hh = h[:, tt, 512 * c:512 * c + 512]
                                rs = col("rs2" if name == "down" else f"rs.ln_ffn_{l}", TT)
                                drains(v.scalar_tensor_tensor(hh, wait_filled(dve, job)[:], rs[:, tt:tt + 1], hh, ALU.mult, ALU.add), job)
                    elif (name, j) in (("down", 0), ("wd", 0)):
                        product_low(15 if name == "down" else product_of("gu", l, 21))
                    elif name == "up":
                        m = product_of(name, l, j)
                        dve.wait_ge(s_relu, m + 1)
                        drains(v.tensor_tensor(product[:, m % 2, :], wait_filled(dve, job)[:], product[:, m % 2, :], ALU.mult), job)
                        if j:
                            product_low(m - 1)
                    elif name == "gu" and j % 2:
                        m = product_of(name, l, j)
                        dve.wait_ge(s_silu, m - 16 + 1)
                        bank = wait_filled(dve, job)
                        drains(v.tensor_tensor(product[:, m % 2, :], bank[:], product[:, m % 2, :], ALU.mult), job)
                        if j > 1:
                            product_low(m - 1)
                    elif name == "a" and j == 1:
                        za = at(A_ZA, TT, 512)
                        s3, rs, t = col(f"ss.a{l}", 3 * TT), col(f"rs.a{l}", 2 * TT), col("hn.t", 32)[:, 0:2 * TT]
                        for i in range(2):
                            wait_drained(dve, f"a{l}.{i}")
                        link(v.tensor_tensor(s3[:, TT:2 * TT], s3[:, 0:TT], s3[:, TT:2 * TT], ALU.add))
                        ss = s3[:, TT:3 * TT]
                        link(v.tensor_scalar(ss, ss, EPS, None, ALU.add))
                        rsqrt(ss, rs, t, 2 * TT)
                        for tt in range(TT):
                            v.tensor_scalar(za[:, tt, 0:384], za[:, tt, 0:384], rs[:, tt:tt + 1], None, ALU.mult)
                            ins = v.tensor_scalar(za[:, tt, 384:512], za[:, tt, 384:512], rs[:, TT + tt:TT + tt + 1], None, ALU.mult)
                        ins.then_inc(s_token_side, 1)
                        if l == 0:
                            dve.wait_ge(s_bound_exp, 1)
                            e, sm, p = col("lb.x", 8), col("lb.s", 4), col("lb.p", 8)
                            link(v.tensor_tensor(sm, e[:, 0:4], e[:, 4:8], ALU.add))
                            link(v.reciprocal(sm, sm))
                            v.tensor_tensor(p[:, 0:4], e[:, 0:4], sm, ALU.mult)
                            link(v.tensor_tensor(p[:, 4:8], e[:, 4:8], sm, ALU.mult))
                            lb, om = col("lb.lb", 8), col("lb.om", 8)
                            v.tensor_tensor(lb[:, 0:4], p[:, 0:4], p[:, 0:4], ALU.subtract)
                            link(v.tensor_tensor(sm, p[:, 0:4], p[:, 4:8], ALU.add))
                            link(v.tensor_tensor(lb[:, 4:8], sm, p[:, 0:4], ALU.subtract))
                            link(v.tensor_scalar(om, lb, -1.0, 1.0, ALU.mult, ALU.add))
                            dve.wait_ge(s_row, 16)
                            for ll in range(L2):
                                r0 = R_LAYER + ll * R_PER + R_LQ
                                lq = row[:, r0:r0 + 128].rearrange("p (a d) -> p a d", a=4)
                                prod = scratch_xs[:, 0:64].rearrange("p (a d) -> p a d", a=2)
                                link(v.tensor_tensor(prod, lq[:, 0:2, :], lq[:, 2:4, :], ALU.mult))
                                ins = v.tensor_reduce(col(f"lam.d{ll}", 2), prod, AX_X, ALU.add)
                                ins.then_inc(s_lambda_in, 1)
                                dve.wait_ge(s_lambda_in, ll + 1)
                    elif name == "b" and j == 1:
                        zb = at(A_ZB, TT, 16, 32)
                        for i in range(2):
                            wait_drained(dve, f"b{l}.{i}")
                        rs = heads_norm(zb, 32, 32, scratch_xs)
                        link(v.tensor_tensor(zb, zb, rs.rearrange("p (a g) -> p a g", a=TT)[:, :, :, None].broadcast_to([P, TT, 16, 32]), ALU.mult))
                        r0 = R_LAYER + l * R_PER + R_DQN
                        g = row[:, r0:r0 + 64].rearrange("p (a d) -> p a d", a=2)[:, :, None, :].broadcast_to([P, 2, 8, 32])
                        for tt in range(TT):
                            z4 = zb[:, tt, :, :].rearrange("p (a g) d -> p a g d", a=2)
                            ins = v.tensor_tensor(z4, z4, g, ALU.mult)
                        link(ins)
                        rope32(zb[:, :, :, 0:16], zb[:, :, :, 16:32], 16).then_inc(s_token_side, 1)
                    elif name == "f" and j == 0:
                        scale(at(A_KK, 4, S)[:, 0:2, :])
                    elif name == "f":
                        scale(at(A_KK, 4, S)[:, 2:4, :])
                        kk, F = at(A_KK, 4, S), at(A_F, 4, S)
                        lb, om = col("lb.lb", 8), col("lb.om", 8)
                        dve.wait_ge(s_sig, 2 * (l + 1))
                        for hd in range(4):
                            c = 4 * l + hd
                            ins = v.tensor_scalar(kk[:, hd, :], kk[:, hd, :], om[:, c:c + 1], lb[:, c:c + 1], ALU.mult, ALU.add)
                        link(ins)
                        v.tensor_scalar(F, kk, 2.0 ** -63, None, ALU.max).then_inc(s_f, 1)
                        v.tensor_scalar(kk, kk, -1.0, 1.0, ALU.mult, ALU.add).then_inc(s_hgrn_k, 1)
                elif kind == "logf":
                    l = step[1]
                    E, F = at(A_E, 4, S + 1), at(A_F, 4, S)
                    v.memset(E[:, :, 0:1], 0.0)
                    ones = scratch_xs[:, 0:S]
                    dve.wait_ge(s_token_side, side_order.index((l, "z")) + 1)
                    link(v.memset(ones, 1.0))
                    dve.wait_ge(s_log_f, l + 1)
                    for hd in range(4):
                        ins = v.tensor_tensor_scan(E[:, hd, 1:S + 1], ones, F[:, hd, :], 0.0, ALU.mult, ALU.add)
                    link(ins)
                    v.tensor_copy(F[0:64, :, :], E[0:64, :, 1:S + 1])
                    link(v.tensor_copy(F[64:128, :, :], E[64:128, :, 0:S]))
                elif kind == "znorm":
                    l = step[1]
                    z = at(A_Z, TT, 8, 96)
                    wait_drained(dve, f"krt{l}")
                    for tt in range(TT):
                        for n in ("uq", "ukv"):
                            wait_drained(dve, f"{n}{l}.{tt}")
                    dve.wait_ge(s_token_side, side_order.index((l, "b")) + 1)
                    rs = heads_norm(z, 16, 96, scratch_xs)
                    link(v.tensor_tensor(z, z, rs.rearrange("p (a g) -> p a g", a=TT)[:, :, :, None].broadcast_to([P, TT, 8, 96]), ALU.mult))
                    r0 = R_LAYER + l * R_PER + R_QN
                    g = row[:, r0:r0 + 192].rearrange("p (a d) -> p a d", a=2)[:, :, None, :].broadcast_to([P, 2, 4, 96])
                    for tt in range(TT):
                        z4 = z[:, tt, :, :].rearrange("p (a g) d -> p a g d", a=2)
                        ins = v.tensor_tensor(z4, z4, g, ALU.mult)
                    link(ins)
                    rope32(z[:, :, :, 64:80], z[:, :, :, 80:96], 8).then_inc(s_token_side, 1)
                elif kind == "mix":
                    k = 4 * step[1]
                    dve.wait_ge(s_mix_high, 2 - step[1])
                    v.tensor_tensor(x_lo[:, k:k + 4, :], oT[:, k:k + 4, :], x_hi[:, k:k + 4, :].bitcast(F32), ALU.subtract).then_inc(s_mix_low, 1)
                elif kind == "conv":
                    for j in range(2):
                        wait_drained(dve, f"u.{j}")
                    dve.wait_ge(s_pads_zeroed, 1)
                    up, uc = at(A_U, 4, UPAD), at(A_UC, 4, S)
                    cw = vec[:, V_CONVW:V_CONVW + 16]
                    for tap in range(4):
                        for ct in range(4):
                            w = cw[:, 4 * ct + tap:4 * ct + tap + 1]
                            src = up[:, ct, tap:tap + S]
                            if tap == 0:
                                ins = v.tensor_scalar(uc[:, ct, :], src, w, vec[:, V_CONVB + ct:V_CONVB + ct + 1], ALU.mult, ALU.add)
                            else:
                                ins = v.scalar_tensor_tensor(uc[:, ct, :], src, w, uc[:, ct, :], ALU.mult, ALU.add)
                        if tap < 3:
                            link(ins)
                        else:
                            ins.then_inc(s_conv, 1)
                elif kind == "softplus":
                    dve.wait_ge(s_softplus_exp, 1)
                    x, s1, s2, acc = col("sp.x", 8), col("sp.s", 8), col("sp.s2", 8), col("sp.acc", 8)
                    link(v.tensor_scalar(s1, x, 2.0, None, ALU.add))
                    link(v.reciprocal(s1, s1))
                    link(v.tensor_tensor(s1, s1, x, ALU.mult))
                    link(v.tensor_tensor(s2, s1, s1, ALU.mult))
                    link(v.memset(acc, 1.0 / 19.0))
                    for n in range(17, 0, -2):
                        link(v.tensor_tensor(acc, acc, s2, ALU.mult))
                        link(v.tensor_scalar(acc, acc, 1.0 / n, None, ALU.add))
                    link(v.tensor_tensor(acc, acc, s1, ALU.mult))
                    link(v.tensor_scalar(s2, vec[:, V_LAM:V_LAM + 8], -1.0, 0.0, ALU.mult, ALU.max))
                    link(v.tensor_scalar(s2, s2, RG_C, None, ALU.mult))
                    link(v.scalar_tensor_tensor(acc, acc, 2.0 * RG_C, s2, ALU.mult, ALU.add))
                elif kind == "rgA":
                    acc = col("sp.acc", 8)
                    r = at(A_RG_R, 8, S)
                    wait_drained(dve, "rg.13")
                    v.tensor_tensor(r, r, acc[:, :, None].broadcast_to([P, 8, S]), ALU.mult).then_inc(s_rg_exponent, 1)
                    ii = at(A_RG_I, 2, 4, S)
                    uc = at(A_UC, 4, S)
                    for z in range(2):
                        link(v.tensor_tensor(ii[:, z], ii[:, z], uc, ALU.mult))
                elif kind == "rgB":
                    dve.wait_ge(s_rg_tanh_exp, 1)
                    r, t, a = at(A_RG_R, 2048), at(A_RG_T, 2048), at(A_RG_A, 2048)
                    link(v.tensor_tensor(r, a, a, ALU.mult))
                    v.scalar_tensor_tensor(t, r, 1.0, t, ALU.add, ALU.mult).then_inc(s_rg_square, 1)
                elif kind == "rgC":
                    t, ii = at(A_RG_T, 2048), at(A_RG_I, 2048)
                    a4, b4, h4 = at(A_RG_A, 2, 4, S), at(A_RG_I, 2, 4, S), at(A_RG_R, 2, 4, S)
                    if step[1] == 0:
                        dve.wait_ge(s_rg_root, 1)
                        link(v.tensor_tensor(ii, ii, t, ALU.mult))
                    elif step[1] < 3:
                        for ct in (0, 1) if step[1] == 1 else (2, 3):
                            v.tensor_tensor_scan(h4[:, 0, ct, :], a4[:, 0, ct, :], b4[:, 0, ct, :], 0.0, ALU.mult, ALU.add)
                            ins = v.tensor_tensor_scan(h4[:, 1, ct, ::-1], a4[:, 1, ct, ::-1], b4[:, 1, ct, ::-1], 0.0, ALU.mult, ALU.add)
                        link(ins)
                    else:
                        link(v.tensor_tensor(h4[:, 0], h4[:, 0], h4[:, 1], ALU.add))
                        v.tensor_tensor(oT[:, 4:8, :], h4[:, 0], at(A_YG, 4, S), ALU.mult).then_inc(s_rec, 1)
                elif kind == "score":
                    phase, hd = step[1:]
                    n, a0, count = ATT[phase, hd]
                    scale = {"dil": 64.0 ** -0.5, "cro": 128.0 ** -0.5, "mla": 96.0 ** -0.5, "dif": 32.0 ** -0.5}[phase[:3]]
                    if phase[:4] == "diff" and hd == 0:
                        l = int(phase[4])
                        dve.wait_ge(s_lambda_exp, l + 1)
                        e, nl = col(f"lam.e{l}", 2), col(f"lam.n{l}", 1)
                        link(v.tensor_tensor(nl, e[:, 1:2], e[:, 0:1], ALU.subtract))
                        link(v.tensor_scalar(nl, nl, LAMBDA_INIT[l], None, ALU.subtract))
                    if phase == "dil" and hd == 0:
                        dve.wait_ge(s_const, 16)
                    for j in range(count):
                        a = a0 + j
                        bank = bank2(wait_filled(dve, f"score{a}"))
                        nm = col(f"nmax{a % 16}", TT)
                        if phase == "dil":
                            if a >= 4:
                                wait_filled(dve, f"turn{ATT[HEAD_OF_UNIT[a - 4]][0]}")
                            sc = at(A_SC1 + 512 * (a % 4), TT, S)
                            drains(v.scalar_tensor_tensor(sc, bank, scale, logc, ALU.mult, ALU.add), f"score{a}")
                            wait_drained(dve, f"score{a}")
                            v.tensor_reduce(nm, sc, AX_X, ALU.max, negate=True).then_inc(s_max, 1)
                        else:
                            mx = col(f"max{a % 4}", TT)
                            link(v.tensor_reduce(mx, bank, AX_X, ALU.max, negate=True))
                            v.tensor_scalar(nm, mx, scale, None, ALU.mult).then_inc(s_max, 1)
                elif kind == "prob":
                    phase, hd = step[1:]
                    n, a0, count = ATT[phase, hd]
                    base = A_SC1 if phase in ("dil", "cross") else A_SC
                    for j in range(count):
                        a = a0 + j
                        if phase == "dil":
                            dve.wait_ge(s_exp, a + 1)
                        else:
                            wait_drained(dve, f"score{a}")
                        ins = v.reciprocal(col(f"rsum{a % 16}", TT), col(f"sum{a % 16}", TT))
                    link(ins)
                    p0 = at(base + 512 * (a0 % 4), TT, S)
                    rs = col(f"rsum{a0 % 16}", TT)
                    if count == 1:
                        v.tensor_scalar(p0[:, 0, :], p0[:, 0, :], rs[:, 0:1], None, ALU.mult)
                        v.tensor_scalar(p0[:, 1, :], p0[:, 1, :], rs[:, 1:2], None, ALU.mult).then_inc(s_prob, 1)
                    else:
                        p1 = at(base + 512 * ((a0 + 1) % 4), TT, S)
                        rs1 = col(f"rsum{(a0 + 1) % 16}", TT)
                        v.tensor_scalar(rs1, rs1, col(f"lam.n{phase[4]}", 1), None, ALU.mult)
                        v.tensor_scalar(p0[:, 0, :], p0[:, 0, :], rs[:, 0:1], None, ALU.mult)
                        link(v.tensor_scalar(p0[:, 1, :], p0[:, 1, :], rs[:, 1:2], None, ALU.mult))
                        v.scalar_tensor_tensor(p0[:, 0, :], p1[:, 0, :], rs1[:, 0:1], p0[:, 0, :], ALU.mult, ALU.add)
                        v.scalar_tensor_tensor(p0[:, 1, :], p1[:, 1, :], rs1[:, 1:2], p0[:, 1, :], ALU.mult, ALU.add).then_inc(s_prob, 1)
                elif kind in ("diffnorm", "hval"):
                    l = step[1]
                    if kind == "diffnorm":
                        o = at(A_DO, TT, 4, 64)
                        for hd in range(4):
                            wait_drained(dve, f"value.diff{l}{hd}")
                        factor, g0 = 1.0 - LAMBDA_INIT[l], R_SUB
                    else:
                        o = at(A_HO, TT, 4, 64)
                        for hp in range(2):
                            wait_drained(dve, f"hval{l}.{hp}")
                        factor, g0 = 0.5, R_ON
                    rs = heads_norm(o, 8, 64, at(A_SCR, 512))
                    link(v.tensor_scalar(rs, rs, factor, None, ALU.mult))
                    link(v.tensor_tensor(o, o, rs.rearrange("p (a g) -> p a g", a=TT)[:, :, :, None].broadcast_to([P, TT, 4, 64]), ALU.mult))
                    r0 = R_LAYER + l * R_PER + g0
                    g = row[:, r0:r0 + 64][:, None, None, :].broadcast_to([P, TT, 4, 64])
                    ins = v.tensor_tensor(o, o, g, ALU.mult)
                    if kind == "hval":
                        link(ins)
                        ins = v.scalar_tensor_tensor(at(A_HO, 512), at(A_SG, 512), 1.0, at(A_HO, 512), ALU.add, ALU.mult)
                    ins.then_inc(s_token_side, 1)
                elif kind == "decay":
                    _, l, i, hp = step
                    if i == 0 and hp == 0:
                        wait_filled(dve, f"value.mla{l}1")
                        wait_drained(dve, f"e{l}.1")
                    level_decay(l, i, hp)
                elif kind == "query":
                    level_query(*step[1:])
                elif kind == "level":
                    level_place(*step[1:])
                elif kind == "gate":
                    _, l, g, half, _ = step
                    job = f"gate{l}.{g}{half}"
                    if g == half == 0:
                        wait_drained(dve, f"fy{l}")
                    k = (4 * g + 2 * half) % 16
                    drains(v.tensor_tensor(at(A_GATE, 16, S)[:, k:k + 2, :], bank2(wait_filled(dve, job)),
                                           rrow[:, None, :].broadcast_to([P, 2, S]), ALU.mult), job)
                elif kind == "merge":
                    _, l, br, _ = step
                    gate = at(A_GATE, 16, S)
                    tmp = junk[:].bitcast(F32)[:, 0:512].rearrange("p (a t) -> p a t", a=2)
                    for j in range(4):
                        job = f"merge{l}.{br}{j}"
                        k = (8 * br + 2 * j) % 16
                        g = (8 * br + 2 * j) // 4
                        dve.wait_ge(s_gate, 16 * l + (8 * br + 2 * j) // 2 + 1)
                        bank = bank2(wait_filled(dve, job))
                        gk, mk = gate[:, k:k + 2, :], merged[:, 2 * j:2 * j + 2, :]
                        if br == 0:
                            drains(v.scalar_tensor_tensor(mk, gk, 1.0, bank, ALU.add, ALU.mult), job)
                        else:
                            drains(v.scalar_tensor_tensor(tmp, gk, 1.0, bank, ALU.add, ALU.mult), job)
                            wait_drained(dve, job)
                            ins = v.tensor_tensor(mk, mk, tmp, ALU.add)
                            if br == 3:
                                ins.then_inc(s_merged_sum, 1)
                                dve.wait_ge(s_merged_sum, 4 * l + j + 1)
                                if j:
                                    merged_low(l, j - 1)
                            elif j == 3 and br == 1:
                                ins.then_inc(s_merged, 1)
                                dve.wait_ge(s_merged, l + 1)
                            else:
                                link(ins)
                    if br == 3:
                        merged_low(l, 3)




def constants():
    c = np.zeros((P, C_SIZE), np.float64)
    p = np.arange(P)
    c[:, C_IDENT:C_IDENT + P] = np.eye(P)
    i, j = np.arange(S)[:, None], np.arange(S)[None, :]
    count = np.zeros((S, S))
    for window, dil in ((128, 1), (512, 4), (2048, 16)):
        count += ((i - j) % dil == 0) & (np.abs(i - j) // dil <= window // (2 * dil))
    logc = np.where(count > 0, np.log(np.maximum(count, 1)), -1e30)
    c[:, C_LOGC:C_LOGC + TT * S] = logc.reshape(TT, P, S).transpose(1, 0, 2).reshape(P, -1)
    c[:, C_FREQ] = 10000.0 ** (-(p % 32) / 32.0)
    ang = np.arange(S)[:, None] / 10000.0 ** (np.arange(0, 32, 2) / 32.0)[None, :]
    for off, f in ((C_COS, np.cos), (C_SIN, np.sin)):
        c[:, off:off + TT * 16] = f(ang).reshape(TT, P, 16).transpose(1, 0, 2).reshape(P, -1)
    d = np.arange(64)
    ph = 2 * np.pi * d[:, None] * d[None, :] / 64
    for g in range(2):
        c[64 * g:64 * g + 64, C_DFTD + 64 * g:C_DFTD + 64 * g + 64] = np.cos(ph) / 8.0
        c[64 * g:64 * g + 64, C_DFTD + P + 64 * g:C_DFTD + P + 64 * g + 64] = np.sin(ph) / 8.0
    ph = 2 * np.pi * ((i * j) % S) / S
    c[:, C_DFTC:C_DFTC + TT * S] = (np.cos(ph) / 16.0).reshape(TT, P, S).transpose(1, 0, 2).reshape(P, -1)
    c[:, C_DFTS:C_DFTS + TT * S] = (-np.sin(ph) / 16.0).reshape(TT, P, S).transpose(1, 0, 2).reshape(P, -1)
    for n, half in enumerate(MASKED):
        same = p[:, None] // (2 * half) == p[None, :] // (2 * half) if half else np.eye(P, dtype=bool)
        c[:, C_MASK + n * P:C_MASK + (n + 1) * P] = same
    return c.astype(np.float32)




def fold(w):
    k = w.shape[0] // P
    return w.reshape(k, P, -1).transpose(1, 0, 2).reshape(P, -1)


def pack_pieces(a):
    pieces = []

    def put(*parts):
        parts = [fold(p) for p in parts]
        n = sum(p.shape[1] for p in parts)
        pieces.append(np.concatenate(parts + ([np.zeros((P, PIECE - n), np.float32)] if n < PIECE else []), axis=1))

    def columns(w, n=256):
        for c in range(0, w.shape[1], n):
            put(w[:, c:c + n])

    def rows(w, n=256):
        for r in range(0, w.shape[0], n):
            put(w[r:r + n])

    w = a["w_in"][0]
    halves = np.concatenate([np.concatenate([64 * hd + 32 * f + np.arange(32) for hd in range(4 * g, 4 * g + 4)]) for g in range(2) for f in range(2)])
    columns(w[:, halves])
    columns(w[:, 512 + halves])
    columns(w[:, 1024:2560])
    columns(a["w_ck"][0])
    columns(a["w_cv"][0])
    columns(a["w_out"][0])
    columns(a["w_cq"][0])
    columns(a["w_co"][0], 512)
    columns(a["w_mlp_in"][0])
    rows(a["w_mlp_out"][0])
    for l in range(L2):
        w = a["w_in_2"][l]
        o = np.cumsum([0, 384, 128, 32, 256, 256, 256, 256, 256, 256, 256, 256, 256, 4096])
        c_q, c_kv, k_rope, fnet, dq, dk, dv, hq, hi, hff, hfb, hg, gate = (w[:, o[i]:o[i + 1]] for i in range(13))
        columns(np.concatenate([c_q, c_kv, dq, dk, hg], 1))
        ukv = a["mla_w_ukv_2"][l].reshape(P, 4, 2, 64).transpose(0, 2, 1, 3).reshape(P, 512)
        put(k_rope, a["mla_w_uq_2"][l], ukv)
        columns(np.concatenate([dv, hi], 1))
        columns(np.stack([hff.reshape(D, 4, 64), hfb.reshape(D, 4, 64)], 2).reshape(D, 512))
        columns(np.concatenate([fnet, hq], 1))
        br = a["w_branch_2"][l]
        columns(gate[:, 0:2048])
        put(br[0])
        put(br[1])
        columns(gate[:, 2048:4096])
        put(br[2])
        put(br[3])
        columns(a["w_out_2"][l])
        gu = a["w_gate_up_2"][l].reshape(D, 2, 11, 256).transpose(0, 2, 1, 3).reshape(D, -1)
        columns(gu)
        rows(a["w_down_2"][l])
    return np.ascontiguousarray(np.stack(pieces))


def pack_vectors(a):
    gains = [a[n][0] for n in GAINS[:4]] + [a["ln_mix_2"][l] for l in range(L2)] + [a["ln_ffn_2"][l] for l in range(L2)]
    gains.append(a["norm_final_g"])
    parts = [g.reshape(KT, P).T for g in gains]
    parts.append(a["conv_w"][0].reshape(4, 4, P).transpose(2, 1, 0).reshape(P, 16))
    parts.append(a["conv_b"][0].reshape(4, P).T)
    ab, xb = (a[n][0].reshape(2, 4, P).transpose(2, 0, 1) for n in ("rg_a_b", "rg_x_b"))
    parts.append(np.stack([ab, xb], 3).reshape(P, 16))
    parts.append(a["rg_lambda"][0].reshape(2, 4, P).transpose(2, 0, 1).reshape(P, 8))
    for l in range(L2):
        parts.append(a["mla_g_qa_2"][l].reshape(3, P).T)
        parts.append(a["mla_g_kva_2"][l].reshape(P, 1))
    lb = a["hgrn_lb_logits_2"].reshape(2, L2, 4, 64).transpose(0, 3, 1, 2).reshape(P, L2 * 4)
    parts.append(lb)
    out = np.ascontiguousarray(np.concatenate(parts, 1))
    assert out.shape == (P, V_SIZE), out.shape
    return out


def pack_rows(a):
    r = [a["norm_final_g"]]
    for l in range(L2):
        r += [a[n + "_2"][l] for n in ("mla_g_qn", "mla_g_kn", "diff_g_qn", "diff_g_kn", "diff_g_sub", "hgrn_g_on",
                                       "diff_lq1", "diff_lq2", "diff_lk1", "diff_lk2")]
    r = np.concatenate(r)
    assert r.shape == (R_SIZE,)
    return np.ascontiguousarray(np.broadcast_to(r, (P, R_SIZE)))


def pack_rg(a):
    out = np.zeros((P, 2, 4, 2, P), np.float32)
    for ax, n in enumerate(("rg_a_w", "rg_x_w")):
        w = a[n][0]
        for z in range(2):
            for g in range(8):
                p0 = 64 * (g % 2)
                out[p0:p0 + 64, z, g // 2, ax, p0:p0 + 64] = w[z, g]
    return out.reshape(P, 16 * P)


def kernel(**inputs):
    import concourse.bacc as bacc
    from concourse.bass_utils import run_bass_kernel_spmd

    a = {n: np.asarray(x) for n, x in inputs.items()}
    arrays = {
        "x": np.ascontiguousarray(a["x"][0]),
        "mem": np.ascontiguousarray(a["mem"][0]),
        "positions": np.ascontiguousarray(np.broadcast_to(a["positions"][0], (P, S))),
        "constants": constants(),
        "vectors": pack_vectors(a),
        "rows": pack_rows(a),
        "rg_weights": pack_rg(a),
        "weight_pieces": pack_pieces(a),
    }
    nc = bacc.Bacc("TRN2", target_bir_lowering=False, num_devices=1)
    args = [nc.dram_tensor(n, v.shape, mybir.dt.from_np(v.dtype), kind="ExternalInput").ap() for n, v in arrays.items()]
    args.append(nc.dram_tensor("out", (S, D), F32, kind="ExternalOutput").ap())
    build(nc, *args)
    r = run_bass_kernel_spmd(nc, [arrays], core_ids=[0])
    return r.results[0]["out"].reshape(1, S, D)
```
